# Optimizing a Trainium2 kernel written in Bass

```python
import math
import jax, jax.numpy as jnp
from jax import lax
import numpy as np

D_MODEL = 1024
BATCH = 1
SEQ = 512
DEPTH = 2
DEC_BATCH = 8
DEC_SEQ = 1
PAST_LEN = 4096
PAGE_SIZE = 128

N_MIXERS = 2
N_ML = (DEPTH + 1) // 2
N_GD = DEPTH // 2
N_MEM = 256
D_FF = 2816
FFN_RES = 0.5
EPS = 1e-6
ML_HEADS = 4
ML_DV = D_MODEL // ML_HEADS
ML_DQK = ML_DV // 2
ML_CHUNK = 64
ML_PROJ = 2 * ML_HEADS * ML_DQK + 2 * D_MODEL + 2 * ML_HEADS
GD_HEADS = 8
GD_DK = 128
GD_DV = D_MODEL // GD_HEADS
GD_CONV = 4
GD_CHUNK = 64
GD_QKV = 2 * GD_HEADS * GD_DK + GD_HEADS * GD_DV
GD_PROJ = GD_QKV + GD_HEADS * GD_DV + 2 * GD_HEADS
XA_HEADS = 4
XA_DH = D_MODEL // XA_HEADS

kernel_name = 'hybrid_mlstm_gdn_macaron_memory_step'

def rms_norm(x, g):
    xf = x.astype(jnp.float32)
    y = xf * lax.rsqrt(jnp.mean(xf * xf, axis=-1, keepdims=True) + EPS)
    return (y * g.astype(jnp.float32)).astype(x.dtype)

def head_rms(x, g):
    y = x * lax.rsqrt(jnp.mean(x * x, axis=-1, keepdims=True) + EPS)
    return y * g.astype(jnp.float32)

def l2_normalize(x):
    return x * lax.rsqrt(jnp.sum(x * x, axis=-1, keepdims=True) + EPS)

def swiglu(h, w_gate, w_up, w_down):
    return (jax.nn.silu(h @ w_gate) * (h @ w_up)) @ w_down

def pad_time(a, pad, value):
    if pad == 0:
        return a
    widths = [(0, 0)] * a.ndim
    widths[1] = (0, pad)
    return jnp.pad(a, widths, constant_values=value)

def chunk_layout(length, chunk):
    c = min(chunk, length)
    n_chunks = -(-length // c)
    return c, n_chunks, n_chunks * c - length

def to_chunks(a, n_chunks, c):
    b = a.shape[0]
    return jnp.moveaxis(a.reshape((b, n_chunks, c) + a.shape[2:]), 1, 0)

def from_chunks(a, length):
    n_chunks, b, c = a.shape[:3]
    return jnp.moveaxis(a, 0, 1).reshape((b, n_chunks * c) + a.shape[3:])[:, :length]

def mlstm_chunked(q, k, v, i_pre, log_f, C0, n0, m0):
    length = q.shape[1]
    c, n_chunks, pad = chunk_layout(length, ML_CHUNK)
    xs = (pad_time(q, pad, 0.0), pad_time(k, pad, 0.0), pad_time(v, pad, 0.0),
          pad_time(i_pre, pad, -jnp.inf), pad_time(log_f, pad, 0.0))
    xs = tuple(to_chunks(a, n_chunks, c) for a in xs)
    incl = jnp.tril(jnp.ones((c, c), dtype=bool))

    def step(carry, inp):
        C, nv, m = carry
        qc, kc, vc, ic, fc = [jnp.moveaxis(a, 2, 1) for a in inp]
        b = jnp.cumsum(fc, axis=-1)
        a_inter = b + m[..., None]
        dmat = jnp.where(incl, b[..., :, None] - b[..., None, :] + ic[..., None, :], -jnp.inf)
        m_t = jnp.maximum(a_inter, jnp.max(dmat, axis=-1))
        w_inter = jnp.exp(a_inter - m_t)
        s_qk = jnp.einsum('bhtd,bhsd->bhts', qc, kc) * jnp.exp(dmat - m_t[..., None])
        num = w_inter[..., None] * jnp.einsum('bhtd,bhde->bhte', qc, C) + jnp.einsum('bhts,bhse->bhte', s_qk, vc)
        den = w_inter * jnp.einsum('bhtd,bhd->bht', qc, nv) + jnp.sum(s_qk, axis=-1)
        h = num / jnp.maximum(jnp.abs(den), jnp.exp(-m_t))[..., None]
        m_new = m_t[..., -1]
        w_k = jnp.exp(b[..., -1:] - b + ic - m_new[..., None])
        carry_decay = jnp.exp(b[..., -1] + m - m_new)
        C_new = carry_decay[..., None, None] * C + jnp.einsum('bhs,bhsd,bhse->bhde', w_k, kc, vc)
        n_new = carry_decay[..., None] * nv + jnp.einsum('bhs,bhsd->bhd', w_k, kc)
        return (C_new, n_new, m_new), jnp.moveaxis(h, 1, 2)

    (C, nv, m), hs = lax.scan(step, (C0, n0, m0), xs)
    return from_chunks(hs, length), C, nv, m

def gdn_chunked(q, k, v, beta, log_g, S0):
    length = q.shape[1]
    c, n_chunks, pad = chunk_layout(length, GD_CHUNK)
    xs = tuple(to_chunks(pad_time(a, pad, 0.0), n_chunks, c) for a in (q, k, v, beta, log_g))
    incl = jnp.tril(jnp.ones((c, c), dtype=bool))
    strict = jnp.tril(jnp.ones((c, c), dtype=bool), -1)
    eye = jnp.eye(c, dtype=jnp.float32)

    def step(S, inp):
        qc, kc, vc, bc, gc = [jnp.moveaxis(a, 2, 1) for a in inp]
        gam = jnp.cumsum(gc, axis=-1)
        decay = jnp.exp(jnp.where(incl, gam[..., :, None] - gam[..., None, :], -jnp.inf))
        kk = jnp.einsum('bhtd,bhsd->bhts', kc, kc)
        a_mat = jnp.where(strict, bc[..., :, None] * kk * decay, 0.0) + eye
        u = lax.linalg.triangular_solve(a_mat, bc[..., None] * vc, left_side=True, lower=True, unit_diagonal=True)
        w = lax.linalg.triangular_solve(a_mat, (bc * jnp.exp(gam))[..., None] * kc,
                                        left_side=True, lower=True, unit_diagonal=True)
        u = u - jnp.einsum('bhtd,bhde->bhte', w, S)
        qk = jnp.einsum('bhtd,bhsd->bhts', qc, kc) * decay
        o = jnp.einsum('bhtd,bhde->bhte', qc * jnp.exp(gam)[..., None], S) + jnp.einsum('bhts,bhse->bhte', qk, u)
        g_last = gam[..., -1]
        k_dec = kc * jnp.exp(g_last[..., None] - gam)[..., None]
        S_new = jnp.exp(g_last)[..., None, None] * S + jnp.einsum('bhsd,bhse->bhde', k_dec, u)
        return S_new, jnp.moveaxis(o, 1, 2)

    S, os_ = lax.scan(step, S0, xs)
    return from_chunks(os_, length), S

def mlstm_mixer(h, w_in, b_i, b_f, g_head, w_out, C0, n0, m0):
    bsz, length, _ = h.shape
    f32 = jnp.float32
    hq = ML_HEADS * ML_DQK
    p = h @ w_in
    q, k, v, o, ig, fg = jnp.split(
        p, [hq, 2 * hq, 2 * hq + D_MODEL, 2 * hq + 2 * D_MODEL, 2 * hq + 2 * D_MODEL + ML_HEADS], axis=-1)
    q = q.astype(f32).reshape(bsz, length, ML_HEADS, ML_DQK)
    k = k.astype(f32).reshape(bsz, length, ML_HEADS, ML_DQK) * ML_DQK ** -0.5
    v = v.astype(f32).reshape(bsz, length, ML_HEADS, ML_DV)
    i_pre = ig.astype(f32) + b_i.astype(f32)
    log_f = jax.nn.log_sigmoid(fg.astype(f32) + b_f.astype(f32))
    hh, C, n, m = mlstm_chunked(q, k, v, i_pre, log_f, C0.astype(f32), n0.astype(f32), m0.astype(f32))
    hh = head_rms(hh, g_head.reshape(ML_HEADS, ML_DV)).reshape(bsz, length, D_MODEL)
    out = (hh * jax.nn.sigmoid(o.astype(f32))).astype(h.dtype)
    return out @ w_out, C, n, m

def gdn_mixer(h, conv_prev, w_in, conv_w, a_log, dt_bias, g_out, w_out, S0):
    bsz, length, _ = h.shape
    f32 = jnp.float32
    p = h @ w_in
    qkv, z, b_pre, a_pre = jnp.split(p, [GD_QKV, GD_QKV + D_MODEL, GD_QKV + D_MODEL + GD_HEADS], axis=-1)
    ext = jnp.concatenate([conv_prev.astype(qkv.dtype), qkv], axis=1)
    conv = ext[:, 0:length] * conv_w[0]
    for j in range(1, GD_CONV):
        conv = conv + ext[:, j:j + length] * conv_w[j]
    conv = jax.nn.silu(conv).astype(f32)
    new_conv = ext[:, length:]
    q, k, v = jnp.split(conv, [GD_HEADS * GD_DK, 2 * GD_HEADS * GD_DK], axis=-1)
    q = l2_normalize(q.reshape(bsz, length, GD_HEADS, GD_DK)) * GD_DK ** -0.5
    k = l2_normalize(k.reshape(bsz, length, GD_HEADS, GD_DK))
    v = v.reshape(bsz, length, GD_HEADS, GD_DV)
    beta = jax.nn.sigmoid(b_pre.astype(f32))
    log_g = -jnp.exp(a_log.astype(f32)) * jax.nn.softplus(a_pre.astype(f32) + dt_bias.astype(f32))
    o, S = gdn_chunked(q, k, v, beta, log_g, S0.astype(f32))
    o = head_rms(o, g_out) * jax.nn.silu(z.astype(f32).reshape(bsz, length, GD_HEADS, GD_DV))
    return o.reshape(bsz, length, D_MODEL).astype(h.dtype) @ w_out, S, new_conv

def mem_kv(mem, g_mem, w_k, w_v):
    bsz = mem.shape[0]
    m = rms_norm(mem, g_mem)
    k = (m @ w_k).reshape(bsz, N_MEM, XA_HEADS, XA_DH)
    v = (m @ w_v).reshape(bsz, N_MEM, XA_HEADS, XA_DH)
    return k, v

def cross_attend(h, k, v, w_q, w_o):
    bsz, length, _ = h.shape
    q = (h @ w_q).reshape(bsz, length, XA_HEADS, XA_DH)
    s = jnp.einsum('blhd,bmhd->bhlm', q, k.astype(q.dtype)).astype(jnp.float32) * XA_DH ** -0.5
    p = jax.nn.softmax(s, axis=-1).astype(h.dtype)
    o = jnp.einsum('bhlm,bmhd->blhd', p, v.astype(h.dtype)).reshape(bsz, length, D_MODEL)
    return o @ w_o

def _trunk(x, mem_k, mem_v, ml_C, ml_n, ml_m, gd_S, gd_conv, P):
    new_C, new_n, new_m, new_S, new_conv = [], [], [], [], []
    for layer in range(DEPTH):
        j = layer // N_MIXERS
        x = x + FFN_RES * swiglu(rms_norm(x, P['g_ffn1'][layer]), P['ffn1_w_gate'][layer],
                                 P['ffn1_w_up'][layer], P['ffn1_w_down'][layer])
        h = rms_norm(x, P['g_mix'][layer])
        if layer % N_MIXERS == 0:
            y, C, n, m = mlstm_mixer(h, P['ml_w_in'][j], P['ml_b_i'][j], P['ml_b_f'][j], P['ml_g_head'][j],
                                     P['ml_w_out'][j], ml_C[j], ml_n[j], ml_m[j])
            new_C.append(C)
            new_n.append(n)
            new_m.append(m)
        else:
            y, S, cv = gdn_mixer(h, gd_conv[j], P['gd_w_in'][j], P['gd_conv_w'][j], P['gd_a_log'][j],
                                 P['gd_dt_bias'][j], P['gd_g_out'][j], P['gd_w_out'][j], gd_S[j])
            new_S.append(S)
            new_conv.append(cv)
        x = x + y
        x = x + cross_attend(rms_norm(x, P['g_xattn'][layer]), mem_k[layer], mem_v[layer],
                             P['xa_w_q'][layer], P['xa_w_o'][layer])
        x = x + FFN_RES * swiglu(rms_norm(x, P['g_ffn2'][layer]), P['ffn2_w_gate'][layer],
                                 P['ffn2_w_up'][layer], P['ffn2_w_down'][layer])
    y = rms_norm(x, P['g_final'])
    return y, jnp.stack(new_C), jnp.stack(new_n), jnp.stack(new_m), jnp.stack(new_S), jnp.stack(new_conv)

def setup_inputs(seed: int = 0) -> dict:
    key = jax.random.key(seed)
    ks = iter(jax.random.split(key, 48))

    def nrm(shape, scale):
        return jax.random.normal(next(ks), shape, jnp.float32) * scale

    def unif(shape, lo, hi):
        return jax.random.uniform(next(ks), shape, jnp.float32, lo, hi)

    def gain(shape):
        return 1.0 + nrm(shape, 0.02)

    D = D_MODEL
    s_d = D ** -0.5
    s_ff = D_FF ** -0.5
    dt = jnp.exp(unif((N_GD, GD_HEADS), math.log(1e-3), math.log(1e-1)))
    return {
        'x_prompt': nrm((BATCH, SEQ, D), 1.0),
        'x_sample': nrm((DEC_BATCH, DEC_SEQ, D), 1.0),
        'mem_prompt': nrm((BATCH, N_MEM, D), 1.0),
        'cache_mem_k': nrm((DEPTH, DEC_BATCH, N_MEM, XA_HEADS, XA_DH), 1.0),
        'cache_mem_v': nrm((DEPTH, DEC_BATCH, N_MEM, XA_HEADS, XA_DH), 1.0),
        'state_mlstm_C': nrm((N_ML, DEC_BATCH, ML_HEADS, ML_DQK, ML_DV), 0.1),
        'state_mlstm_n': nrm((N_ML, DEC_BATCH, ML_HEADS, ML_DQK), 0.1),
        'state_mlstm_m': nrm((N_ML, DEC_BATCH, ML_HEADS), 1.0),
        'state_gdn_S': nrm((N_GD, DEC_BATCH, GD_HEADS, GD_DK, GD_DV), 0.1),
        'state_gdn_conv': nrm((N_GD, DEC_BATCH, GD_CONV - 1, GD_QKV), 1.0),
        'g_ffn1': gain((DEPTH, D)),
        'ffn1_w_gate': nrm((DEPTH, D, D_FF), s_d),
        'ffn1_w_up': nrm((DEPTH, D, D_FF), s_d),
        'ffn1_w_down': nrm((DEPTH, D_FF, D), s_ff),
        'g_mix': gain((DEPTH, D)),
        'ml_w_in': nrm((N_ML, D, ML_PROJ), s_d),
        'ml_b_i': -2.0 + nrm((N_ML, ML_HEADS), 0.1),
        'ml_b_f': unif((N_ML, ML_HEADS), 3.0, 6.0),
        'ml_g_head': gain((N_ML, ML_HEADS * ML_DV)),
        'ml_w_out': nrm((N_ML, D, D), s_d),
        'gd_w_in': nrm((N_GD, D, GD_PROJ), s_d),
        'gd_conv_w': nrm((N_GD, GD_CONV, GD_QKV), GD_CONV ** -0.5),
        'gd_a_log': jnp.log(unif((N_GD, GD_HEADS), 1.0, 16.0)),
        'gd_dt_bias': dt + jnp.log(-jnp.expm1(-dt)),
        'gd_g_out': gain((N_GD, GD_DV)),
        'gd_w_out': nrm((N_GD, D, D), s_d),
        'g_xattn': gain((DEPTH, D)),
        'g_mem': gain((DEPTH, D)),
        'xa_w_q': nrm((DEPTH, D, D), s_d),
        'xa_w_k': nrm((DEPTH, D, D), s_d),
        'xa_w_v': nrm((DEPTH, D, D), s_d),
        'xa_w_o': nrm((DEPTH, D, D), s_d),
        'g_ffn2': gain((DEPTH, D)),
        'ffn2_w_gate': nrm((DEPTH, D, D_FF), s_d),
        'ffn2_w_up': nrm((DEPTH, D, D_FF), s_d),
        'ffn2_w_down': nrm((DEPTH, D_FF, D), s_ff),
        'g_final': gain((D,)),
    }

def reference(x_prompt, x_sample, mem_prompt, cache_mem_k, cache_mem_v, state_mlstm_C, state_mlstm_n,
              state_mlstm_m, state_gdn_S, state_gdn_conv, g_ffn1, ffn1_w_gate, ffn1_w_up, ffn1_w_down, g_mix,
              ml_w_in, ml_b_i, ml_b_f, ml_g_head, ml_w_out, gd_w_in, gd_conv_w, gd_a_log, gd_dt_bias, gd_g_out,
              gd_w_out, g_xattn, g_mem, xa_w_q, xa_w_k, xa_w_v, xa_w_o, g_ffn2, ffn2_w_gate, ffn2_w_up,
              ffn2_w_down, g_final):
    P = {
        'g_ffn1': g_ffn1, 'ffn1_w_gate': ffn1_w_gate, 'ffn1_w_up': ffn1_w_up, 'ffn1_w_down': ffn1_w_down,
        'g_mix': g_mix,
        'ml_w_in': ml_w_in, 'ml_b_i': ml_b_i, 'ml_b_f': ml_b_f, 'ml_g_head': ml_g_head, 'ml_w_out': ml_w_out,
        'gd_w_in': gd_w_in, 'gd_conv_w': gd_conv_w, 'gd_a_log': gd_a_log, 'gd_dt_bias': gd_dt_bias,
        'gd_g_out': gd_g_out, 'gd_w_out': gd_w_out,
        'g_xattn': g_xattn, 'xa_w_q': xa_w_q, 'xa_w_o': xa_w_o,
        'g_ffn2': g_ffn2, 'ffn2_w_gate': ffn2_w_gate, 'ffn2_w_up': ffn2_w_up, 'ffn2_w_down': ffn2_w_down,
        'g_final': g_final,
    }
    f32 = jnp.float32
    mks, mvs = [], []
    for layer in range(DEPTH):
        k, v = mem_kv(mem_prompt, g_mem[layer], xa_w_k[layer], xa_w_v[layer])
        mks.append(k)
        mvs.append(v)
    prompt_mem_k = jnp.stack(mks)
    prompt_mem_v = jnp.stack(mvs)
    zC = jnp.zeros((N_ML, BATCH, ML_HEADS, ML_DQK, ML_DV), f32)
    zn = jnp.zeros((N_ML, BATCH, ML_HEADS, ML_DQK), f32)
    zm = jnp.zeros((N_ML, BATCH, ML_HEADS), f32)
    zS = jnp.zeros((N_GD, BATCH, GD_HEADS, GD_DK, GD_DV), f32)
    zconv = jnp.zeros((N_GD, BATCH, GD_CONV - 1, GD_QKV), x_prompt.dtype)
    y_prompt, p_C, p_n, p_m, p_S, p_conv = _trunk(x_prompt, prompt_mem_k, prompt_mem_v, zC, zn, zm, zS, zconv, P)
    y_sample, s_C, s_n, s_m, s_S, s_conv = _trunk(x_sample, cache_mem_k, cache_mem_v, state_mlstm_C, state_mlstm_n,
                                                  state_mlstm_m, state_gdn_S, state_gdn_conv, P)
    return (y_prompt, y_sample, prompt_mem_k, prompt_mem_v, p_C, p_n, p_m, p_S, p_conv, s_C, s_n, s_m, s_S, s_conv)


_drawn_inputs = setup_inputs


def setup_inputs(seed=0):
    import zlib

    import numpy as np

    out = dict(_drawn_inputs(seed))
    spreads = {}
    factors = {'ml_g_head': 3.755,
     'gd_g_out': 24.777,
     'g_xattn': 8.0,
     'g_mem': 2.82,
     'g_ffn2': 4.733,
     'g_final': 7.184}
    for name, (base, spread) in spreads.items():
        noise = np.random.default_rng([zlib.crc32(name.encode()), seed]).standard_normal(out[name].shape)
        drawn = base * np.exp(spread * noise) if base else spread * noise
        out[name] = __import__('jax').numpy.asarray(drawn.astype(out[name].dtype))
    for name, factor in factors.items():
        out[name] = (out[name] * factor).astype(out[name].dtype)
    return out
```

```python
from contextlib import ExitStack, contextmanager

import concourse.bass as bass
from concourse import mybir

ALU = mybir.AluOpType
ACT = mybir.ActivationFunctionType
AX = mybir.AxisListType
F32 = mybir.dt.float32
F32R = mybir.dt.float32r
BF16 = mybir.dt.bfloat16

P = 128
D = 1024
KC = D // P
LP = 512
NS = 8
T = LP + NS
TH = T // 2
FF = 2816
FC = FF // P
FH = FC // 2
NTG = 5
TG = T // NTG
NMEM = 256
MT = NMEM // P
XH = 4
XD = D // XH
MLH = 4
MLQ = 512
GH = 8
EPS = 1e-6
TB = LP // P
BIG = 1e30


class Own:

    def __init__(self, eng, sem):
        self.eng, self.sem, self.base, self.k, self.i, self.per = eng, sem, 0, 0, None, 0

    def link(self, ins):
        self.k += 1
        ins.then_inc(self.sem, 1)
        n = self.base + self.k
        self.eng.wait_ge(self.sem, n if self.i is None else self.i * self.per + n)

    @contextmanager
    def loop(self, count, per):
        self.base, self.k, self.per = self.base + self.k, 0, per
        with self.eng.Fori(0, count) as i:
            self.i = i
            yield i
            assert self.k == per, (self.k, per)
        self.base, self.k, self.i = self.base + count * per, 0, None


class Steps:

    def __init__(self, sem, names):
        self.sem, self.n, self.at = sem, len(names), {x: k + 1 for k, x in enumerate(names)}
        assert len(self.at) == self.n
        self.told = 0

    def done(self, ins, *name, r=0):
        assert self.told % self.n + 1 == self.at[name], (name, self.told)
        self.told += 1
        ins.then_inc(self.sem, 1)

    def wait(self, eng, *name, r=0):
        eng.wait_ge(self.sem, r * self.n + self.at[name])


def halves(ap):
    return ap.rearrange("p (a b) -> p a b", a=2)


def program(nc, a, o):
    with ExitStack() as ctx:
        def sb(name, shape, dt=F32):
            return ctx.enter_context(nc.sbuf_tensor(name, shape, dt))

        def sem(name):
            return ctx.enter_context(nc.semaphore(name))

        x = sb("x", [P, KC, T])
        base_xg = nc.sbuf_base
        xg_hi = sb("xg_hi", [P, KC, T], F32R)
        xg_lo = sb("xg_lo", [P, KC, T], F32R)
        raw = sb("raw", [P, 4, FH * P])
        w_hi = sb("w_hi", [P, 2, FH * P], F32R)
        w_lo = sb("w_lo", [P, 2, FH * P], F32R)
        R = sb("R", [P, T])
        ssq = sb("ssq", [P, T])
        sq = sb("sq", [P, 2, T])
        tmp = sb("tmp", [P, 3, T + 4])
        ident = sb("ident", [P, P])
        ones = sb("ones", [P, P])
        causal = sb("causal", [P, P], BF16)
        level = sb("level", [P, 7, P], BF16)
        mhalf = sb("mhalf", [P, 128])
        cols = sb("cols", [P, 97])
        convw = sb("convw", [P, 96])
        msq = sb("msq", [TG, NTG])
        rtok = sb("rtok", [TG, NTG])
        small = sb("small", [P, 16])
        gm_raw = sb("gm_raw", [P, KC, P])
        keep = sb("keep", [P, 400])
        base = nc.sbuf_base
        room = 2 * FC * T * 4
        ctx.enter_context(nc.sbuf_tensor("region", [P, room // 4], F32))

        def placed(start, room):
            at = [start]

            def put(name, shape, dt=F32):
                n = 4
                for k in shape[1:]:
                    n *= k
                t = nc.alloc_sbuf_tensor_at(name, shape, dt, offset=at[0])
                at[0] += (n + 31) // 32 * 32
                assert at[0] <= start + room, (name, at[0] - start - room)
                return t
            return put

        put = placed(base, room)
        hid_hi = put("hid_hi", [P, FC, T], F32R)
        hid_lo = put("hid_lo", [P, FC, T], F32R)

        ACC = ctx.enter_context(nc.psum_tensor("ACC", [P, 4, 512], F32))
        M = ctx.enter_context(nc.psum_tensor("M", [P, 4, 512], F32))

        w_in = [sem(f"w_in{s}") for s in range(4)]
        w_hi_done = sem("w_hi_done")
        w_split = sem("w_split")
        mm_done = sem("mm_done")
        acc_free = sem("acc_free")
        silu_done = sem("silu_done")
        hid_ready = sem("hid_ready")
        xg_hi_done = sem("xg_hi_done")
        xg_ready = sem("xg_ready")
        sq_done = sem("sq_done")
        ssq_added = sem("ssq_added")
        nrm_tok = sem("nrm_tok")
        nrm_ms = sem("nrm_ms")
        nrm_pow = sem("nrm_pow")
        nrm_bc = sem("nrm_bc")
        act_own = sem("act_own")
        dve_own = sem("dve_own")
        pool_own = sem("pool_own")
        ins_done = sem("ins_done")
        stored = sem("stored")
        cv_acc = sem("cv_acc")
        cv_silu = sem("cv_silu")

        VEC = ["g_ffn1:0", "g_ffn1:1", "g_mix:0", "g_mix:1", "g_xattn:0", "g_xattn:1", "g_mem:0", "g_mem:1",
               "g_ffn2:0", "g_ffn2:1", "g_final", "ml_g_head:0"]
        vec_at = {v: KC * n for n, v in enumerate(VEC)}

        def gcol(name, c):
            return cols[:, vec_at[name] + c:vec_at[name] + c + 1]

        class Phase:
            pass

        phases = []

        def phase(name, kind, units, kn, src, **more):
            p = Phase()
            p.name, p.kind, p.units, p.kn, p.src = name, kind, units, kn, src
            p.u0 = sum(q.units for q in phases)
            p.per_tile = 2 if kind == "down" else 1
            p.t0 = sum(q.units // q.per_tile for q in phases)
            p.norm = more.get("norm")
            p.gain = more.get("gain")
            p.res = more.get("res")
            p.factor = more.get("factor", 1.0)
            p.layer = more.get("layer", 0)
            p.ff = more.get("ff")
            p.rhs = more.get("rhs")
            p.n0 = more.get("n0", 0)
            phases.append(p)
            return p

        def cols_src(w):
            full = w.shape[1] // P * P
            v = w[:, 0:full].rearrange("(k p) (n c) -> n p k c", p=P, c=P)
            return lambda n: v[n] if isinstance(n, int) else v[bass.ds(n, 1)].rearrange("o p k c -> (o p) k c")

        n_norm = [0]
        n_res = [1]
        n_ff = [0]

        def ffn(which, l, gain_after):
            g = a[f"ffn{which}_w_gate"][l].rearrange("(k p) (n c) -> n p k c", p=P, c=P)
            u = a[f"ffn{which}_w_up"][l].rearrange("(k p) (n c) -> n p k c", p=P, c=P)
            dn = a[f"ffn{which}_w_down"][l].rearrange("(h k p) (n c) -> n h p k c", p=P, c=P, h=2)

            def gu(i, j):
                w = g if j % 2 == 0 else u
                return w[bass.ds(i * 2 + j // 2, 1)].rearrange("o p k c -> (o p) k c")

            def down(i, j):
                return dn[bass.ds(i * 2 + j // 2, 1), j % 2].rearrange("o p k c -> (o p) k c")
            gp = phase(f"ffn{which}_{l}_gu", "gateup", 2 * FC, KC, gu, norm=n_norm[0], ff=n_ff[0])
            dp = phase(f"ffn{which}_{l}_down", "down", 2 * KC, FH, down, gain=gain_after, res=n_res[0], factor=0.5,
                       ff=n_ff[0])
            n_norm[0] += 1
            n_res[0] += 1
            n_ff[0] += 1
            return [gp, dp]

        def by4(f):
            return lambda i, j: f(i * 4 + j)

        def out_proj(name, w, gain_after, l):
            p = phase(name, "out", KC, KC, by4(cols_src(w)), gain=gain_after, res=n_res[0], layer=l)
            n_res[0] += 1
            return p

        FF10 = ffn(1, 0, "g_mix:0")
        ML_IN = phase("ml_in", "proj", 24, KC, by4(cols_src(a["ml_w_in"][0])), norm=n_norm[0], n0=0)
        n_norm[0] += 1
        ML_OUT = out_proj("ml_out", a["ml_w_out"][0], "g_xattn:0", 0)

        def attn_phases(l):
            q = phase(f"xq_{l}", "q", KC, KC, by4(cols_src(a["xa_w_q"][l])), layer=l, norm=n_norm[0])
            k = phase(f"xk_{l}", "memkv", KC, KC, by4(cols_src(a["xa_w_k"][l])), layer=l, n0=0)
            v = phase(f"xv_{l}", "memkv", KC, KC, by4(cols_src(a["xa_w_v"][l])), layer=l, n0=KC)
            n_norm[0] += 1
            ou = out_proj(f"xo_{l}", a["xa_w_o"][l], f"g_ffn2:{l}", l)
            return [q, k, v, ou]
        XA0 = attn_phases(0)
        FF20 = ffn(2, 0, "g_ffn1:1")
        FF11 = ffn(1, 1, "g_mix:1")
        GD_IN = phase("gd_in", "conv", 24, KC, by4(cols_src(a["gd_w_in"][0][:, 0:3072])), norm=n_norm[0])
        n_norm[0] += 1
        GD_Z = phase("gd_z", "projz", 8, KC, by4(cols_src(a["gd_w_in"][0][:, 3072:4096])), n0=24)
        GD_OUT = out_proj("gd_out", a["gd_w_out"][0], "g_xattn:1", 1)
        XA1 = attn_phases(1)
        FF21 = ffn(2, 1, "g_final")
        N_NORM = n_norm[0]
        for p, q in zip(phases, phases[1:] + [None]):
            p.next = q
        assert all(p.units % 4 == 0 and p.t0 % 2 == 0 for p in phases)

        XG = 2 * KC * T * 4
        put = placed(base, room)
        xin = put("xin", [P, TB, D])
        xin_s = put("xin_s", [NS, D])
        vec_in = put("vec_in", [97, P])
        conv_in = put("conv_in", [96, P])

        put = placed(base, room)
        pm = put("pm", [P, 24, T])
        rest = base + 24 * T * 4
        put = placed(rest, room - 24 * T * 4)
        gm_hi = put("gm_hi", [P, KC, P], F32R)
        gm_lo = put("gm_lo", [P, KC, P], F32R)
        put = placed(rest, room - 24 * T * 4)
        ml_vN = put("ml_vN", [P, TB, D])
        ml_kw = put("ml_kw", [P, TB, 512])
        ml_PT = put("ml_PT", [P, 1280])
        ml_W = put("ml_W", [P, 1280])
        ml_Cst = put("ml_Cst", [P, MLH, 256])
        put = placed(rest, room - 24 * T * 4)
        ml_C = put("ml_C", [P, 2, NS, 256])
        ml_Vd = put("ml_Vd", [NS, NS, 256])
        ml_k8 = put("ml_k8", [NS, 512])
        ml_v8 = put("ml_v8", [NS, D])
        put = placed(rest, room - 24 * T * 4)
        ml_y_hi = put("ml_y_hi", [P, KC, T], F32R)
        ml_y_lo = put("ml_y_lo", [P, KC, T], F32R)
        put = placed(base_xg, XG)
        rw = [put(f"rw{n}", [GH, T]) for n in range(8)]
        ml_Dg = put("ml_Dg", [P, TB, P])
        ml_sq = put("ml_sq", [P, 2, LP])
        ml_em = put("ml_em", [P, 16])
        ml_mrow = put("ml_mrow", [1, 512])
        ml_n0 = put("ml_n0", [32, P])
        ml_sb = put("ml_sb", [P, 100])
        ml_rs = put("ml_rs", [MLH, 32])
        ml_rse = put("ml_rse", [MLH, 32])
        ml_t8 = put("ml_t8", [P, 12, 64])
        masks_at = put

        put = placed(base, room)
        kvT = put("kvT", [P, 2 * KC, NMEM])
        vN = put("vN", [P, MT, D])
        kN = put("kN", [P, MT, D])
        qT = put("qT", [P, KC, T])
        at_now = base + (2 * KC * NMEM + 2 * MT * D + KC * T) * 4
        ay_hi = nc.alloc_sbuf_tensor_at("ay_hi", [P, KC, T], F32R, offset=at_now)
        ay_lo = nc.alloc_sbuf_tensor_at("ay_lo", [P, KC, T], F32R, offset=at_now + KC * T * 4)
        assert at_now + XG <= base + room
        memg_hi = nc.alloc_sbuf_tensor_at("memg_hi", [P, KC, NMEM], F32R, offset=at_now)
        memg_lo = nc.alloc_sbuf_tensor_at("memg_lo", [P, KC, NMEM], F32R, offset=at_now + KC * NMEM * 4)
        memN = nc.alloc_sbuf_tensor_at("memN", [P, MT, D], F32, offset=at_now - (MT * D + KC * T) * 4)
        put = placed(at_now + XG, room - (at_now + XG - base))
        memT = put("memT", [P, KC, NMEM])
        put = placed(at_now + XG, room - (at_now + XG - base))
        pr = put("pr", [P, TB, NMEM])
        prT = put("prT", [P, MT, LP])
        put = placed(base_xg, XG)
        RING = 4
        cache = put("cache", [P, RING, MT, D])

        put = placed(base, room)
        gp = put("gp", [P, 32, T])
        rest_g = base + 32 * T * 4
        put = placed(rest_g, room - 32 * T * 4)
        gg_hi = put("gg_hi", [P, KC, P], F32R)
        gg_lo = put("gg_lo", [P, KC, P], F32R)
        cst = put("cst", [P, 24, 24])
        st_in = put("st_in", [24, 3072])
        put = placed(rest_g, room - 32 * T * 4)
        gamr = put("gamr", [GH, LP])
        vNc = put("vNc", [P, GH, P])
        kdec = put("kdec", [P, GH, P])
        rr = put("rr", [P, GH, P])
        uu = put("uu", [P, GH, P])
        SS = put("SS", [P, GH, P])
        put = placed(rest_g, room - 32 * T * 4)
        gUd = put("gUd", [NS, 2, NS, P])
        gk8 = put("gk8", [NS, D])
        gu8 = put("gu8", [NS, D])
        gsm = put("gsm", [P, 6, 64])
        put = placed(base_xg, XG)
        gw = [put(f"gw{n}", [GH, T]) for n in range(6)]
        cvo = put("cvo", [11, 3072])
        gms = put("gms", [P, 2, 192])
        grt = put("grt", [P, 2, 192])
        put = placed(base_xg, XG)
        NT, X, Y, DT, XT, QKD, kTe, qTe = [put(n, [P, GH, P]) for n in
                                           ("NT", "X", "Y", "DT", "XT", "QKD", "kTe", "qTe")]
        put = placed(base_xg, XG)
        sS = put("sS", [P, 2, 4, NS, P])
        put = placed(base, 16 * T * 4)
        gy_hi = put("gy_hi", [P, KC, T], F32R)
        gy_lo = put("gy_lo", [P, KC, T], F32R)
        xs = keep[:, 0:264].rearrange("p (n t) -> p n t", n=24)

        def rhs_of(ph):
            if ph.kind == "down":
                return hid_hi, hid_lo
            if ph.name == "ml_out":
                return ml_y_hi, ml_y_lo
            if ph.name == "gd_out":
                return gy_hi, gy_lo
            if ph.name.startswith("xo"):
                return ay_hi, ay_lo
            if ph.kind == "memkv":
                return memg_hi, memg_lo
            return xg_hi, xg_lo

        def pe_unit(pe, ph, j, i, extra=None):
            t = j // 2 if ph.per_tile == 2 else j
            pair, slot = t % 2, j % 2
            u = ph.u0 + j
            tau = ph.t0 + t
            hi, lo = rhs_of(ph)
            k0 = (j % 2) * FH if ph.per_tile == 2 else 0
            first, last = (j % 2 == 0, j % 2 == 1) if ph.per_tile == 2 else (True, True)
            pe.wait_ge(w_split, i * 4 + (u + 1))
            if first and not (tau < 2 and isinstance(i, int) and i == 0):
                pe.wait_ge(acc_free, i * (4 // ph.per_tile) + (tau - 1))
            for k in range(ph.kn):
                wh = w_hi[:, slot, k * P:(k + 1) * P]
                wl = w_lo[:, slot, k * P:(k + 1) * P]
                begin, end = first and k == 0, last and k == ph.kn - 1
                if extra:
                    extra(k)
                for h in range(1 if ph.kind == "memkv" else 2):
                    if ph.kind == "memkv":
                        out, m = ACC[:, 2 * pair, 0:NMEM], slice(0, NMEM)
                    else:
                        out, m = ACC[:, 2 * pair + h, 0:TH], slice(h * TH, h * TH + TH)
                    pe.matmul(out, wh, hi[:, k0 + k, m], start=begin, stop=False)
                    pe.matmul(out, wh, lo[:, k0 + k, m], start=False, stop=False)
                    mm = pe.matmul(out, wl, hi[:, k0 + k, m], start=False, stop=end)
            mm.then_inc(mm_done, 1)

        def pe_norm_tok(pe, r):
            pe.wait_ge(ssq_added, (KC - 1) * (r + 1))
            for g in range(NTG):
                mm = pe.matmul(M[0:TG, 0, g:g + 1], ssq[:, g * TG:(g + 1) * TG], ones[:, 0:1], start=True, stop=True)
            mm.then_inc(nrm_tok, 1)

        def pe_norm_bc(pe, r):
            pe.wait_ge(nrm_pow, r + 1)
            for g in range(NTG):
                out = M[:, 1, g * TG:(g + 1) * TG] if g < 4 else M[:, 2, 0:TG]
                mm = pe.matmul(out, rtok[:, g:g + 1].to_broadcast([TG, P]), ident[0:TG, 0:TG], start=True, stop=True)
            mm.then_inc(nrm_bc, 1)

        def pe_phase(pe, ph, before={}):
            r = ph.norm
            for j in range(4):
                def extra(k, j=j):
                    if j == 1 and k == 3 and r is not None:
                        pe_norm_bc(pe, r)
                    if j == 0 and ph.kind in ("gateup", "proj", "conv", "q"):
                        pe.wait_ge(xg_ready, KC * r + k + 1)
                    if j == 0 and ph.kind == "down" and k == 0:
                        pe.wait_ge(hid_ready, FC * (ph.ff + 1))
                if j in before:
                    before[j]()
                pe_unit(pe, ph, j, 0, extra)
                if j == 0 and r is not None:
                    pe_norm_tok(pe, r)
            if before:
                assert ph.units == 8
                for j in range(4):
                    if 4 + j in before:
                        before[4 + j]()
                    pe_unit(pe, ph, j, 1)
            elif ph.units > 4:
                with pe.Fori(1, ph.units // 4) as i:
                    for j in range(4):
                        pe_unit(pe, ph, j, i)

        def sp_phase(sp, ph, first=True, others=True):
            def unit(i, j):
                u = ph.u0 + j
                if not (isinstance(i, int) and u + 4 * i < 4):
                    sp.wait_ge(w_split, i * 4 + (u - 3))
                sp.dma_start(raw[:, j, 0:ph.kn * P].rearrange("p (k c) -> p k c", c=P), ph.src(i, j)).then_inc(w_in[j], 16)
            if first:
                for j in range(4):
                    unit(0, j)
            if others and ph.units > 4:
                with sp.Fori(1, ph.units // 4) as i:
                    for j in range(4):
                        unit(i, j)

        def act_split(act, ph, i, j, d):
            u, q = ph.u0 + j + d, ph
            n = q.kn * P
            act.wait_ge(w_in[(j + d) % 4], i * 16 + 16 * (u // 4 + 1))
            if d == 2:
                act.wait_ge(mm_done, i * 4 + (u - 1))
            act.activation(w_hi[:, j % 2, 0:n], raw[:, (j + d) % 4, 0:n], ACT.Copy).then_inc(w_hi_done, 1)

        def dve_split(dve, ph, i, j, d):
            u = ph.u0 + j + d
            n = ph.kn * P
            dve.wait_ge(w_hi_done, i * 4 + (u + 1))
            dve.tensor_tensor(w_lo[:, j % 2, 0:n], raw[:, (j + d) % 4, 0:n], w_hi[:, j % 2, 0:n].bitcast(F32),
                              ALU.subtract).then_inc(w_split, 1)

        def split_next(split, eng, ph, j):
            q = ph.next
            u = q.u0 + j - 2
            n = q.kn * P
            s = j % 2
            if split is act_split:
                eng.wait_ge(w_in[j - 2], 16 * (u // 4 + 1))
                eng.wait_ge(mm_done, u - 1)
                eng.activation(w_hi[:, s, 0:n], raw[:, j - 2, 0:n], ACT.Copy).then_inc(w_hi_done, 1)
            else:
                eng.wait_ge(w_hi_done, u + 1)
                eng.tensor_tensor(w_lo[:, s, 0:n], raw[:, j - 2, 0:n], w_hi[:, s, 0:n].bitcast(F32),
                                  ALU.subtract).then_inc(w_split, 1)

        def act_chunk(act, c, res, gain, ready):
            ready()
            act.activation(xg_hi[:, c, :], x[:, c, :], ACT.Copy, scale=gcol(gain, c)).then_inc(xg_hi_done, 1)
            if c == 0:
                act.activation(ssq[:], x[:, c, :], ACT.Square).then_inc(sq_done, 1)
            else:
                if c > 2:
                    act.wait_ge(ssq_added, (KC - 1) * res + c - 2)
                elif res > 0:
                    act.wait_ge(ssq_added, (KC - 1) * res)
                act.activation(sq[:, c % 2, :], x[:, c, :], ACT.Square).then_inc(sq_done, 1)

        def dve_chunk(dve, c, res, gain):
            dve.wait_ge(xg_hi_done, KC * res + c + 1)
            dve.scalar_tensor_tensor(xg_lo[:, c, :], x[:, c, :], gcol(gain, c), xg_hi[:, c, :].bitcast(F32),
                                     ALU.mult, ALU.subtract).then_inc(xg_ready, 1)

        def pool_chunks(pool, res):
            for c in range(1, KC):
                pool.wait_ge(sq_done, KC * res + c + 1)
                if c > 1:
                    pool.wait_ge(ssq_added, (KC - 1) * res + c - 1)
                pool.tensor_tensor(ssq[:], ssq[:], sq[:, c % 2, :], ALU.add).then_inc(ssq_added, 1)
            pool.wait_ge(nrm_ms, res + 1)
            pool.tensor_tensor(rtok[:], msq[:], mhalf[0:TG, 0:NTG], ALU.pow).then_inc(nrm_pow, 1)

        def dve_norm(dve, own, r):
            dve.wait_ge(nrm_tok, r + 1)
            dve.tensor_scalar(msq[:], M[0:TG, 0, 0:NTG], 1.0 / D, EPS, ALU.mult, ALU.add).then_inc(nrm_ms, 1)
            dve.wait_ge(nrm_bc, r + 1)
            own.link(dve.tensor_copy(R[:, 0:4 * TG], M[:, 1, 0:4 * TG]))
            own.link(dve.tensor_copy(R[:, 4 * TG:T], M[:, 2, 0:TG]))

        def acc_of(pair):
            return ACC[:, 2 * pair:2 * pair + 2, 0:TH]

        def act_phase(act, ph, after={}):
            its = ph.units // 4
            assert not after or its == 2

            def step(i, j, last):
                split_ahead(act_split, act, ph, i, j, last)
                if ph.kind == "gateup" and j % 2 == 0:
                    act.wait_ge(acc_free, i * 4 + (ph.t0 + j + 1))
                    act.activation(tmp[:, 1, 0:T], tmp[:, 0, 0:T], ACT.Silu).then_inc(silu_done, 1)
                if ph.res is not None and (ph.kind == "out" or j % 2 == 1):
                    c = 4 * i + j if ph.kind == "out" else 2 * i + j // 2
                    act_chunk(act, c, ph.res, ph.gain, lambda: act.wait_ge(acc_free, ph.t0 + c + 1))
                if ph.kind == "conv" and not (isinstance(i, int) and i == 0 and j == 0):
                    conv_silu(i, j - 1)
                if after and 4 * i + j in after:
                    after[4 * i + j]()

            def conv_silu(i, j):
                act.wait_ge(cv_acc, i * 4 + (j + 1))
                act.activation(gp[:, bass.ds(i * 4 + j, 1), 0:LP].rearrange("p o t -> p (o t)"),
                               sq[:, (j + 4) % 2, 0:LP], ACT.Silu).then_inc(cv_silu, 1)
            start = 0
            if ph.kind == "conv":
                start = 1
                for j in range(4):
                    step(0, j, False)
            if ph.kind in ("gateup", "proj", "projz", "conv") and its > 1 and not after:
                with act.Fori(start, its - 1) as i:
                    for j in range(4):
                        step(i, j, False)
            elif its > 1:
                for i in range(its - 1):
                    for j in range(4):
                        step(i, j, False)
            for j in range(4):
                step(its - 1, j, True)
            if ph.kind == "conv":
                conv_silu(its - 1, 3)

        def dve_phase(dve, own, ph, after={}):
            its = ph.units // 4
            assert not after or its == 2
            links = {"gateup": 4, "conv": 16}.get(ph.kind, 0)

            def step(i, j, last):
                unit_step(i, j, last)
                if after and 4 * i + j in after:
                    after[4 * i + j]()

            def unit_step(i, j, last):
                split_ahead(dve_split, dve, ph, i, j, last)
                if ph.per_tile == 2 and j % 2 == 0:
                    return
                t = j // 2 if ph.per_tile == 2 else j
                pair = t % 2
                dve.wait_ge(mm_done, i * 4 + (ph.u0 + j + 1))
                tau1 = ph.t0 + t + 1
                if ph.kind == "gateup" and j % 2 == 0:
                    dve.tensor_tensor(halves(tmp[:, 0, 0:T]), acc_of(pair), halves(R[:]), ALU.mult).then_inc(acc_free, 1)
                elif ph.kind == "gateup":
                    n = i * 2 + j // 2
                    dve.tensor_tensor(halves(tmp[:, 2, 0:T]), acc_of(pair), halves(R[:]), ALU.mult).then_inc(acc_free, 1)
                    dve.wait_ge(acc_free, i * 4 + tau1)
                    dve.wait_ge(silu_done, i * 2 + (FC * ph.ff + j // 2 + 1))
                    own.link(dve.tensor_tensor(tmp[:, 2, 0:T], tmp[:, 1, 0:T], tmp[:, 2, 0:T], ALU.mult))
                    own.link(dve.tensor_copy(hid_hi[:, bass.ds(n, 1), :].rearrange("p o t -> p (o t)"), tmp[:, 2, 0:T]))
                    dve.tensor_tensor(hid_lo[:, bass.ds(n, 1), :].rearrange("p o t -> p (o t)"), tmp[:, 2, 0:T],
                                      hid_hi[:, bass.ds(n, 1), :].rearrange("p o t -> p (o t)").bitcast(F32),
                                      ALU.subtract).then_inc(hid_ready, 1)
                elif ph.res is not None:
                    c = 2 * i + t if ph.per_tile == 2 else 4 * i + t
                    dve.scalar_tensor_tensor(halves(x[:, c, :]), acc_of(pair), ph.factor, halves(x[:, c, :]),
                                             ALU.mult, ALU.add).then_inc(acc_free, 1)
                    dve_chunk(dve, c, ph.res, ph.gain)
                elif ph.kind in ("proj", "projz", "q"):
                    to = {"proj": pm, "projz": gp, "q": qT}[ph.kind]
                    n = i * 4 + (ph.n0 + j)
                    dst = to[:, bass.ds(n, 1), :].rearrange("p o (a b) -> p (o a) b", a=2)
                    dve.tensor_tensor(dst, acc_of(pair), halves(R[:]), ALU.mult).then_inc(acc_free, 1)
                elif ph.kind == "memkv":
                    dve.tensor_copy(kvT[:, ph.n0 + 4 * i + j, :], ACC[:, 2 * pair, 0:NMEM]).then_inc(acc_free, 1)
                elif ph.kind == "conv":
                    s = j % 2
                    n = i * 4 + j
                    dve.tensor_tensor(halves(tmp[:, s, 3:3 + T]), acc_of(pair), halves(R[:]), ALU.mult).then_inc(acc_free, 1)
                    dve.wait_ge(acc_free, i * 4 + tau1)
                    own.link(dve.tensor_copy(xs[:, bass.ds(n, 1), :].rearrange("p o t -> p (o t)"), tmp[:, s, LP:LP + 11]))
                    if s is not None and not (isinstance(i, int) and i == 0 and j < 2):
                        dve.wait_ge(cv_silu, i * 4 + (j - 1))

                    def w(tap):
                        return convw[:, bass.ds(i * 4 + (tap * 24 + j), 1)]
                    own.link(dve.tensor_scalar(sq[:, s, 0:LP], tmp[:, s, 0:LP], w(0), None, ALU.mult))
                    for tap in (1, 2, 3):
                        ins = dve.scalar_tensor_tensor(sq[:, s, 0:LP], tmp[:, s, tap:tap + LP], w(tap),
                                                       sq[:, s, 0:LP], ALU.mult, ALU.add)
                        if tap < 3:
                            own.link(ins)
                        else:
                            ins.then_inc(cv_acc, 1)
            if ph.kind == "conv":
                for j in range(4):
                    if j == 0:
                        own.link(dve.memset(tmp[:, 0:2, 0:3], 0.0))
                    if j == 0:
                        split_ahead(dve_split, dve, ph, 0, 0, False)
                        dve_norm(dve, own, ph.norm)
                        step_no_split(step, dve, ph, 0, j)
                    else:
                        step(0, j, False)
                with dve_loop(own, dve, 1, its - 1, 16) as i:
                    for j in range(4):
                        step(i, j, False)
                for j in range(4):
                    step(its - 1, j, True)
                return
            looped = ph.kind in ("gateup", "proj", "projz") and its > 1 and not after
            if ph.norm is not None:
                split_ahead(dve_split, dve, ph, 0, 0, its == 1)
                dve_norm(dve, own, ph.norm)
                step_no_split(step, dve, ph, 0, 0)
                for j in range(1, 4):
                    step(0, j, its == 1)
                start = 1
            else:
                start = 0
            if looped and its - 1 > start:
                with dve_loop(own, dve, start, its - 1, links) as i:
                    for j in range(4):
                        step(i, j, False)
            else:
                for i in range(start, its - 1):
                    for j in range(4):
                        step(i, j, False)
            if its - 1 >= start:
                for j in range(4):
                    step(its - 1, j, True)

        skip_split = [False]

        def step_no_split(step, dve, ph, i, j):
            skip_split[0] = True
            step(i, j, False)
            skip_split[0] = False
        def split_ahead(split, eng, ph, i, j, last):   
            if skip_split[0]:
                return
            if not last or j < 2:
                split(eng, ph, i, j, 2)
            elif ph.next is not None:
                split_next(split, eng, ph, j)

        @contextmanager
        def dve_loop(own, dve, lo, hi, per):
            own.base, own.k, own.per = own.base + own.k - lo * per, 0, per
            with dve.Fori(lo, hi) as i:
                own.i = i
                yield i
                assert own.k == per, (own.k, per)
            own.base, own.k, own.i = own.base + hi * per, 0, None

        def steps(name, names):
            return Steps(sem(name), [n if isinstance(n, tuple) else (n,) for n in names])

        su_pe = steps("su_pe", ["vec"] + [("x", c) for c in range(KC)])
        su_dve = steps("su_dve", ["vec", "xs"] + [("x", c) for c in range(KC)])
        su_pool = steps("su_pool", ["const"])
        g_split = sem("g_split")
        g_hi = sem("g_hi")
        g_in = sem("g_in")
        XA = [XA0, XA1]
        at_in = sem("at_in")
        c_in = [sem(f"c_in{n}") for n in range(RING)]
        kv_out = sem("kv_out")
        at_pe = steps("at_pe", ["memT", "q8"] + [("qb", b) for b in range(NS)] + [("kvN", n) for n in range(4)]
                      + [("s", 0), "sT", ("s", 1)]
                      + [x for h in range(XH) for x in [("t", h)] + ([("pv", 2 * h - 2), ("pv", 2 * h - 1)] if h > 0 else ["pT8"])
                         + [("o", h)] + ([("s", h + 2)] if h < XH - 2 else [])] + [("pv", 6), ("pv", 7)])
        at_act = steps("at_act", ["msq", "memr", "memhi"] + [("kvN", n) for n in range(4)] + [("e", 0), "e8"]
                       + [x for h in range(XH) for x in
                          [("pT", h)] + ([("e", h + 1)] if h < XH - 1 else []) + [("yh", h)]] + ["y8"])
        at_dve = steps("at_dve", ["ms", "memT", "memlo", "q8"] + [("sc", b) for b in range(NS)] + [("nb", 0), "nb8"]
                       + [x for h in range(XH) for x in [("pn", h)] + ([("nb", h + 1)] if h < XH - 1 else [])
                          + (["pn8", "pT8"] if h == 0 else []) + [("yl", h)]] + ["yl8"])
        at_pool = steps("at_pool", ["r"])

        def loads_of_setup():
            f = [(xin[:], a["x_prompt"][0].rearrange("(b p) d -> p b d", p=P)), (xin_s[:], a["x_sample"][:, 0, :])]
            for n, v in enumerate(VEC):
                name, l = (v.split(":") + [None])[:2]
                src = a[name] if l is None else a[name][int(l)]
                f.append((vec_in[n * KC:(n + 1) * KC, :], src.rearrange("(c p) -> c p", p=P)))
            f.append((vec_in[96:97, :], a["gd_g_out"]))
            f.append((conv_in[:], a["gd_conv_w"][0].rearrange("j (c p) -> (j c) p", p=P)))
            for n, v in enumerate(["ml_b_i", "ml_b_f", "gd_a_log", "gd_dt_bias"]):
                f.append((small[0:a[v].shape[1], n:n + 1], a[v].rearrange("o h -> h o")))
            return f
        SETUP = loads_of_setup()

        def sp_setup(sp):
            for dst, src in SETUP:
                sp.dma_start(dst, src).then_inc(ins_done, 16)

        def sp_gate(sp, w, c0, n):
            for k, at in ((0, 0), (1, 32)):
                sp.dma_start(gm_raw[:, :, at:at + n],
                             w[:, c0 + k * n:c0 + (k + 1) * n].rearrange("(k p) c -> p k c", p=P)).then_inc(g_in, 16)

        def pe_setup(pe):
            su_pool.wait(pe, "const")
            pe.wait_ge(ins_done, 16 * len(SETUP))
            pe.transpose(M[:, 0, 0:97], vec_in[:], ident[0:97, 0:97])
            pe.transpose(M[:, 0, 128:224], conv_in[:], ident[0:96, 0:96])
            for c in range(KC):
                mm = pe.transpose(M[:, 1, c * NS:(c + 1) * NS], xin_s[:, c * P:(c + 1) * P], ident[0:NS, 0:NS])
            su_pe.done(mm, "vec")
            for c in range(KC):
                if c >= 4:
                    su_dve.wait(pe, "x", c - 4)
                for b in range(TB):
                    mm = pe.transpose(ACC[:, c % 4, b * P:(b + 1) * P], xin[:, b, c * P:(c + 1) * P], ident[:])
                su_pe.done(mm, "x", c)
            su_dve.wait(pe, "x", KC - 1)

        def dve_setup(dve, own):
            own.link(dve.memset(tmp[:], 0.0))
            su_pe.wait(dve, "vec")
            own.link(dve.tensor_copy(cols[:], M[:, 0, 0:97]))
            su_dve.done(dve.tensor_copy(convw[:], M[:, 0, 128:224]), "vec")
            su_dve.done(dve.tensor_copy(x[:, :, LP:T], M[:, 1, 0:KC * NS].rearrange("p (c t) -> p c t", t=NS)), "xs")
            for c in range(KC):
                su_pe.wait(dve, "x", c)
                su_dve.done(dve.tensor_copy(x[:, c, 0:LP], ACC[:, c % 4, :]), "x", c)
                dve_chunk(dve, c, 0, "g_ffn1:0")

        def act_setup(act):
            for c in range(KC):
                act_chunk(act, c, 0, "g_ffn1:0", lambda: su_dve.wait(act, "x", c))

        def first_splits_act(act):
            for u in (0, 1):
                act.wait_ge(w_in[u], 16)
                act.activation(w_hi[:, u, 0:KC * P], raw[:, u, 0:KC * P], ACT.Copy).then_inc(w_hi_done, 1)

        def first_splits_dve(dve):
            for u in (0, 1):
                dve.wait_ge(w_hi_done, u + 1)
                dve.tensor_tensor(w_lo[:, u, 0:KC * P], raw[:, u, 0:KC * P], w_hi[:, u, 0:KC * P].bitcast(F32),
                                  ALU.subtract).then_inc(w_split, 1)

        def pool_setup(pool, own):
            own.link(pool.memset(ones[:], 1.0))
            own.link(pool.memset(mhalf[:], -0.5))
            own.link(pool.memset(gm_raw[:], 0.0))
            bd = [hid_lo[:, 0, n * P:(n + 1) * P].bitcast(F32) for n in range(2)] if False else None
            own.link(pool.memset(sq[:, 0, 0:P], 0.0))
            own.link(pool.affine_select(out=ident[:], in_=sq[:, 0, 0:P], compare_op=ALU.not_equal, fill=1.0, base=0,
                                        pattern=[[-1, P]], channel_multiplier=1))
            own.link(pool.affine_select(out=causal[:], in_=sq[:, 0, 0:P], compare_op=ALU.is_ge, fill=BIG, base=0,
                                        pattern=[[1, P]], channel_multiplier=-1))
            prev = ident[:]
            for l in range(7):
                B = 2 << l
                cur = sq[:, (l + 1) % 2, 0:P]
                v = cur.rearrange("p (n b) -> p n b", b=B)
                own.link(pool.memset(cur, 1.0))
                own.link(pool.affine_select(out=v, in_=v, compare_op=ALU.is_ge, fill=0.0, base=0,
                                            pattern=[[-B, P // B], [0, B]], channel_multiplier=1))
                own.link(pool.affine_select(out=v, in_=v, compare_op=ALU.is_ge, fill=0.0, base=B - 1,
                                            pattern=[[B, P // B], [0, B]], channel_multiplier=-1))
                ins = pool.tensor_tensor(level[:, l, :], cur, prev, ALU.subtract)
                if l < 6:
                    own.link(ins)
                prev = cur
            su_pool.done(ins, "const")

        rm = keep[:, 392:394]
        macc = keep[:, 390:392]
        sc = keep[:, 0:64]
        P32 = keep[0:32, 64:320]
        pT8 = keep[:, 320:384]

        def pool_cache(pool, l, phs):
            for n in range(2 * NS):
                if n < RING:
                    pool.wait_ge(mm_done, phs[1].u0)
                elif n - RING < NS:
                    at_dve.wait(pool, "sc", n - RING, r=l)
                else:
                    at_pe.wait(pool, "pv", n - RING - NS, r=l)
                src = a["cache_mem_k" if n < NS else "cache_mem_v"][l, n % NS].rearrange("(m p) h d -> p m (h d)", p=P)
                pool.dma_start(cache[:, n % RING], src).then_inc(c_in[n % RING], 16)

        def cache_wait(eng, l, n):
            eng.wait_ge(c_in[n % RING], 16 * ((l * 2 * NS + n) // RING + 1))

        def sp_mem(sp, l, phs):
            if l >= 0:
                sp.wait_ge(mm_done, phs[0].u0)
            sp.dma_start(memN[:], a["mem_prompt"][0].rearrange("(m p) d -> p m d", p=P)).then_inc(at_in, 16)

        def sp_kv_out(sp, l):
            at_act.wait(sp, "kvN", 1, r=l)
            sp.dma_start(o["mem_k"][l].rearrange("(m p) d -> p m d", p=P), kN[:]).then_inc(kv_out, 16)
            at_act.wait(sp, "kvN", 3, r=l)
            sp.dma_start(o["mem_v"][l].rearrange("(m p) d -> p m d", p=P), vN[:]).then_inc(kv_out, 16)

        def act_mem(act, own, l):
            def squares():
                act.wait_ge(at_in, 16 * (l + 1))
                for m in range(MT):
                    ins = act.activation(memT[:].rearrange("p c m -> p (c m)")[:, m * D:(m + 1) * D], memN[:, m, :],
                                         ACT.Square, accum_out=macc[:, m:m + 1])
                at_act.done(ins, "msq")

            def scaled():
                at_pool.wait(act, "r", r=l)
                for m in range(MT):
                    ins = act.activation(memN[:, m, :], memN[:, m, :], ACT.Copy, scale=rm[:, m:m + 1])
                at_act.done(ins, "memr")

            def high():
                at_dve.wait(act, "memT", r=l)
                for c in range(KC):
                    ins = act.activation(memg_hi[:, c, :], memT[:, c, :], ACT.Copy, scale=gcol(f"g_mem:{l}", c))
                at_act.done(ins, "memhi")
            return {1: squares, 3: scaled, 5: high}

        def dve_mem(dve, own, l):
            def mean():
                at_act.wait(dve, "msq", r=l)
                at_dve.done(dve.tensor_scalar(macc, macc, 1.0 / D, EPS, ALU.mult, ALU.add), "ms")

            def to_sbuf():
                at_pe.wait(dve, "memT", r=l)
                at_dve.done(dve.tensor_copy(memT[:].rearrange("p (b c) m -> p b (c m)", b=4), M[:]), "memT")

            def low():
                at_act.wait(dve, "memhi", r=l)
                for c in range(KC):
                    ins = dve.scalar_tensor_tensor(memg_lo[:, c, :], memT[:, c, :], gcol(f"g_mem:{l}", c),
                                                   memg_hi[:, c, :].bitcast(F32), ALU.mult, ALU.subtract)
                at_dve.done(ins, "memlo")
            return {1: mean, 4: to_sbuf, 6: low}

        def pool_mem(pool, l):
            at_dve.wait(pool, "ms", r=l)
            at_pool.done(pool.tensor_tensor(rm, macc, mhalf[:, 0:MT], ALU.pow), "r")

        def pe_mem(pe, l):
            pe.wait_ge(acc_free, XA[l][0].t0 + 2)
            at_act.wait(pe, "memr", r=l)
            for c in range(KC):
                for m in range(MT):
                    mm = pe.transpose(M[:, c // 2, (c % 2) * NMEM + m * P:(c % 2) * NMEM + (m + 1) * P],
                                      memN[:, m, c * P:(c + 1) * P], ident[:])
            at_pe.done(mm, "memT")

        def pe_kv_natural(pe, l, phs):
            pe.wait_ge(acc_free, phs[2].t0 + KC)
            at_dve.wait(pe, "sc", NS - 1, r=l)
            for n in range(4):
                b0 = 2 * (n % 2)
                if n >= 2:
                    at_act.wait(pe, "kvN", n - 2, r=l)
                for c in range(KC):
                    mm = pe.transpose(M[:, b0 + c // 4, (c % 4) * P:(c % 4 + 1) * P],
                                      kvT[:, (n // 2) * KC + c, (n % 2) * P:(n % 2 + 1) * P], ident[:])
                at_pe.done(mm, "kvN", n)

        def act_kv_natural(act, l):
            for n in range(4):
                b0 = 2 * (n % 2)
                at_pe.wait(act, "kvN", n, r=l)
                to = (kN if n < 2 else vN)[:, n % 2, :].rearrange("p (b c) -> p b c", b=2)
                at_act.done(act.activation(to, M[:, b0:b0 + 2, :], ACT.Copy), "kvN", n)

        SCALE = float(XD) ** -0.5

        def pe_queries(pe, l, phs):
            def by_token():
                pe.wait_ge(acc_free, phs[0].t0 + KC)
                for c in range(KC):
                    mm = pe.transpose(M[0:NS, c // 4, (c % 4) * P:(c % 4 + 1) * P], qT[:, c, LP:T], ident[:])
                at_pe.done(mm, "q8")

            def spread(b):
                if b == 0:
                    at_dve.wait(pe, "q8", r=l)
                if b >= 2:
                    at_dve.wait(pe, "sc", b - 2, r=l)
                for d in range(2):
                    mm = pe.matmul(M[:, 2 * ((b + 1) % 2) + d, :], ident[0:NS, b:b + 1].to_broadcast([NS, P]),
                                   q8n[0:NS, d * 512:(d + 1) * 512], start=True, stop=True)
                at_pe.done(mm, "qb", b)
            k = {1: by_token, 2: lambda: spread(0), 4: lambda: spread(1), 6: lambda: spread(2)}
            v = {0: lambda: spread(3), 2: lambda: spread(4), 4: lambda: spread(5), 6: lambda: spread(6)}
            return k, v, lambda: spread(7)

        def pe_attn(pe, l, phs):
            def scores(h):
                if h > 0:
                    at_act.wait(pe, "e", h - 1, r=l)
                for b in range(TB):
                    for k in range(2):
                        mm = pe.matmul(M[:, b // 2, (b % 2) * NMEM:(b % 2 + 1) * NMEM], qT[:, 2 * h + k, b * P:(b + 1) * P],
                                       kvT[:, 2 * h + k, :], start=k == 0, stop=k == 1)
                at_pe.done(mm, "s", h)

            def values(b):
                cache_wait(pe, l, NS + b)
                for c in range(KC):
                    for m in range(MT):
                        mm = pe.matmul(ACC[:, 2, c * NS + b:c * NS + b + 1], cache[:, (NS + b) % RING, m, c * P:(c + 1) * P],
                                       pT8[:, m * 32 + b * XH + c // 2:m * 32 + b * XH + c // 2 + 1], start=m == 0, stop=m == MT - 1)
                at_pe.done(mm, "pv", b)
            at_act.wait(pe, "kvN", 3, r=l)
            scores(0)
            for m in range(MT):
                mm = pe.transpose(ACC[0:32, 2, m * P:(m + 1) * P], sc[:, m * 32:(m + 1) * 32], ident[:])
            at_pe.done(mm, "sT")
            scores(1)
            for h in range(XH):
                at_dve.wait(pe, "pn", h, r=l)
                for m in range(MT):
                    for b in range(TB):
                        mm = pe.transpose(ACC[:, m, b * P:(b + 1) * P], pr[:, b, m * P:(m + 1) * P], ident[:])
                at_pe.done(mm, "t", h)
                if h == 0:
                    at_dve.wait(pe, "pn8", r=l)
                    for m in range(MT):
                        mm = pe.transpose(ACC[:, 3, m * 32:(m + 1) * 32], P32[:, m * P:(m + 1) * P], ident[0:32, 0:32])
                    at_pe.done(mm, "pT8")
                else:
                    if h == 1:
                        at_dve.wait(pe, "pT8", r=l)
                    values(2 * h - 2)
                    values(2 * h - 1)
                at_act.wait(pe, "pT", h, r=l)
                if h > 0:
                    at_dve.wait(pe, "yl", h - 1, r=l)
                for d in range(2):
                    for m in range(MT):
                        mm = pe.matmul(M[:, 2 + d, :], vN[:, m, (2 * h + d) * P:(2 * h + d + 1) * P], prT[:, m, :],
                                       start=m == 0, stop=m == MT - 1)
                at_pe.done(mm, "o", h)
                if h < XH - 2:
                    scores(h + 2)
            values(6)
            values(7)
            at_dve.wait(pe, "yl8", r=l)

        q8n = sq[:].rearrange("p a t -> p (a t)")[:, 0:D]
        st4 = tmp[:, 0, 0:4]
        nb4 = tmp[:, 0, 4:8]
        den4 = tmp[:, 0, 8:12]
        rd4 = tmp[:, 0, 12:16]
        st8, nb8, den8, rd8 = [tmp[0:32, 0, 16 + n:17 + n] for n in range(4)]

        def act_attn(act, own, l):
            def exps(h):
                at_dve.wait(act, "nb", h, r=l)
                for b in range(TB):
                    ins = act.activation(pr[:, b, :], M[:, b // 2, (b % 2) * NMEM:(b % 2 + 1) * NMEM], ACT.Exp,
                                         bias=nb4[:, b:b + 1], scale=SCALE, accum_out=den4[:, b:b + 1])
                at_act.done(ins, "e", h)
            exps(0)
            at_dve.wait(act, "nb8", r=l)
            at_act.done(act.activation(P32, ACC[0:32, 2, 0:NMEM], ACT.Exp, bias=nb8, scale=SCALE, accum_out=den8), "e8")
            for h in range(XH):
                at_pe.wait(act, "t", h, r=l)
                if h > 0:
                    at_pe.wait(act, "o", h - 1, r=l)
                at_act.done(act.activation(prT[:], ACC[:, 0:2, :], ACT.Copy), "pT", h)
                if h < XH - 1:
                    exps(h + 1)
                at_pe.wait(act, "o", h, r=l)
                at_act.done(act.activation(ay_hi[:, 2 * h:2 * h + 2, 0:LP], M[:, 2:4, :], ACT.Copy), "yh", h)
            at_pe.wait(act, "pv", NS - 1, r=l)
            at_act.done(act.activation(ay_hi[:, :, LP:T], ACC[:, 2, 0:KC * NS].rearrange("p (c b) -> p c b", b=NS), ACT.Copy), "y8")

        def dve_scores(dve, l):
            def sample_scores(b):
                if b == 0:
                    at_pe.wait(dve, "q8", r=l)
                    at_dve.done(dve.tensor_copy(q8n[0:NS, :].rearrange("p (a b) -> p a b", a=2), M[0:NS, 0:2, :]), "q8")
                at_pe.wait(dve, "qb", b, r=l)
                cache_wait(dve, l, b)
                for m in range(MT):
                    for h in range(XH):
                        kc = cache[:, b % RING, m, h * XD:(h + 1) * XD]
                        at = m * 32 + b * XH + h
                        ins = dve.tensor_tensor_reduce(kc, kc, M[:, 2 * ((b + 1) % 2) + h // 2, (h % 2) * XD:(h % 2 + 1) * XD],
                                                       1.0, 0.0, ALU.mult, ALU.add, sc[:, at:at + 1])
                at_dve.done(ins, "sc", b)
            do = [lambda b=b: sample_scores(b) for b in range(NS)]
            return {1: do[0], 3: do[1], 5: do[2], 7: do[3]}, {1: do[4], 3: do[5], 5: do[6]}, do[7]

        def dve_attn(dve, own, l):
            def lo(h):
                at_act.wait(dve, "yh", h, r=l)
                at_dve.done(dve.tensor_tensor(ay_lo[:, 2 * h:2 * h + 2, 0:LP], M[:, 2:4, :],
                                              ay_hi[:, 2 * h:2 * h + 2, 0:LP].bitcast(F32), ALU.subtract), "yl", h)

            def bound(h):
                at_pe.wait(dve, "s", h, r=l)
                own.link(dve.tensor_reduce(st4, M[:, 0:2, :].rearrange("p a (b m) -> p (a b) m", b=2), AX.X, ALU.max))
                at_dve.done(dve.tensor_scalar(nb4, st4, -SCALE, None, ALU.mult), "nb", h)

            bound(0)
            at_pe.wait(dve, "sT", r=l)
            own.link(dve.tensor_reduce(st8, ACC[0:32, 2, 0:NMEM], AX.X, ALU.max))
            at_dve.done(dve.tensor_scalar(nb8, st8, -SCALE, None, ALU.mult), "nb8")
            for h in range(XH):
                at_act.wait(dve, "e", h, r=l)
                own.link(dve.reciprocal(rd4, den4))
                at_dve.done(dve.tensor_tensor(pr[:], pr[:], rd4.unsqueeze(2).to_broadcast([P, TB, NMEM]), ALU.mult), "pn", h)
                if h < XH - 1:
                    bound(h + 1)
                if h == 0:
                    at_act.wait(dve, "e8", r=l)
                    own.link(dve.reciprocal(rd8, den8))
                    at_dve.done(dve.tensor_scalar(P32, P32, rd8, None, ALU.mult), "pn8")
                    at_pe.wait(dve, "pT8", r=l)
                    at_dve.done(dve.tensor_copy(pT8, ACC[:, 3, 0:64]), "pT8")
                lo(h)
            at_act.wait(dve, "y8", r=l)
            at_dve.done(dve.tensor_tensor(ay_lo[:, :, LP:T], ACC[:, 2, 0:KC * NS].rearrange("p (c b) -> p c b", b=NS),
                                          ay_hi[:, :, LP:T].bitcast(F32), ALU.subtract), "yl8")

        ml_pe = steps("ml_pe", [("vT", 0), ("vT", 1), "gates", ("vT", 2), ("vT", 3), "n0", "small"] + [("kT", b) for b in range(TB)]
                      + ["st", ("Mb", 0), ("S", 0)]
                      + [x for h in range(MLH) for x in [("num", h)] + ([("Mb", h + 1), ("S", h + 1)] if h < MLH - 1 else [])
                         + [("nsq", h)]]
                      + ["kv8", "n8"] + [x for h in range(MLH) for x in [("out", h), ("hs", h)]] + ["nsq8"]
                      + [("rb", h) for h in range(MLH)])
        ml_act = steps("ml_act", ["ksc"] + [("vN", b) for b in range(TB)] + ["lnf", "rse", "ex", "stc"]
                       + [x for h in range(MLH) for x in [("W", h), ("sqn", h)]] + ["sig"])
        ml_dve = steps("ml_dve", ["graw", "rows", "sb"] + [("kw", b) for b in range(TB)]
                       + [x for h in range(MLH) for x in [("dg", h), ("PT", h), ("tok", h)]]
                       + ["ms", "kv8", "n", "n8"] + [x for h in range(MLH) for x in [("Vd", h), ("C", h)]]
                       + ["sq8", "ms8", "y8"] + [("y", h) for h in range(MLH)])
        ml_pool = steps("ml_pool", ["rt", "r8"])
        ml_ld = sem("ml_ld")
        ml_cin = [sem(f"ml_cin{n}") for n in range(2)]
        ml_cout = [sem(f"ml_cout{n}") for n in range(2)]
        ml_out = sem("ml_out")
        g_raw_free = sem("g_raw_free")

        class MLstm:
            uT = keep[:, 0:16]
            emT = keep[:, 16:32]
            wkT = keep[0:NS, 32:36]
            wS = keep[:, 36:52]
            SB = keep[:, 64:164].rearrange("p (h x) -> p h x", h=MLH)
            n0T = keep[:, 170:202].rearrange("p (b h) -> p h b", h=MLH)
            dk = keep[:, 204:220]
            nk = keep[:, 220:236]
            rt = keep[:, 236:252]
            n0 = keep[0:32, 256:384]
            m0T = small[0:MLH, 4:12]
            off = [0, 512, 896, 1152]
            bo = [0, 0, 0, 0]
            Sbank = [(0, 0), (1, 0), (2, 0), (2, 256)]
            g4 = slice(0, MLH)

            def loads(self):
                return [(self.n0, a["state_mlstm_n"][0].rearrange("b h d -> (b h) d")),
                        (self.m0T, a["state_mlstm_m"][0].rearrange("b h -> h b"))]

            def sp_early(self, sp):
                for dst, src in self.loads():
                    sp.dma_start(dst, src, allow_slow_non_contiguous=True).then_inc(ml_ld, 16)
                su_pool.wait(sp, "const")
                sp_gate(sp, a["ml_w_in"][0], 3072, MLH)

            def sp_mid(self, sp):
                pass

            def c_load(self, sp, h):
                sp.dma_start(ml_C[:, h % 2], a["state_mlstm_C"][0, :, h].rearrange("b p e -> p b e")).then_inc(ml_cin[h % 2], 16)

            def sp(self, sp):
                ml_act.wait(sp, "stc")
                sp.dma_start(o["p_C"].rearrange("h p e -> p h e"), ml_Cst[:]).then_inc(ml_out, 16)
                sp.dma_start(o["p_n"], ml_mrow[:]).then_inc(ml_out, 16)
                sp.dma_start(o["p_m"], rw[1][self.g4, LP - 1:LP]).then_inc(ml_out, 16)
                sp.dma_start(o["s_m"].rearrange("b h -> h b"), rw[3][self.g4, 0:NS],
                             allow_slow_non_contiguous=True).then_inc(ml_out, 16)
                ml_pe.wait(sp, "num", MLH - 1)
                self.c_load(sp, 0)
                self.c_load(sp, 1)
                ml_dve.wait(sp, "n8")
                sp.dma_start(o["s_n"], ml_n0[:]).then_inc(ml_out, 16)
                for h in range(MLH):
                    ml_dve.wait(sp, "C", h)
                    sp.dma_start(o["s_C"][:, h].rearrange("b p e -> p b e"), ml_C[:, h % 2]).then_inc(ml_cout[h % 2], 16)
                    if h + 2 < MLH:
                        ml_pe.wait(sp, "hs", h)
                        sp.wait_ge(ml_cout[h % 2], 16 * (h // 2 + 1))
                        self.c_load(sp, h + 2)

            def sp_end(self, sp):
                sp.wait_ge(ml_out, 16 * 5)
                for q in ml_cout:
                    sp.wait_ge(q, 16 * MLH // 2)

            def pe(self, pe):
                pe.wait_ge(acc_free, ML_IN.t0 + ML_IN.units)
                for b in range(TB):
                    if b >= 2:
                        ml_act.wait(pe, "vN", b - 2)
                    for c in range(KC):
                        mm = pe.transpose(ACC[:, 2 * (b % 2) + c // 4, (c % 4) * P:(c % 4 + 1) * P],
                                          pm[:, 8 + c, b * P:(b + 1) * P], ident[:])
                    ml_pe.done(mm, "vT", b)
                    if b == 1:
                        ml_pe.done(pe_gates(pe, 0), "gates")
                pe.wait_ge(ml_ld, 32)
                ml_pe.done(pe.transpose(M[:, 0, 0:32], self.n0, ident[0:32, 0:32]), "n0")
                ml_act.wait(pe, "rse")
                for b in range(TB):
                    pe.transpose(M[:, 1, b * MLH:(b + 1) * MLH], rw[6][self.g4, b * P:(b + 1) * P], ident[self.g4, self.g4])
                    pe.transpose(M[:, 1, 16 + b * MLH:16 + (b + 1) * MLH], rw[1][self.g4, b * P:(b + 1) * P],
                                 ident[self.g4, self.g4])
                pe.transpose(M[0:NS, 1, 32:36], ml_rse[:, 8:16], ident[self.g4, self.g4])
                for h in range(MLH):
                    mm = pe.matmul(M[:, 1, 64 + 25 * h:89 + 25 * h], ident[self.g4, h:h + 1].to_broadcast([MLH, P]),
                                   ml_rse[:, 0:25], start=True, stop=True)
                ml_pe.done(mm, "small")
                ml_act.wait(pe, "vN", TB - 1)
                ml_act.wait(pe, "ksc")
                for b in range(TB):
                    for h in range(MLH):
                        mm = pe.transpose(ACC[:, b, h * P:(h + 1) * P], pm[:, MLH + h, b * P:(b + 1) * P], ident[:])
                    ml_pe.done(mm, "kT", b)
                ml_dve.wait(pe, "kw", TB - 1)
                for h in range(MLH):
                    for b in range(TB):
                        pe.matmul(M[:, 2 + h // 2, (h % 2) * 256:(h % 2 + 1) * 256], ml_kw[:, b, h * P:(h + 1) * P],
                                  ml_vN[:, b, h * 256:(h + 1) * 256], start=b == 0, stop=b == TB - 1)
                for b in range(TB):
                    mm = pe.matmul(M[0:1, 0, :], ones[:, 0:1], ml_kw[:, b, :], start=b == 0, stop=b == TB - 1)
                ml_pe.done(mm, "st")

                def scores(h):
                    if h > 0:
                        ml_act.wait(pe, "W", h - 1)
                    ml_pe.done(pe.matmul(M[:, 1, :], ident[self.g4, h:h + 1].to_broadcast([MLH, P]), rw[7][self.g4, 0:LP],
                                         start=True, stop=True), "Mb", h)
                    if h > 0:
                        ml_dve.wait(pe, "PT", h - 1)
                    for s in range(TB):
                        bank, at = self.Sbank[s]
                        mm = pe.matmul(ACC[:, bank, at:at + LP - s * P], pm[:, MLH + h, s * P:(s + 1) * P],
                                       pm[:, h, s * P:LP], start=True, stop=True)
                    ml_pe.done(mm, "S", h)
                scores(0)
                ml_act.wait(pe, "stc")
                for h in range(MLH):
                    ml_dve.wait(pe, "PT", h)
                    if h > 0:
                        ml_act.wait(pe, "sqn", h - 1)
                        ml_dve.wait(pe, "tok", h - 1)
                    for e in range(2):
                        for s in range(TB):
                            pe.matmul(M[:, 2 + e, s * P:LP], ml_vN[:, s, h * 256 + e * P:h * 256 + (e + 1) * P],
                                      ml_PT[:, self.off[s]:self.off[s] + LP - s * P], start=s == 0, stop=s == TB - 1)
                    for b in range(TB):
                        for s in range(b + 1):
                            at = self.off[s] + (b - s) * P
                            mm = pe.matmul(M[:, 0, b:b + 1], ml_PT[:, at:at + P], ones[:, 0:1], start=s == 0, stop=s == b)
                    ml_pe.done(mm, "num", h)
                    if h < MLH - 1:
                        scores(h + 1)
                    ml_act.wait(pe, "sqn", h)
                    for b in range(TB):
                        for e in range(2):
                            mm = pe.matmul(M[:, 0, 4 + b:5 + b], ml_sq[:, e, b * P:(b + 1) * P], ones[:, 0:1],
                                           start=e == 0, stop=e == 1)
                    ml_pe.done(mm, "nsq", h)
                ml_dve.wait(pe, "ms")
                for h in range(MLH):
                    pe.transpose(M[0:NS, 1, h * P:(h + 1) * P], pm[:, MLH + h, LP:T], ident[:])
                for c in range(KC):
                    mm = pe.transpose(ACC[0:NS, c // 4, (c % 4) * P:(c % 4 + 1) * P], pm[:, 8 + c, LP:T], ident[:])
                ml_pe.done(mm, "kv8")
                ml_dve.wait(pe, "n")
                pe.matmul(M[:, 3, 0:32], ones[:], ml_t8[:, 3, 0:32], start=True, stop=True)
                ml_pe.done(pe.transpose(M[0:32, 0, 0:P], ml_t8[:, 4, 0:32], ident[:]), "n8")
                for h in range(MLH):
                    ml_dve.wait(pe, "Vd", h)
                    for q in range(4):
                        mm = pe.matmul(ACC[:, q, :], ml_k8[:, h * P:(h + 1) * P],
                                       ml_Vd[:, 2 * q:2 * q + 2, :].rearrange("k b e -> k (b e)"), start=True, stop=True)
                    ml_pe.done(mm, "out", h)
                    ml_dve.wait(pe, "C", h)
                    for e in range(2):
                        for b in range(NS):
                            at = (h * 2 + e) * NS + b
                            mm = pe.matmul(M[:, 2, at:at + 1], ml_C[:, h % 2, b, e * P:(e + 1) * P], pm[:, h, LP + b:LP + b + 1],
                                           start=True, stop=True)
                    ml_pe.done(mm, "hs", h)
                ml_dve.wait(pe, "sq8")
                ml_pe.done(pe.matmul(M[:, 3, 64:128], ones[:], ml_t8[:, 8, :], start=True, stop=True), "nsq8")
                ml_pool.wait(pe, "rt")
                for h in range(MLH):
                    for b in range(TB):
                        mm = pe.matmul(ACC[:, h, b * P:(b + 1) * P],
                                       self.rt[:, b * MLH + h:b * MLH + h + 1].to_broadcast([P, P]), ident[:], start=True, stop=True)
                    ml_pe.done(mm, "rb", h)
                ml_dve.wait(pe, "y", MLH - 1)

            def act(self, act, own):
                act_gates(act, gm_hi, 0)
                act.wait_ge(acc_free, ML_IN.t0 + 8)
                ml_act.done(act.activation(pm[:, 4:8, :], pm[:, 4:8, :], ACT.Copy, scale=float(P) ** -0.5), "ksc")
                act.wait_ge(g_split, 1)
                for b in range(TB):
                    ml_pe.wait(act, "vT", b)
                    if b == 0:
                        ml_pe.wait(act, "gates")
                    ml_act.done(act.activation(ml_vN[:, b].rearrange("p (a c) -> p a c", a=2),
                                               ACC[:, 2 * (b % 2):2 * (b % 2) + 2, :], ACT.Copy), "vN", b)
                ml_dve.wait(act, "graw")
                g = self.g4
                own.link(act.activation(rw[2][g], rw[0][g], ACT.Identity, bias=small[g, 0:1]))
                own.link(act.activation(rw[3][g], rw[1][g], ACT.Abs, bias=small[g, 1:2]))
                own.link(act.activation(rw[3][g], rw[3][g], ACT.Exp, scale=-1.0))
                ml_act.done(act.activation(rw[3][g], rw[3][g], ACT.Ln, bias=ones[g, 0:1]), "lnf")
                ml_dve.wait(act, "rows")
                ml_act.done(act.activation(ml_rse[:, 0:24], ml_rs[:, 0:24], ACT.Exp), "rse")
                ml_dve.wait(act, "sb")
                act.activation(self.wS, self.wS, ACT.Exp)
                ml_act.done(act.activation(self.emT, self.emT, ACT.Exp, scale=-1.0), "ex")
                ml_pe.wait(act, "st")
                act.activation(ml_Cst[:].rearrange("p (a h) e -> p a (h e)", a=2), M[:, 2:4, :], ACT.Copy)
                ml_act.done(act.activation(ml_mrow[:], M[0:1, 0, :], ACT.Copy), "stc")
                for h in range(MLH):
                    ml_dve.wait(act, "dg", h)
                    if h > 0:
                        ml_dve.wait(act, "PT", h - 1)
                    for s in range(TB):
                        at = self.off[s]
                        u = self.uT[:, s * MLH + h:s * MLH + h + 1]
                        ins = act.activation(ml_W[:, at:at + P], ml_Dg[:, s, :], ACT.Exp, scale=-1.0, bias=u)
                        if s < TB - 1:
                            act.activation(ml_W[:, at + P:at + LP - s * P], M[:, 1, (s + 1) * P:LP], ACT.Exp, scale=-1.0, bias=u)
                    ml_act.done(ins, "W", h)
                    ml_pe.wait(act, "num", h)
                    if h > 0:
                        ml_pe.wait(act, "nsq", h - 1)
                    act.activation(ml_sq[:], M[:, 2:4, :], ACT.Square)
                    ml_act.done(act.activation(pm[:, 8 + 2 * h:10 + 2 * h, 0:LP], M[:, 2:4, :], ACT.Copy), "sqn", h)
                own.link(act.activation(pm[:, 16:24, :], pm[:, 16:24, :], ACT.Sigmoid))
                for c in range(KC):
                    ins = act.activation(pm[:, 16 + c, :], pm[:, 16 + c, :], ACT.Copy, scale=gcol("ml_g_head:0", c))
                ml_act.done(ins, "sig")
                act.wait_ge(ml_out, 16 * 5)

            def dve(self, dve, own):
                g = self.g4
                dve_gates(dve, gm_hi, gm_lo, 0)
                ml_pe.wait(dve, "gates")
                v2 = lambda ap: ap.rearrange("p (a b) -> p a b", a=2)
                dve.tensor_tensor(v2(rw[0][g]), M[g, 2:4, 0:TH], halves(R[g]), ALU.mult)
                ml_dve.done(dve.tensor_tensor(v2(rw[1][g]), M[32:36, 2:4, 0:TH], halves(R[32:36]), ALU.mult), "graw")
                ml_act.wait(dve, "lnf")
                own.link(dve.tensor_scalar(rw[4][g], rw[1][g], small[g, 1:2], 0.0, ALU.add, ALU.min))
                own.link(dve.tensor_tensor(rw[4][g], rw[4][g], rw[3][g], ALU.subtract))
                own.link(dve.tensor_tensor_scan(rw[5][g, 0:LP], ones[g, 0:1].to_broadcast([MLH, LP]), rw[4][g, 0:LP], 0.0,
                                                ALU.mult, ALU.add))
                own.link(dve.tensor_tensor(rw[6][g, 0:LP], rw[2][g, 0:LP], rw[5][g, 0:LP], ALU.subtract))
                own.link(dve.tensor_tensor_scan(rw[7][g, 0:LP], rw[6][g, 0:LP], rw[6][g, 0:LP], 0.0, ALU.max, ALU.max))
                own.link(dve.tensor_tensor(rw[1][g, 0:LP], rw[5][g, 0:LP], rw[7][g, 0:LP], ALU.add))
                own.link(dve.tensor_copy(ml_rse[:, 24:25], rw[7][g, LP - 1:LP]))
                dve.wait_ge(ml_ld, 32)
                m, am = rw[3][g, 0:NS], rw[3][g, NS:2 * NS]
                own.link(dve.tensor_tensor(am, rw[4][g, LP:T], self.m0T, ALU.add))
                own.link(dve.tensor_tensor(m, am, rw[2][g, LP:T], ALU.max))
                dve.tensor_tensor(ml_rs[:, 0:8], am, m, ALU.subtract)
                dve.tensor_tensor(ml_rs[:, 8:16], rw[2][g, LP:T], m, ALU.subtract)
                ml_dve.done(dve.tensor_scalar(ml_rs[:, 16:24], m, -1.0, None, ALU.mult), "rows")
                ml_pe.wait(dve, "small")
                own.link(dve.tensor_copy(keep[:, 0:32], M[:, 1, 0:32]))
                own.link(dve.tensor_copy(keep[0:NS, 32:36], M[0:NS, 1, 32:36]))
                own.link(dve.tensor_copy(keep[:, 64:164], M[:, 1, 64:164]))
                own.link(dve.tensor_copy(keep[:, 170:202], M[:, 0, 0:32]))
                ml_dve.done(dve.tensor_tensor(self.wS.rearrange("p (b h) -> p b h", h=MLH),
                                              self.uT.rearrange("p (b h) -> p b h", h=MLH),
                                              self.SB[:, :, 24].unsqueeze(1).to_broadcast([P, TB, MLH]), ALU.subtract), "sb")
                ml_act.wait(dve, "ex")
                for b in range(TB):
                    ml_pe.wait(dve, "kT", b)
                    ml_dve.done(dve.tensor_tensor(ml_kw[:, b].rearrange("p (h d) -> p h d", h=MLH),
                                                  ACC[:, b].rearrange("p (h d) -> p h d", h=MLH),
                                                  self.wS[:, b * MLH:(b + 1) * MLH].unsqueeze(2).to_broadcast([P, MLH, P]),
                                                  ALU.mult), "kw", b)
                for h in range(MLH):
                    ml_pe.wait(dve, "Mb", h)
                    if h > 0:
                        ml_act.wait(dve, "W", h - 1)
                    ml_dve.done(dve.tensor_tensor(ml_Dg[:], M[:, 1].rearrange("p (b t) -> p b t", b=TB),
                                                  causal[:].unsqueeze(1).to_broadcast([P, TB, P]), ALU.add), "dg", h)
                    ml_act.wait(dve, "W", h)
                    ml_pe.wait(dve, "S", h)
                    dve.tensor_tensor(ml_PT[:, 0:512], ml_W[:, 0:512], ACC[:, 0, :], ALU.mult)
                    dve.tensor_tensor(ml_PT[:, 512:896], ml_W[:, 512:896], ACC[:, 1, 0:384], ALU.mult)
                    ml_dve.done(dve.tensor_tensor(ml_PT[:, 896:1280], ml_W[:, 896:1280], ACC[:, 2, 0:384], ALU.mult), "PT", h)
                    ml_pe.wait(dve, "nsq", h)
                    own.link(dve.tensor_copy(self.dk.rearrange("p (b h) -> p b h", h=MLH)[:, :, h], M[:, 0, 0:4]))
                    ml_dve.done(dve.tensor_copy(self.nk.rearrange("p (b h) -> p b h", h=MLH)[:, :, h], M[:, 0, 4:8]), "tok", h)
                ml_dve.wait(dve, "tok", MLH - 1)
                own.link(dve.tensor_tensor(self.dk, self.dk, self.dk, ALU.mult))
                own.link(dve.tensor_tensor(self.emT, self.emT, self.emT, ALU.mult))
                own.link(dve.tensor_tensor(self.dk, self.dk, self.emT, ALU.max))
                own.link(dve.tensor_scalar(self.dk, self.dk, EPS, None, ALU.mult))
                ml_dve.done(dve.scalar_tensor_tensor(self.nk, self.nk, 1.0 / 256, self.dk, ALU.mult, ALU.add), "ms")
                ml_pe.wait(dve, "kv8")
                own.link(dve.tensor_copy(ml_k8[:], M[0:NS, 1, :]))
                ml_dve.done(dve.tensor_copy(ml_v8[:].rearrange("p (a b) -> p a b", a=2), ACC[0:NS, 0:2, :]), "kv8")
                t8 = lambda n: ml_t8[:, n, 0:32].rearrange("p (h b) -> p h b", h=MLH)
                wi, wk, em = self.SB[:, :, 0:8], self.SB[:, :, 8:16], self.SB[:, :, 16:24]
                own.link(dve.tensor_tensor(t8(0), self.n0T, wi, ALU.mult))
                own.link(dve.tensor_tensor(t8(1), pm[:, 4:8, LP:T], wk, ALU.mult))
                own.link(dve.tensor_tensor(t8(2), t8(0), t8(1), ALU.add))
                own.link(dve.tensor_tensor(t8(3), pm[:, 0:4, LP:T], t8(2), ALU.mult))
                ml_dve.done(dve.tensor_copy(ml_t8[:, 4, 0:32].rearrange("p (b h) -> p h b", h=MLH), t8(2)), "n")
                ml_pe.wait(dve, "n8")
                own.link(dve.tensor_tensor(t8(0), em, em, ALU.mult))
                own.link(dve.tensor_copy(ml_t8[:, 1, 0:32], M[:, 3, 0:32]))
                own.link(dve.tensor_tensor(t8(1), t8(1), t8(1), ALU.mult))
                own.link(dve.tensor_tensor(t8(5), t8(1), t8(0), ALU.max))
                own.link(dve.tensor_scalar(t8(5), t8(5), EPS, None, ALU.mult))
                ml_dve.done(dve.tensor_copy(ml_n0[:], M[0:32, 0, 0:P]), "n8")
                for h in range(MLH):
                    dw = ml_t8[0:NS, 6, 8 * h:8 * h + 8]
                    own.link(dve.tensor_scalar(dw, ident[0:NS, 0:NS], self.wkT[:, h:h + 1], None, ALU.mult))
                    ml_dve.done(dve.tensor_tensor(ml_Vd[:], ml_v8[:, h * 256:(h + 1) * 256].unsqueeze(1).to_broadcast([NS, NS, 256]),
                                                  dw.unsqueeze(2).to_broadcast([NS, NS, 256]), ALU.mult), "Vd", h)
                    ml_pe.wait(dve, "out", h)
                    dve.wait_ge(ml_cin[h % 2], 16 * (h // 2 + 1))
                    for b in range(NS):
                        ins = dve.scalar_tensor_tensor(ml_C[:, h % 2, b, :], ml_C[:, h % 2, b, :], self.SB[:, h, b:b + 1],
                                                       ACC[:, b // 2, (b % 2) * 256:(b % 2 + 1) * 256], ALU.mult, ALU.add)
                    ml_dve.done(ins, "C", h)
                ml_pe.wait(dve, "hs", MLH - 1)
                own.link(dve.tensor_copy(ml_t8[:, 7, :], M[:, 2, 0:64]))
                ml_dve.done(dve.tensor_tensor(ml_t8[:, 8, :], ml_t8[:, 7, :], ml_t8[:, 7, :], ALU.mult), "sq8")
                ml_pe.wait(dve, "nsq8")
                own.link(dve.tensor_copy(ml_t8[:, 9, :], M[:, 3, 64:128]))
                s4 = ml_t8[:, 9, :].rearrange("p (h e b) -> p h e b", h=MLH, e=2)
                own.link(dve.tensor_tensor(t8(10), s4[:, :, 0, :], s4[:, :, 1, :], ALU.add))
                ml_dve.done(dve.scalar_tensor_tensor(t8(10), t8(10), 1.0 / 256, t8(5), ALU.mult, ALU.add), "ms8")
                ml_pool.wait(dve, "r8")
                num = ml_t8[:, 7, :].rearrange("p (h e b) -> p h e b", h=MLH, e=2)
                own.link(dve.tensor_tensor(ml_t8[:, 0, :].rearrange("p (h e b) -> p h e b", h=MLH, e=2), num,
                                           t8(11).unsqueeze(2).to_broadcast([P, MLH, 2, NS]), ALU.mult))
                ml_act.wait(dve, "sig")
                y8 = ml_t8[:, 0, :].rearrange("p (c b) -> p c b", b=NS)
                own.link(dve.tensor_tensor(y8, y8, pm[:, 16:24, LP:T], ALU.mult))
                for q in ml_cout:
                    dve.wait_ge(q, 16 * MLH // 2)
                ml_pe.wait(dve, "nsq8")
                own.link(dve.tensor_copy(ml_y_hi[:, :, LP:T], y8))
                ml_dve.done(dve.tensor_tensor(ml_y_lo[:, :, LP:T], y8, ml_y_hi[:, :, LP:T].bitcast(F32), ALU.subtract), "y8")
                for h in range(MLH):
                    ml_pe.wait(dve, "rb", h)
                    c = slice(2 * h, 2 * h + 2)
                    n = pm[:, 8 + 2 * h:10 + 2 * h, 0:LP]
                    own.link(dve.tensor_tensor(n, n, ACC[:, h, :].unsqueeze(1).to_broadcast([P, 2, LP]), ALU.mult))
                    own.link(dve.tensor_tensor(n, n, pm[:, 16 + 2 * h:18 + 2 * h, 0:LP], ALU.mult))
                    own.link(dve.tensor_copy(ml_y_hi[:, c, 0:LP], n))
                    ml_dve.done(dve.tensor_tensor(ml_y_lo[:, c, 0:LP], n, ml_y_hi[:, c, 0:LP].bitcast(F32), ALU.subtract), "y", h)
                dve.wait_ge(ml_out, 16 * 5)

            def pool(self, pool, own):
                ml_dve.wait(pool, "ms")
                ml_pool.done(pool.tensor_tensor(self.rt, self.nk, mhalf[:, 0:16], ALU.pow), "rt")
                ml_dve.wait(pool, "ms8")
                ml_pool.done(pool.tensor_tensor(ml_t8[:, 11, 0:32], ml_t8[:, 10, 0:32], mhalf[:, 0:32], ALU.pow), "r8")

        def pe_gates(pe, n):
            pe.wait_ge(g_split, n + 1)
            hi, lo = (gm_hi, gm_lo) if n == 0 else (gg_hi, gg_lo)
            for k in range(KC):
                for h in range(2):
                    out, m = M[:, 2 + h, 0:TH], slice(h * TH, h * TH + TH)
                    pe.matmul(out, hi[:, k, :], xg_hi[:, k, m], start=k == 0, stop=False)
                    pe.matmul(out, hi[:, k, :], xg_lo[:, k, m], start=False, stop=False)
                    mm = pe.matmul(out, lo[:, k, :], xg_hi[:, k, m], start=False, stop=k == KC - 1)
            return mm

        def act_gates(act, hi, n):
            act.wait_ge(g_in, 32 * (n + 1))
            act.activation(hi[:], gm_raw[:], ACT.Copy).then_inc(g_hi, 1)

        def dve_gates(dve, hi, lo, n):
            dve.wait_ge(g_hi, n + 1)
            dve.tensor_tensor(lo[:], gm_raw[:], hi[:].bitcast(F32), ALU.subtract).then_inc(g_split, 1)
        MLX = MLstm()

        G2 = range(2)
        gd_pe = steps("gd_pe", ["cs", "gates", "cvA", "cvB"] + [("sq", n) for n in range(16)] + ["small"]
                      + [("nb", n) for n in range(16)]
                      + [x for c in range(TB) for x in
                         [(s, c, g) for g in G2 for s in ("gb", "kk", "qk", "v")] + [("kt", c, g) for g in G2]
                         + [("y", c, 0, g) for g in G2]
                         + [(s, c, l, g) for l in range(1, 7) for s in ("y", "xy") for g in G2]
                         + [(s, c, g) for s in ("ks", "u", "o", "ds") for g in G2 if s != "ks" or c > 0]]
                      + ["k8"] + [(s, q) for s in ("sk", "ut") for q in G2] + [("out", 0)]
                      + [y for h in range(GH) for y in ([("out", h + 1)] if h < GH - 1 else []) + [("o8", h)]]
                      + [("fs", h) for h in range(GH)] + [("fb", h) for h in range(GH)])
        gd_act = steps("gd_act", ["lg", "rse", "cs8"] + [("sq", n) for n in range(16)] + ["kd", "rt"]
                       + [x for c in range(TB) for x in [(s, c, g) for g in G2 for s in ("dt", "v")]
                          + [("y", c, l, g) for l in range(1, 7) for g in G2] + [("o", c, g) for g in G2]]
                       + ["z"] + [("fsq", h) for h in range(GH)] + ["fr"])
        gd_dve = steps("gd_dve", ["cst", "graw", "rows", "cs8", "cvA", "cvB", "small", "ms"] + [("nb", n) for n in range(16)]
                       + [x for c in range(TB) for x in
                          [("dg", c, g) for g in G2] + [("nt", c, g) for g in G2] + [("kd", c, g) for g in G2]
                          + [("x", c, l, g) for l in range(7) for g in G2]
                          + [(s, c, g) for s in ("r", "u", "s") for g in G2 if s != "r" or c > 0]]
                       + ["k8"] + [("u8", q) for q in G2] + [("Ud", 0)]
                       + [y for h in range(GH) for y in ([("Ud", h + 1)] if h < GH - 1 else []) + [("S8", h)]]
                       + ["o8", "fms", "fr", "y8"] + [("y", h) for h in range(GH)])
        gd_ld = sem("gd_ld")
        gd_st = sem("gd_st")
        gd_sst = sem("gd_sst")
        gd_sS = [sem(f"gd_sS{n}") for n in G2]

        class Gdn:
            g8 = slice(0, GH)
            gamT = keep[:, 264:296]
            betaT = keep[:, 296:328]
            kdS = keep[:, 328:360]
            egl = keep[:, 360:392]
            SB = keep[:, 0:160].rearrange("p (h x) -> p h x", h=GH)

            def bank(self, g, n):
                return (ACC if n < 2 else M)[:, 2 * g + n % 2, :]

            def four(self, ap):
                return ap.rearrange("p (h t) -> p h t", h=4)

            def per(self, ap, c, g):
                return ap[:, c * GH + 4 * g:c * GH + 4 * g + 4].unsqueeze(2).to_broadcast([P, 4, P])

            def sp_early(self, sp):
                sp.wait_ge(g_split, 1)
                sp_gate(sp, a["gd_w_in"][0], 4096, GH)

            def sp_mid(self, sp):
                sp.wait_ge(mm_done, GD_IN.u0)
                sp.dma_start(st_in[:], a["state_gdn_conv"][0].rearrange("b j f -> (b j) f")).then_inc(gd_ld, 16)

            def sp(self, sp):
                sp.dma_start(o["s_conv"][:, 0:2, :], a["state_gdn_conv"][0][:, 1:3, :]).then_inc(gd_st, 16)
                gd_dve.wait(sp, "cvB")
                sp.dma_start(o["p_conv"], cvo[0:3, :]).then_inc(gd_st, 16)
                sp.dma_start(o["s_conv"][:, 2, :], cvo[3:11, :]).then_inc(gd_st, 16)
                def load(q):
                    for hh in range(4):
                        sp.dma_start(sS[:, q, hh], a["state_gdn_S"][0, :, 4 * q + hh].rearrange("b p e -> p b e")).then_inc(gd_sS[q], 16)
                gd_dve.wait(sp, "x", TB - 1, 6, 1)
                load(0)
                for g in G2:
                    gd_dve.wait(sp, "s", TB - 1, g)
                gd_act.wait(sp, "o", TB - 1, 1)
                load(1)
                sp.dma_start(o["p_S"].rearrange("h p e -> p h e"), SS[:]).then_inc(gd_st, 16)
                for h in range(GH):
                    gd_dve.wait(sp, "S8", h)
                    sp.dma_start(o["s_S"][:, h].rearrange("b p e -> p b e"), sS[:, h // 4, h % 4]).then_inc(gd_sst, 16)

            def sp_end(self, sp):
                sp.wait_ge(gd_st, 16 * 4)
                sp.wait_ge(gd_sst, 16 * GH)

            def pe(self, pe):
                pe.wait_ge(acc_free, GD_Z.t0 + GD_Z.units)
                pe.wait_ge(gd_ld, 16)
                for n in range(24):
                    mm = pe.transpose(M[:, n // 12, (n % 12) * 24:(n % 12 + 1) * 24], st_in[:, n * P:(n + 1) * P],
                                      ident[0:24, 0:24])
                gd_pe.done(mm, "cs")
                gd_pe.done(pe_gates(pe, 1), "gates")
                for n in range(16):
                    mm = pe.transpose(ACC[0:11, n // 4, (n % 4) * P:(n % 4 + 1) * P], xs[:, n, :], ident[:])
                gd_pe.done(mm, "cvA")
                gd_dve.wait(pe, "cst")
                for n in range(8):
                    mm = pe.transpose(M[0:11, n // 4, (n % 4) * P:(n % 4 + 1) * P], xs[:, 16 + n, :], ident[:])
                gd_pe.done(mm, "cvB")
                gd_dve.wait(pe, "graw")
                for n in range(16):
                    gd_act.wait(pe, "sq", n)
                    for b in range(TB):
                        pe.matmul(M[:, 2, b * 16 + n:b * 16 + n + 1], sq[:, n % 2, b * P:(b + 1) * P], ones[:, 0:1],
                                  start=True, stop=True)
                    mm = pe.matmul(M[:, 3, n * NS:(n + 1) * NS], ones[:], sq[:, n % 2, LP:T], start=True, stop=True)
                    gd_pe.done(mm, "sq", n)
                gd_act.wait(pe, "rse")
                gd_dve.wait(pe, "cvB")
                for b in range(TB):
                    pe.transpose(M[:, 0, b * GH:(b + 1) * GH], gamr[:, b * P:(b + 1) * P], ident[self.g8, self.g8])
                    pe.transpose(M[:, 0, 32 + b * GH:32 + (b + 1) * GH], gw[0][:, b * P:(b + 1) * P], ident[self.g8, self.g8])
                for h in range(GH):
                    mm = pe.matmul(M[:, 0, 64 + 20 * h:84 + 20 * h], ident[self.g8, h:h + 1].to_broadcast([GH, P]),
                                   gw[4][:, 0:20], start=True, stop=True)
                gd_pe.done(mm, "small")
                gd_dve.wait(pe, "ms")
                for n in range(16):
                    if n >= 4:
                        gd_dve.wait(pe, "nb", n - 4)
                    elif n == 0:
                        gd_dve.wait(pe, "cvA")
                    for b in range(TB):
                        mm = pe.matmul(ACC[:, n % 4, b * P:(b + 1) * P],
                                       grt[:, 1, b * 16 + n:b * 16 + n + 1].to_broadcast([P, P]), ident[:], start=True, stop=True)
                    gd_pe.done(mm, "nb", n)
                gd_dve.wait(pe, "nb", 15)
                gd_act.wait(pe, "kd")
                for c in range(TB):
                    self.pe_chunk(pe, c)
                self.pe_sample(pe)
                for h in range(GH):
                    gd_act.wait(pe, "fsq", h)
                    for b in range(TB):
                        pe.matmul(M[:, 1, b * GH + h:b * GH + h + 1], sq[:, h % 2, b * P:(b + 1) * P], ones[:, 0:1],
                                  start=True, stop=True)
                    mm = pe.matmul(M[:, 2, h * NS:(h + 1) * NS], ones[:], sq[:, h % 2, LP:T], start=True, stop=True)
                    gd_pe.done(mm, "fs", h)
                gd_dve.wait(pe, "fr")
                for h in range(GH):
                    if h >= 4:
                        gd_dve.wait(pe, "y", h - 4)
                    for b in range(TB):
                        mm = pe.matmul(ACC[:, h % 4, b * P:(b + 1) * P],
                                       keep[:, b * GH + h:b * GH + h + 1].to_broadcast([P, P]), ident[:], start=True, stop=True)
                    gd_pe.done(mm, "fb", h)
                gd_dve.wait(pe, "y", GH - 1)

            def pe_chunk(self, pe, c):
                t = slice(c * P, (c + 1) * P)

                def heads(g, f):
                    for q in range(4):
                        mm = f(4 * g + q, slice(q * P, (q + 1) * P))
                    return mm
                for g in G2:
                    B = [self.bank(g, n) for n in range(4)]
                    if c > 0:
                        gd_dve.wait(pe, "s", c - 1, g)
                        gd_act.wait(pe, "o", c - 1, g)
                    gd_pe.done(heads(g, lambda h, q: pe.matmul(B[0][:, q], ident[self.g8, h:h + 1].to_broadcast([GH, P]),
                                                               gamr[:, t], start=True, stop=True)), "gb", c, g)
                    gd_pe.done(heads(g, lambda h, q: pe.matmul(B[1][:, q], gp[:, GH + h, t], gp[:, GH + h, t],
                                                               start=True, stop=True)), "kk", c, g)
                    gd_pe.done(heads(g, lambda h, q: pe.matmul(B[2][:, q], gp[:, GH + h, t], gp[:, h, t],
                                                               start=True, stop=True)), "qk", c, g)
                    gd_pe.done(heads(g, lambda h, q: pe.transpose(B[3][:, q], gp[:, 16 + h, t], ident[:])), "v", c, g)
                for g in G2:
                    gd_act.wait(pe, "dt", c, g)
                    gd_pe.done(heads(g, lambda h, q: pe.transpose(self.bank(g, 0)[:, q], gp[:, GH + h, t], ident[:])), "kt", c, g)
                for l in range(7):
                    for g in G2:
                        if l == 0:
                            gd_dve.wait(pe, "kd", c, g)
                        else:
                            gd_dve.wait(pe, "x", c, l - 1, g)
                        gd_pe.done(heads(g, lambda h, q: pe.matmul(self.bank(g, 1)[:, q], rr[:, h, :],
                                                                   ident[:] if l == 0 else X[:, h, :],
                                                                   start=True, stop=True)), "y", c, l, g)
                    for g in G2:
                        if l == 0:
                            continue
                        gd_act.wait(pe, "y", c, l, g)
                        if l == 1:
                            gd_act.wait(pe, "v", c, g)
                        if l < 6:
                            heads(g, lambda h, q: pe.matmul(self.bank(g, 2)[:, q], XT[:, h, :], Y[:, h, :], start=True, stop=True))
                        gd_pe.done(heads(g, lambda h, q: pe.matmul(self.bank(g, 3)[:, q], Y[:, h, :], XT[:, h, :],
                                                                   start=True, stop=True)), "xy", c, l, g)
                if c > 0:
                    for g in G2:
                        gd_dve.wait(pe, "x", c, 6, g)
                        gd_pe.done(heads(g, lambda h, q: pe.matmul(self.bank(g, 0)[:, q], kTe[:, h, :], SS[:, h, :],
                                                                   start=True, stop=True)), "ks", c, g)
                for g in G2:
                    gd_dve.wait(pe, *(("r", c, g) if c > 0 else ("x", c, 6, g)))
                    src = rr if c > 0 else vNc
                    gd_pe.done(heads(g, lambda h, q: pe.matmul(self.bank(g, 1)[:, q], XT[:, h, :], src[:, h, :],
                                                               start=True, stop=True)), "u", c, g)

                def out(h, q, g):
                    if c > 0:
                        pe.matmul(self.bank(g, 2)[:, q], SS[:, h, :], qTe[:, h, :], start=True, stop=False)
                    return pe.matmul(self.bank(g, 2)[:, q], uu[:, h, :], QKD[:, h, :], start=c == 0, stop=True)
                for g in G2:
                    gd_dve.wait(pe, "u", c, g)
                    gd_pe.done(heads(g, lambda h, q: out(h, q, g)), "o", c, g)
                for g in G2:
                    gd_pe.done(heads(g, lambda h, q: pe.matmul(self.bank(g, 3)[:, q], kdec[:, h, :], uu[:, h, :],
                                                               start=True, stop=True)), "ds", c, g)

            def pe_sample(self, pe):
                for g in G2:
                    gd_dve.wait(pe, "s", TB - 1, g)
                    gd_act.wait(pe, "o", TB - 1, g)
                for h in range(GH):
                    mm = pe.transpose(ACC[0:NS, h // 4, (h % 4) * P:(h % 4 + 1) * P], gp[:, GH + h, LP:T], ident[:])
                gd_pe.done(mm, "k8")
                gd_dve.wait(pe, "k8")
                for q in G2:
                    pe.wait_ge(gd_sS[q], 64)
                    for hh in range(4):
                        for b in range(NS):
                            at = hh * NS + b
                            mm = pe.matmul(M[:, q, at:at + 1], sS[:, q, hh, b, :], gp[:, GH + 4 * q + hh, LP + b:LP + b + 1],
                                           start=True, stop=True)
                    gd_pe.done(mm, "sk", q)
                for q in G2:
                    gd_dve.wait(pe, "u8", q)
                    for hh in range(4):
                        mm = pe.transpose(M[0:NS, 2 + q, hh * P:(hh + 1) * P], gsm[:, 1, (4 * q + hh) * NS:(4 * q + hh + 1) * NS],
                                          ident[:])
                    gd_pe.done(mm, "ut", q)

                def outer(h):
                    gd_dve.wait(pe, "Ud", h)
                    if h >= 2:
                        gd_dve.wait(pe, "S8", h - 2)
                    for k in range(2):
                        mm = pe.matmul(ACC[:, 2 * (h % 2) + k, :], gk8[:, h * P:(h + 1) * P],
                                       gUd[:, h % 2, 4 * k:4 * k + 4, :].rearrange("k b e -> k (b e)"), start=True, stop=True)
                    gd_pe.done(mm, "out", h)
                outer(0)
                for h in range(GH):
                    if h < GH - 1:
                        outer(h + 1)
                    gd_dve.wait(pe, "S8", h)
                    for b in range(NS):
                        mm = pe.matmul(M[:, 0, 64 + h * NS + b:65 + h * NS + b], sS[:, h // 4, h % 4, b, :],
                                       gp[:, h, LP + b:LP + b + 1], start=True, stop=True)
                    gd_pe.done(mm, "o8", h)

            def act(self, act, own):
                act_gates(act, gg_hi, 1)
                g = self.g8
                gd_dve.wait(act, "graw")
                own.link(act.activation(small[g, 12:13], small[g, 2:3], ACT.Exp))
                own.link(act.activation(gw[2][:], gw[1][:], ACT.Abs, bias=small[g, 3:4]))
                own.link(act.activation(gw[2][:], gw[2][:], ACT.Exp, scale=-1.0))
                own.link(act.activation(gw[2][:], gw[2][:], ACT.Ln, bias=ones[g, 0:1]))
                gd_act.done(act.activation(gw[0][:], gw[0][:], ACT.Sigmoid), "lg")
                gd_dve.wait(act, "rows")
                gd_act.done(act.activation(gw[4][:, 4:12], gw[4][:, 4:12], ACT.Exp), "rse")
                gd_dve.wait(act, "cs8")
                gd_act.done(act.activation(gp[:, 0:24, LP:T], gms[:, 0].rearrange("p (n b) -> p n b", b=NS), ACT.Silu), "cs8")
                gd_act.wait(act, "cs8")
                for n in range(16):
                    if n >= 2:
                        gd_pe.wait(act, "sq", n - 2)
                    gd_act.done(act.activation(sq[:, n % 2, :], gp[:, n, :], ACT.Square), "sq", n)
                gd_dve.wait(act, "small")
                act.activation(self.kdS, self.kdS, ACT.Exp)
                gd_act.done(act.activation(self.egl, self.egl, ACT.Exp), "kd")
                act.wait_ge(gms_ready, 1)
                gd_act.done(act.activation(grt[:, 1], grt[:, 0], ACT.Sqrt), "rt")
                for c in range(TB):
                    t = slice(c * P, (c + 1) * P)
                    for g in G2:
                        hs = slice(4 * g, 4 * g + 4)
                        gd_dve.wait(act, "dg", c, g)
                        act.activation(Y[:, hs], self.four(self.bank(g, 0)), ACT.Exp)
                        gd_act.done(act.activation(DT[:, hs], DT[:, hs], ACT.Exp), "dt", c, g)
                        gd_pe.wait(act, "v", c, g)
                        gd_act.done(act.activation(vNc[:, hs], self.four(self.bank(g, 3)), ACT.Copy), "v", c, g)
                    for l in range(1, 7):
                        for g in G2:
                            hs = slice(4 * g, 4 * g + 4)
                            gd_pe.wait(act, "y", c, l, g)
                            gd_act.done(act.activation(Y[:, hs], self.four(self.bank(g, 1)), ACT.Copy), "y", c, l, g)
                    for g in G2:
                        gd_pe.wait(act, "o", c, g)
                        gd_act.done(act.activation(gp[:, 16 + 4 * g:20 + 4 * g, t], self.four(self.bank(g, 2)), ACT.Copy), "o", c, g)
                own.link(act.activation(gp[:, 24:32, :], gp[:, 24:32, :], ACT.Silu))
                gd_act.done(act.activation(gp[:, 24:32, :], gp[:, 24:32, :], ACT.Copy, scale=cols[:, 96:97]), "z")
                gd_dve.wait(act, "o8")
                for h in range(GH):
                    if h >= 2:
                        gd_pe.wait(act, "fs", h - 2)
                    gd_act.done(act.activation(sq[:, h % 2, :], gp[:, 16 + h, :], ACT.Square), "fsq", h)
                gd_dve.wait(act, "fms")
                gd_act.done(act.activation(keep[:, 0:128], keep[:, 0:128], ACT.Sqrt), "fr")
                act.wait_ge(gd_sst, 16 * GH)

            def dve(self, dve, own):
                g = self.g8
                v2 = lambda ap: ap.rearrange("p (a b) -> p a b", a=2)
                dve_gates(dve, gg_hi, gg_lo, 1)
                gd_pe.wait(dve, "cs")
                gd_dve.done(dve.tensor_copy(cst[:].rearrange("p (a n) x -> p a n x", a=2),
                                            M[:, 0:2, 0:288].rearrange("p a (n x) -> p a n x", x=24)), "cst")
                gd_pe.wait(dve, "gates")
                dve.tensor_tensor(v2(gw[0][:]), M[0:GH, 2:4, 0:TH], halves(R[0:GH]), ALU.mult)
                gd_dve.done(dve.tensor_tensor(v2(gw[1][:]), M[32:40, 2:4, 0:TH], halves(R[32:40]), ALU.mult), "graw")
                gd_act.wait(dve, "lg")
                own.link(dve.tensor_scalar(gw[3][:], gw[1][:], small[g, 3:4], 0.0, ALU.add, ALU.max))
                own.link(dve.tensor_tensor(gw[3][:], gw[3][:], gw[2][:], ALU.add))
                own.link(dve.tensor_scalar(gw[3][:], gw[3][:], small[g, 12:13], -1.0, ALU.mult, ALU.mult))
                for b in range(TB):
                    own.link(dve.tensor_tensor_scan(gamr[:, b * P:(b + 1) * P], ones[g, 0:1].to_broadcast([GH, P]),
                                                    gw[3][:, b * P:(b + 1) * P], 0.0, ALU.mult, ALU.add))
                own.link(dve.tensor_copy(gw[4][:, 0:4], gamr[:].rearrange("p (b t) -> p b t", t=P)[:, :, P - 1]))
                own.link(dve.tensor_copy(gw[4][:, 12:20], gw[0][:, LP:T]))
                gd_dve.done(dve.tensor_copy(gw[4][:, 4:12], gw[3][:, LP:T]), "rows")
                cs = cst[:].rearrange("p n (b j) -> p n b j", j=3)
                acc, one = [gms[:, k].rearrange("p (n b) -> p n b", b=NS) for k in range(2)]
                cw = lambda j: convw[:, j * 24:(j + 1) * 24].unsqueeze(2).to_broadcast([P, 24, NS])
                own.link(dve.tensor_tensor(acc, cs[:, :, :, 0], cw(0), ALU.mult))
                for j in (1, 2, 3):
                    own.link(dve.tensor_tensor(one, cs[:, :, :, j] if j < 3 else xs[:, :, 3:11], cw(j), ALU.mult))
                    ins = dve.tensor_tensor(acc, acc, one, ALU.add)
                    if j < 3:
                        own.link(ins)
                gd_dve.done(ins, "cs8")
                gd_pe.wait(dve, "cvA")
                gd_dve.done(dve.tensor_copy(cvo[:, 0:2048].rearrange("p (a b) -> p a b", a=4), ACC[0:11]), "cvA")
                gd_pe.wait(dve, "cvB")
                gd_dve.done(dve.tensor_copy(cvo[:, 2048:3072].rearrange("p (a b) -> p a b", a=2), M[0:11, 0:2]), "cvB")
                gd_pe.wait(dve, "small")
                own.link(dve.tensor_copy(keep[:, 264:328], M[:, 0, 0:64]))
                own.link(dve.tensor_copy(keep[:, 0:160], M[:, 0, 64:224]))
                bh = lambda ap: ap.rearrange("p (b h) -> p b h", h=GH)
                glast = self.SB[:, :, 0:4].rearrange("p h b -> p b h")
                own.link(dve.tensor_copy(bh(self.egl), glast))
                gd_dve.done(dve.tensor_tensor(bh(self.kdS), glast, bh(self.gamT), ALU.subtract), "small")
                gd_pe.wait(dve, "sq", 15)
                own.link(dve.tensor_scalar(grt[:, 0, 0:64], M[:, 2, 0:64], EPS, None, ALU.add))
                dve.tensor_scalar(grt[:, 0, 64:192], M[:, 3, 0:128], EPS, None, ALU.add).then_inc(gms_ready, 1)
                gd_act.wait(dve, "rt")
                own.link(dve.reciprocal(grt[:, 1], grt[:, 1]))
                rq = grt[:, 1, 0:64].rearrange("p (b n) -> p b n", n=16)[:, :, 0:8]
                own.link(dve.tensor_scalar(grt[:, 1, 64:128], grt[:, 1, 64:128], float(P) ** -0.5, None, ALU.mult))
                gd_dve.done(dve.tensor_scalar(rq, rq, float(P) ** -0.5, None, ALU.mult), "ms")
                s8 = grt[:, 1, 64:192].rearrange("p (n b) -> p n b", b=NS)
                own.link(dve.tensor_tensor(gp[:, 0:16, LP:T], gp[:, 0:16, LP:T], s8, ALU.mult))
                for n in range(16):
                    gd_pe.wait(dve, "nb", n)
                    gd_dve.done(dve.tensor_tensor(gp[:, n, 0:LP], gp[:, n, 0:LP], ACC[:, n % 4, :], ALU.mult), "nb", n)
                dve.wait_ge(gd_st, 48)
                gd_dve.wait(dve, "nb", 15)
                for c in range(TB):
                    self.dve_chunk(dve, own, c)
                self.dve_sample(dve, own)
                gd_pe.wait(dve, "fs", GH - 1)
                own.link(dve.tensor_scalar(keep[:, 0:32], M[:, 1, 0:32], 1.0 / P, EPS, ALU.mult, ALU.add))
                own.link(dve.tensor_scalar(keep[:, 64:128], M[:, 2, 0:64], 1.0 / P, EPS, ALU.mult, ALU.add))
                gd_dve.done(dve.memset(keep[:, 32:64], 1.0), "fms")
                gd_act.wait(dve, "fr")
                own.link(dve.reciprocal(keep[:, 0:32], keep[:, 0:32]))
                gd_dve.done(dve.reciprocal(keep[:, 64:128], keep[:, 64:128]), "fr")
                gd_dve.wait(dve, "fr")
                n = gp[:, 16:24, LP:T]
                own.link(dve.tensor_tensor(n, n, keep[:, 64:128].rearrange("p (h b) -> p h b", b=NS), ALU.mult))
                own.link(dve.tensor_tensor(n, n, gp[:, 24:32, LP:T], ALU.mult))
                own.link(dve.tensor_copy(gy_hi[:, :, LP:T], n))
                gd_dve.done(dve.tensor_tensor(gy_lo[:, :, LP:T], n, gy_hi[:, :, LP:T].bitcast(F32), ALU.subtract), "y8")
                for h in range(GH):
                    gd_pe.wait(dve, "fb", h)
                    n = gp[:, 16 + h, 0:LP]
                    own.link(dve.tensor_tensor(n, n, ACC[:, h % 4, :], ALU.mult))
                    own.link(dve.tensor_tensor(n, n, gp[:, 24 + h, 0:LP], ALU.mult))
                    own.link(dve.tensor_copy(gy_hi[:, h, 0:LP], n))
                    gd_dve.done(dve.tensor_tensor(gy_lo[:, h, 0:LP], n, gy_hi[:, h, 0:LP].bitcast(F32), ALU.subtract), "y", h)
                dve.wait_ge(gd_sst, 16 * GH)

            def dve_chunk(self, dve, own, c):
                t = slice(c * P, (c + 1) * P)
                eye = ident[:].unsqueeze(1).to_broadcast([P, 4, P])
                for g in G2:
                    hs = slice(4 * g, 4 * g + 4)
                    gd_pe.wait(dve, "gb", c, g)
                    own.link(dve.tensor_tensor(DT[:, hs], self.four(self.bank(g, 0)), self.per(self.gamT, c, g), ALU.subtract))
                    gd_dve.done(dve.tensor_tensor(DT[:, hs], DT[:, hs], causal[:].unsqueeze(1).to_broadcast([P, 4, P]),
                                                  ALU.subtract), "dg", c, g)
                for g in G2:
                    hs = slice(4 * g, 4 * g + 4)
                    gd_act.wait(dve, "dt", c, g)
                    gd_pe.wait(dve, "kk", c, g)
                    own.link(dve.tensor_tensor(NT[:, hs], DT[:, hs], self.four(self.bank(g, 1)), ALU.mult))
                    own.link(dve.tensor_tensor(NT[:, hs], NT[:, hs], self.per(self.betaT, c, g), ALU.mult))
                    gd_pe.wait(dve, "qk", c, g)
                    dve.tensor_tensor(QKD[:, hs], DT[:, hs], self.four(self.bank(g, 2)), ALU.mult)
                    dve.tensor_tensor(kTe[:, hs], gp[:, GH + 4 * g:GH + 4 * g + 4, t], Y[:, hs], ALU.mult)
                    gd_dve.done(dve.tensor_tensor(qTe[:, hs], gp[:, 4 * g:4 * g + 4, t], Y[:, hs], ALU.mult), "nt", c, g)
                for g in G2:
                    hs = slice(4 * g, 4 * g + 4)
                    own.link(dve.tensor_tensor(rr[:, hs], NT[:, hs], level[:, 0].unsqueeze(1).to_broadcast([P, 4, P]), ALU.mult))
                    own.link(dve.tensor_tensor(XT[:, hs], eye, rr[:, hs], ALU.subtract))
                    gd_pe.wait(dve, "kt", c, g)
                    gd_dve.done(dve.tensor_tensor(kdec[:, hs], self.four(self.bank(g, 0)), self.per(self.kdS, c, g), ALU.mult),
                                "kd", c, g)
                for l in range(7):
                    for g in G2:
                        hs = slice(4 * g, 4 * g + 4)
                        if l == 0:
                            gd_pe.wait(dve, "y", c, 0, g)
                            ins = dve.tensor_tensor(X[:, hs], eye, self.four(self.bank(g, 1)), ALU.subtract)
                        else:
                            gd_pe.wait(dve, "xy", c, l, g)
                            if l < 6:
                                dve.tensor_tensor(X[:, hs], X[:, hs], self.four(self.bank(g, 2)), ALU.subtract)
                            ins = dve.tensor_tensor(XT[:, hs], XT[:, hs], self.four(self.bank(g, 3)), ALU.subtract)
                        if l < 6:
                            ins = dve.tensor_tensor(rr[:, hs], NT[:, hs], level[:, l + 1].unsqueeze(1).to_broadcast([P, 4, P]),
                                                    ALU.mult)
                        gd_dve.done(ins, "x", c, l, g)
                if c > 0:
                    for g in G2:
                        hs = slice(4 * g, 4 * g + 4)
                        gd_pe.wait(dve, "ks", c, g)
                        gd_dve.done(dve.tensor_tensor(rr[:, hs], vNc[:, hs], self.four(self.bank(g, 0)), ALU.subtract), "r", c, g)
                for g in G2:
                    hs = slice(4 * g, 4 * g + 4)
                    gd_pe.wait(dve, "u", c, g)
                    gd_dve.done(dve.tensor_tensor(uu[:, hs], self.four(self.bank(g, 1)), self.per(self.betaT, c, g), ALU.mult),
                                "u", c, g)
                for g in G2:
                    gd_pe.wait(dve, "ds", c, g)
                    hs = slice(4 * g, 4 * g + 4)
                    if c == 0:
                        ins = dve.tensor_copy(SS[:, hs], self.four(self.bank(g, 3)))
                    else:
                        for q in range(4):
                            h = 4 * g + q
                            ins = dve.scalar_tensor_tensor(SS[:, h, :], SS[:, h, :], self.egl[:, c * GH + h:c * GH + h + 1],
                                                           self.bank(g, 3)[:, q * P:(q + 1) * P], ALU.mult, ALU.add)
                    gd_dve.done(ins, "s", c, g)

            def dve_sample(self, dve, own):
                gd_pe.wait(dve, "k8")
                gd_dve.done(dve.tensor_copy(gk8[:].rearrange("p (a b) -> p a b", a=2), ACC[0:NS, 0:2, :]), "k8")
                for q in G2:
                    gd_pe.wait(dve, "sk", q)
                    gg, bb = self.SB[:, 4 * q:4 * q + 4, 4:12], self.SB[:, 4 * q:4 * q + 4, 12:20]
                    t = gsm[:, 0, 32 * q:32 * q + 32].rearrange("p (h b) -> p h b", b=NS)
                    own.link(dve.tensor_tensor(t, M[:, q, 0:32].rearrange("p (h b) -> p h b", b=NS), gg, ALU.mult))
                    own.link(dve.tensor_tensor(t, gp[:, 16 + 4 * q:20 + 4 * q, LP:T], t, ALU.subtract))
                    gd_dve.done(dve.tensor_tensor(gsm[:, 1, 32 * q:32 * q + 32].rearrange("p (h b) -> p h b", b=NS), t, bb,
                                                  ALU.mult), "u8", q)
                for q in G2:
                    gd_pe.wait(dve, "ut", q)
                    own.link(dve.tensor_copy(gu8[:, 512 * q:512 * (q + 1)], M[0:NS, 2 + q, :]))

                def diagonal(h):
                    gd_dve.done(dve.tensor_tensor(gUd[:, h % 2], gu8[:, h * P:(h + 1) * P].unsqueeze(1).to_broadcast([NS, NS, P]),
                                                  ident[0:NS, 0:NS].unsqueeze(2).to_broadcast([NS, NS, P]), ALU.mult), "Ud", h)
                diagonal(0)
                for h in range(GH):
                    if h < GH - 1:
                        diagonal(h + 1)
                    gd_pe.wait(dve, "out", h)
                    for b in range(NS):
                        s = sS[:, h // 4, h % 4, b, :]
                        ins = dve.scalar_tensor_tensor(s, s, self.SB[:, h, 4 + b:5 + b],
                                                       ACC[:, 2 * (h % 2) + b // 4, (b % 4) * P:(b % 4 + 1) * P],
                                                       ALU.mult, ALU.add)
                    gd_dve.done(ins, "S8", h)
                gd_pe.wait(dve, "o8", GH - 1)
                gd_dve.done(dve.tensor_copy(gp[:, 16:24, LP:T], M[:, 0, 64:128].rearrange("p (h b) -> p h b", b=NS)), "o8")
        gms_ready = sem("gms_ready")
        GDX = Gdn()

        fi_pe = steps("fi_pe", [("t", n) for n in range(TB + 1)])
        fi_act = steps("fi_act", [("g", c) for c in range(KC)])
        fi_dve = steps("fi_dve", [("y", n) for n in range(TB + 1)])
        put = placed(base, room)
        yf = put("yf", [P, TB + 1, D])
        fg = put("fg", [P, KC, T])
        rfin = put("rfin", [P, 8])
        NRES = n_res[0] - 1

        def pe_final(pe):
            pe.wait_ge(ssq_added, (KC - 1) * (NRES + 1))
            for b in range(TB + 1):
                n = P if b < TB else NS
                mm = pe.matmul(M[0:n, 0, b:b + 1], ssq[:, b * P:b * P + n], ones[:, 0:1], start=True, stop=True)
            mm.then_inc(nrm_tok, 1)
            fi_act.wait(pe, "g", KC - 1)
            for b in range(TB + 1):
                n = P if b < TB else NS
                s = ACC[:, 2 * (b % 2):2 * (b % 2) + 2, :]
                if b >= 2:
                    fi_dve.wait(pe, "y", b - 2)
                for c in range(KC):
                    mm = pe.transpose(s[0:n, c // 4, (c % 4) * P:(c % 4 + 1) * P], fg[:, c, b * P:b * P + n], ident[:])
                fi_pe.done(mm, "t", b)

        def act_final(act):
            for c in range(KC):
                fi_act.done(act.activation(fg[:, c, :], x[:, c, :], ACT.Copy, scale=gcol("g_final", c)), "g", c)

        def dve_final(dve, own):
            dve.wait_ge(nrm_tok, N_NORM + 1)
            own.link(dve.memset(rfin[:], 1.0))
            own.link(dve.tensor_scalar(rfin[:, 0:TB], M[:, 0, 0:TB], 1.0 / D, EPS, ALU.mult, ALU.add))
            dve.tensor_scalar(rfin[0:NS, TB:TB + 1], M[0:NS, 0, TB:TB + 1], 1.0 / D, EPS, ALU.mult, ALU.add).then_inc(nrm_ms, 1)
            dve.wait_ge(nrm_pow, NRES + 1)
            for b in range(TB + 1):
                n = P if b < TB else NS
                fi_pe.wait(dve, "t", b)
                fi_dve.done(dve.tensor_scalar(yf[0:n, b, :].rearrange("p (a c) -> p a c", a=2),
                                              ACC[0:n, 2 * (b % 2):2 * (b % 2) + 2, :], rfin[0:n, b:b + 1], None, ALU.mult), "y", b)

        def pool_final(pool, res):
            for c in range(1, KC):
                pool.wait_ge(sq_done, KC * res + c + 1)
                if c > 1:
                    pool.wait_ge(ssq_added, (KC - 1) * res + c - 1)
                pool.tensor_tensor(ssq[:], ssq[:], sq[:, c % 2, :], ALU.add).then_inc(ssq_added, 1)
            pool.wait_ge(nrm_ms, NRES + 1)
            pool.tensor_tensor(rfin[:, 0:TB + 1], rfin[:, 0:TB + 1], mhalf[:, 0:TB + 1], ALU.pow).then_inc(nrm_pow, 1)

        def sp_final(sp):
            for b in range(TB):
                fi_dve.wait(sp, "y", b)
                sp.dma_start(o["y_prompt"][b * P:(b + 1) * P, :], yf[:, b, :]).then_inc(stored, 16)
            fi_dve.wait(sp, "y", TB)
            sp.dma_start(o["y_sample"], yf[0:NS, TB, :]).then_inc(stored, 16)
            sp.wait_ge(stored, 16 * (TB + 1))
            sp.wait_ge(kv_out, 16 * 4)

        def sp_attention(sp, l, phs):
            sp_mem(sp, l, phs)
            for ph in phs[:3]:
                sp_phase(sp, ph)
            sp_phase(sp, phs[3], others=False)
            sp_kv_out(sp, l)
            sp_phase(sp, phs[3], first=False)

        def pe_attention(pe, l, phs):
            pe_phase(pe, phs[0], before={4: lambda: pe_mem(pe, l)})
            k, v, rest = pe_queries(pe, l, phs)
            at_dve.wait(pe, "memlo", r=l)
            pe_phase(pe, phs[1], before=k)
            pe_phase(pe, phs[2], before=v)
            rest()
            pe_kv_natural(pe, l, phs)
            pe_attn(pe, l, phs)
            pe_phase(pe, phs[3])

        def act_attention(act, own, l, phs):
            act_phase(act, phs[0], after=act_mem(act, own, l))
            act_phase(act, phs[1])
            act_phase(act, phs[2])
            act_kv_natural(act, l)
            act_attn(act, own, l)
            act_phase(act, phs[3])

        def dve_attention(dve, own, l, phs):
            dve_phase(dve, own, phs[0], after=dve_mem(dve, own, l))
            k, v, rest = dve_scores(dve, l)
            dve_phase(dve, own, phs[1], after=k)
            dve_phase(dve, own, phs[2], after=v)
            rest()
            dve_attn(dve, own, l)
            dve_phase(dve, own, phs[3])

        block = ctx.enter_context(nc.Block())

        @block.sync
        def _(sp):
            sp_setup(sp)
            MLX.sp_early(sp)
            for ph in FF10:
                sp_phase(sp, ph)
            MLX.sp_mid(sp)
            sp_phase(sp, ML_IN)
            sp_phase(sp, ML_OUT, others=False)
            MLX.sp(sp)
            sp_phase(sp, ML_OUT, first=False)
            GDX.sp_early(sp)
            sp_attention(sp, 0, XA0)
            for ph in FF20 + FF11:
                sp_phase(sp, ph)
            sp_phase(sp, GD_IN, others=False)
            GDX.sp_mid(sp)
            sp_phase(sp, GD_IN, first=False)
            sp_phase(sp, GD_Z)
            sp_phase(sp, GD_OUT, others=False)
            GDX.sp(sp)
            sp_phase(sp, GD_OUT, first=False)
            sp_attention(sp, 1, XA1)
            for ph in FF21:
                sp_phase(sp, ph)
            sp_final(sp)
            MLX.sp_end(sp)
            GDX.sp_end(sp)

        @block.tensor
        def _(pe):
            pe_setup(pe)
            for ph in FF10:
                pe_phase(pe, ph)
            pe_phase(pe, ML_IN)
            MLX.pe(pe)
            pe_phase(pe, ML_OUT)
            pe_attention(pe, 0, XA0)
            for ph in FF20 + FF11:
                pe_phase(pe, ph)
            pe_phase(pe, GD_IN)
            pe_phase(pe, GD_Z)
            GDX.pe(pe)
            pe_phase(pe, GD_OUT)
            pe_attention(pe, 1, XA1)
            for ph in FF21:
                pe_phase(pe, ph)
            pe_final(pe)

        @block.scalar
        def _(act):
            own = Own(act, act_own)
            first_splits_act(act)
            act_setup(act)
            for ph in FF10:
                act_phase(act, ph)
            act_phase(act, ML_IN)
            MLX.act(act, own)
            act_phase(act, ML_OUT)
            act_attention(act, own, 0, XA0)
            for ph in FF20 + FF11:
                act_phase(act, ph)
            act_phase(act, GD_IN)
            act_phase(act, GD_Z)
            GDX.act(act, own)
            act_phase(act, GD_OUT)
            act_attention(act, own, 1, XA1)
            for ph in FF21:
                act_phase(act, ph)
            act_final(act)

        @block.vector
        def _(dve):
            own = Own(dve, dve_own)
            first_splits_dve(dve)
            dve_setup(dve, own)
            for ph in FF10:
                dve_phase(dve, own, ph)
            dve_phase(dve, own, ML_IN)
            MLX.dve(dve, own)
            dve_phase(dve, own, ML_OUT)
            dve_attention(dve, own, 0, XA0)
            for ph in FF20 + FF11:
                dve_phase(dve, own, ph)
            dve_phase(dve, own, GD_IN)
            dve_phase(dve, own, GD_Z)
            GDX.dve(dve, own)
            dve_phase(dve, own, GD_OUT)
            dve_attention(dve, own, 1, XA1)
            for ph in FF21:
                dve_phase(dve, own, ph)
            dve_final(dve, own)

        @block.gpsimd
        def _(pool):
            own = Own(pool, pool_own)
            pool_setup(pool, own)
            pool_chunks(pool, 0)
            pool_chunks(pool, 1)
            MLX.pool(pool, own)
            pool_chunks(pool, 2)
            pool_mem(pool, 0)
            pool_cache(pool, 0, XA0)
            pool_chunks(pool, 3)
            pool_chunks(pool, 4)
            pool_chunks(pool, 5)
            pool_chunks(pool, 6)
            pool_mem(pool, 1)
            pool_cache(pool, 1, XA1)
            pool_chunks(pool, 7)
            pool_final(pool, NRES)


_INS = ['x_prompt', 'x_sample', 'mem_prompt', 'cache_mem_k', 'cache_mem_v', 'state_mlstm_C', 'state_mlstm_n',
        'state_mlstm_m', 'state_gdn_S', 'state_gdn_conv', 'g_ffn1', 'ffn1_w_gate', 'ffn1_w_up', 'ffn1_w_down', 'g_mix',
        'ml_w_in', 'ml_b_i', 'ml_b_f', 'ml_g_head', 'ml_w_out', 'gd_w_in', 'gd_conv_w', 'gd_a_log', 'gd_dt_bias',
        'gd_g_out', 'gd_w_out', 'g_xattn', 'g_mem', 'xa_w_q', 'xa_w_k', 'xa_w_v', 'xa_w_o', 'g_ffn2', 'ffn2_w_gate',
        'ffn2_w_up', 'ffn2_w_down', 'g_final']
_OUTS = [("y_prompt", (LP, D), (1, LP, D)), ("y_sample", (NS, D), (NS, 1, D)),
         ("mem_k", (2, NMEM, D), (2, 1, NMEM, XH, XD)), ("mem_v", (2, NMEM, D), (2, 1, NMEM, XH, XD)),
         ("p_C", (MLH, P, 256), (1, 1, MLH, P, 256)), ("p_n", (1, MLH * P), (1, 1, MLH, P)), ("p_m", (MLH, 1), (1, 1, MLH)),
         ("p_S", (GH, P, P), (1, 1, GH, P, P)), ("p_conv", (3, 3072), (1, 1, 3, 3072)),
         ("s_C", (NS, MLH, P, 256), (1, NS, MLH, P, 256)), ("s_n", (NS * MLH, P), (1, NS, MLH, P)),
         ("s_m", (NS, MLH), (1, NS, MLH)), ("s_S", (NS, GH, P, P), (1, NS, GH, P, P)),
         ("s_conv", (NS, 3, 3072), (1, NS, 3, 3072))]


def kernel(**inputs):
    import numpy as _np
    import concourse.bacc as _bacc
    from concourse import mybir as _mybir
    from concourse.bass_utils import run_bass_kernel_spmd as _run

    nc = _bacc.Bacc("TRN2", target_bir_lowering=False, num_devices=1)
    arrays, a, o = {}, {}, {}
    for name in _INS:
        v = _np.ascontiguousarray(inputs[name])
        arrays[f"in_{name}"] = v
        a[name] = nc.dram_tensor(f"in_{name}", v.shape, _mybir.dt.from_np(v.dtype), kind="ExternalInput").ap()
    for name, shape, _ in _OUTS:
        o[name] = nc.dram_tensor(f"out_{name}", shape, F32, kind="ExternalOutput").ap()
    program(nc, a, o)
    r = _run(nc, [arrays], core_ids=[0])
    return tuple(_np.asarray(r.results[0][f"out_{name}"]).reshape(full) for name, _, full in _OUTS)
```

```python
from contextlib import ExitStack, contextmanager

import concourse.bass as bass
from concourse import mybir

ALU = mybir.AluOpType
ACT = mybir.ActivationFunctionType
AX = mybir.AxisListType
F32 = mybir.dt.float32
F32R = mybir.dt.float32r
BF16 = mybir.dt.bfloat16

P = 128
D = 1024
KC = D // P
LP = 512
NS = 8
T = LP + NS
TH = T // 2
FF = 2816
FC = FF // P
FH = FC // 2
NTG = 5
TG = T // NTG
NMEM = 256
MT = NMEM // P
XH = 4
XD = D // XH
MLH = 4
MLQ = 512
GH = 8
EPS = 1e-6
TB = LP // P
BIG = 1e30


class Own:

    def __init__(self, eng, sem):
        self.eng, self.sem, self.base, self.k, self.i, self.per = eng, sem, 0, 0, None, 0

    def link(self, ins):
        self.k += 1
        ins.then_inc(self.sem, 1)
        n = self.base + self.k
        self.eng.wait_ge(self.sem, n if self.i is None else self.i * self.per + n)

    @contextmanager
    def loop(self, count, per):
        self.base, self.k, self.per = self.base + self.k, 0, per
        with self.eng.Fori(0, count) as i:
            self.i = i
            yield i
            assert self.k == per, (self.k, per)
        self.base, self.k, self.i = self.base + count * per, 0, None


class Steps:

    def __init__(self, sem, names):
        self.sem, self.n, self.at = sem, len(names), {x: k + 1 for k, x in enumerate(names)}
        assert len(self.at) == self.n
        self.told = 0

    def done(self, ins, *name, r=0):
        assert self.told % self.n + 1 == self.at[name], (name, self.told)
        self.told += 1
        ins.then_inc(self.sem, 1)

    def wait(self, eng, *name, r=0):
        eng.wait_ge(self.sem, r * self.n + self.at[name])


def halves(ap):
    return ap.rearrange("p (a b) -> p a b", a=2)


def program(nc, a, o):
    with ExitStack() as ctx:
        def sb(name, shape, dt=F32):
            return ctx.enter_context(nc.sbuf_tensor(name, shape, dt))

        def sem(name):
            return ctx.enter_context(nc.semaphore(name))

        x = sb("x", [P, KC, T])
        base_xg = nc.sbuf_base
        xg_hi = sb("xg_hi", [P, KC, T], F32R)
        xg_lo = sb("xg_lo", [P, KC, T], F32R)
        raw = sb("raw", [P, 4, FH * P])
        w_hi = sb("w_hi", [P, 2, FH * P], F32R)
        w_lo = sb("w_lo", [P, 2, FH * P], F32R)
        R = sb("R", [P, T])
        ssq = sb("ssq", [P, T])
        base_sq = nc.sbuf_base
        sq = sb("sq", [P, 2, T])
        base_tmp = nc.sbuf_base
        tmp = sb("tmp", [P, 3, T + 4])
        two = sb("two", [40, NS])
        two_r = sb("two_r", [40, NS], F32R)
        ident_r = sb("ident_r", [40, 40], F32R)
        ident = sb("ident", [P, P])
        ones = sb("ones", [P, P])
        pick = sb("pick", [P, 80])
        causal = sb("causal", [P, P], BF16)
        level = sb("level", [P, 7, P], BF16)
        mhalf = sb("mhalf", [P, 128])
        cols = sb("cols", [P, 97])
        convw = sb("convw", [P, 96])
        msq = sb("msq", [TG, NTG])
        rtok = sb("rtok", [TG, NTG])
        small = sb("small", [P, 16])
        gm_raw = sb("gm_raw", [P, KC, P])
        keep = sb("keep", [P, 400])
        base = nc.sbuf_base
        room = 2 * FC * T * 4
        ctx.enter_context(nc.sbuf_tensor("region", [P, room // 4], F32))

        def placed(start, room):
            at = [start]

            def put(name, shape, dt=F32):
                n = 4
                for k in shape[1:]:
                    n *= k
                t = nc.alloc_sbuf_tensor_at(name, shape, dt, offset=at[0])
                at[0] += (n + 31) // 32 * 32
                assert at[0] <= start + room, (name, at[0] - start - room)
                return t
            return put

        put = placed(base, room)
        hid_hi = put("hid_hi", [P, FC, T], F32R)
        hid_lo = put("hid_lo", [P, FC, T], F32R)

        ACC = ctx.enter_context(nc.psum_tensor("ACC", [P, 4, 512], F32))
        M = ctx.enter_context(nc.psum_tensor("M", [P, 4, 512], F32))

        w_in = [sem(f"w_in{s}") for s in range(4)]
        w_hi_done = sem("w_hi_done")
        w_split = sem("w_split")
        mm_done = sem("mm_done")
        acc_free = sem("acc_free")
        silu_done = sem("silu_done")
        hid_ready = sem("hid_ready")
        xg_hi_done = sem("xg_hi_done")
        xg_ready = sem("xg_ready")
        sq_done = sem("sq_done")
        ssq_added = sem("ssq_added")
        nrm_tok = sem("nrm_tok")
        nrm_ms = sem("nrm_ms")
        nrm_pow = sem("nrm_pow")
        nrm_bc = sem("nrm_bc")
        act_own = sem("act_own")
        dve_own = sem("dve_own")
        pool_own = sem("pool_own")
        ins_done = sem("ins_done")
        stored = sem("stored")
        cv_acc = sem("cv_acc")
        cv_silu = sem("cv_silu")

        VEC = ["g_ffn1:0", "g_ffn1:1", "g_mix:0", "g_mix:1", "g_xattn:0", "g_xattn:1", "g_mem:0", "g_mem:1",
               "g_ffn2:0", "g_ffn2:1", "g_final", "ml_g_head:0"]
        vec_at = {v: KC * n for n, v in enumerate(VEC)}

        def gcol(name, c):
            return cols[:, vec_at[name] + c:vec_at[name] + c + 1]

        class Phase:
            pass

        phases = []

        def phase(name, kind, units, kn, src, **more):
            p = Phase()
            p.name, p.kind, p.units, p.kn, p.src = name, kind, units, kn, src
            p.u0 = sum(q.units for q in phases)
            p.per_tile = 2 if kind == "down" else 1
            p.t0 = sum(q.units // q.per_tile for q in phases)
            p.norm = more.get("norm")
            p.gain = more.get("gain")
            p.res = more.get("res")
            p.factor = more.get("factor", 1.0)
            p.layer = more.get("layer", 0)
            p.ff = more.get("ff")
            p.rhs = more.get("rhs")
            p.n0 = more.get("n0", 0)
            phases.append(p)
            return p

        def cols_src(w):
            full = w.shape[1] // P * P
            v = w[:, 0:full].rearrange("(k p) (n c) -> n p k c", p=P, c=P)
            return lambda n: v[n] if isinstance(n, int) else v[bass.ds(n, 1)].rearrange("o p k c -> (o p) k c")

        n_norm = [0]
        n_res = [1]
        n_ff = [0]

        def ffn(which, l, gain_after):
            g = a[f"ffn{which}_w_gate"][l].rearrange("(k p) (n c) -> n p k c", p=P, c=P)
            u = a[f"ffn{which}_w_up"][l].rearrange("(k p) (n c) -> n p k c", p=P, c=P)
            dn = a[f"ffn{which}_w_down"][l].rearrange("(h k p) (n c) -> n h p k c", p=P, c=P, h=2)

            def gu(i, j):
                w = g if j % 2 == 0 else u
                return w[bass.ds(i * 2 + j // 2, 1)].rearrange("o p k c -> (o p) k c")

            def down(i, j):
                return dn[bass.ds(i * 2 + j // 2, 1), j % 2].rearrange("o p k c -> (o p) k c")
            gp = phase(f"ffn{which}_{l}_gu", "gateup", 2 * FC, KC, gu, norm=n_norm[0], ff=n_ff[0])
            dp = phase(f"ffn{which}_{l}_down", "down", 2 * KC, FH, down, gain=gain_after, res=n_res[0], factor=0.5,
                       ff=n_ff[0])
            n_norm[0] += 1
            n_res[0] += 1
            n_ff[0] += 1
            return [gp, dp]

        def by4(f):
            return lambda i, j: f(i * 4 + j)

        def out_proj(name, w, gain_after, l):
            p = phase(name, "out", KC, KC, by4(cols_src(w)), gain=gain_after, res=n_res[0], layer=l)
            n_res[0] += 1
            return p

        FF10 = ffn(1, 0, "g_mix:0")
        ML_IN = phase("ml_in", "proj", 24, KC, by4(cols_src(a["ml_w_in"][0])), norm=n_norm[0], n0=0)
        n_norm[0] += 1
        ML_OUT = out_proj("ml_out", a["ml_w_out"][0], "g_xattn:0", 0)

        def attn_phases(l):
            q = phase(f"xq_{l}", "q", KC, KC, by4(cols_src(a["xa_w_q"][l])), layer=l, norm=n_norm[0])
            k = phase(f"xk_{l}", "memkv", KC, KC, by4(cols_src(a["xa_w_k"][l])), layer=l, n0=0)
            v = phase(f"xv_{l}", "memkv", KC, KC, by4(cols_src(a["xa_w_v"][l])), layer=l, n0=KC)
            n_norm[0] += 1
            ou = out_proj(f"xo_{l}", a["xa_w_o"][l], f"g_ffn2:{l}", l)
            return [q, k, v, ou]
        XA0 = attn_phases(0)
        FF20 = ffn(2, 0, "g_ffn1:1")
        FF11 = ffn(1, 1, "g_mix:1")
        GD_IN = phase("gd_in", "conv", 24, KC, by4(cols_src(a["gd_w_in"][0][:, 0:3072])), norm=n_norm[0])
        n_norm[0] += 1
        GD_Z = phase("gd_z", "projz", 8, KC, by4(cols_src(a["gd_w_in"][0][:, 3072:4096])), n0=24)
        GD_OUT = out_proj("gd_out", a["gd_w_out"][0], "g_xattn:1", 1)
        XA1 = attn_phases(1)
        FF21 = ffn(2, 1, "g_final")
        N_NORM = n_norm[0]
        for p, q in zip(phases, phases[1:] + [None]):
            p.next = q
        assert all(p.units % 4 == 0 and p.t0 % 2 == 0 for p in phases)

        XG = 2 * KC * T * 4
        put = placed(base, room)
        xin = put("xin", [P, TB, D])
        xin_s = put("xin_s", [NS, D])
        vec_in = put("vec_in", [97, P])
        conv_in = put("conv_in", [96, P])

        put = placed(base, room)
        pm = put("pm", [P, 24, T])
        rest = base + 24 * T * 4
        put = placed(rest, room - 24 * T * 4)
        gm_hi = put("gm_hi", [P, KC, P], F32R)
        gm_lo = put("gm_lo", [P, KC, P], F32R)
        put = placed(rest, room - 24 * T * 4)
        ml_vN = put("ml_vN", [P, TB, D])
        ml_kw = put("ml_kw", [P, TB, 512])
        ml_PT = put("ml_PT", [P, 1280])
        ml_W = put("ml_W", [P, 1280])
        ml_Cst = put("ml_Cst", [P, MLH, 256])
        put = placed(rest, room - 24 * T * 4)
        ml_C = put("ml_C", [P, 2, NS, 256])
        ml_Vd = put("ml_Vd", [40, NS, 256], F32R)
        ml_k8 = put("ml_k8", [NS, 512])
        ml_k40 = put("ml_k40", [40, 2, 512], F32R)
        ml_v40 = put("ml_v40", [40, D], F32R)
        put = placed(rest, room - 24 * T * 4)
        ml_y_hi = put("ml_y_hi", [P, KC, T], F32R)
        ml_y_lo = put("ml_y_lo", [P, KC, T], F32R)
        put = placed(base_xg, XG)
        rw = [put(f"rw{n}", [GH, T]) for n in range(8)]
        ml_Dg = put("ml_Dg", [P, TB, P])
        ml_sq = put("ml_sq", [P, 2, LP])
        ml_em = put("ml_em", [P, 16])
        ml_mrow = put("ml_mrow", [1, 512])
        ml_n0 = put("ml_n0", [32, P])
        ml_sb = put("ml_sb", [P, 100])
        ml_rs = put("ml_rs", [MLH, 32])
        ml_rse = put("ml_rse", [MLH, 32])
        ml_t8 = put("ml_t8", [P, 12, 64])

        put = placed(base, room)
        kT_hi = put("kT_hi", [P, KC, NMEM], F32R)
        kT_lo = put("kT_lo", [P, KC, NMEM], F32R)
        at_v, at_q = base + 2 * KC * NMEM * 4, base + 3 * KC * NMEM * 4
        at_mem, at_pr, at_k = at_q + XG, at_q + XG + 2 * KC * NMEM * 4, at_q + XG + 3 * KC * NMEM * 4
        vT = put("vT", [P, KC, NMEM])
        q_hi = put("q_hi", [P, KC, T], F32R)
        q_lo = put("q_lo", [P, KC, T], F32R)
        memg_hi = put("memg_hi", [P, KC, NMEM], F32R)
        memg_lo = put("memg_lo", [P, KC, NMEM], F32R)
        memT = put("memT", [P, KC, NMEM])
        kT = put("kT", [P, KC, NMEM])
        memN = nc.alloc_sbuf_tensor_at("memN", [P, MT, D], F32, offset=at_v)
        vN = nc.alloc_sbuf_tensor_at("vN", [P, MT, D], F32, offset=at_v)
        vN_hi = nc.alloc_sbuf_tensor_at("vN_hi", [P, MT, D], F32R, offset=at_mem)
        vN_lo = nc.alloc_sbuf_tensor_at("vN_lo", [P, MT, D], F32R, offset=at_mem + MT * D * 4)
        kN = nc.alloc_sbuf_tensor_at("kN", [P, MT, D], F32, offset=at_pr)
        prT_hi = nc.alloc_sbuf_tensor_at("prT_hi", [P, MT, LP], F32R, offset=at_pr)
        prT_lo = nc.alloc_sbuf_tensor_at("prT_lo", [P, MT, LP], F32R, offset=at_pr + MT * LP * 4)
        pr = nc.alloc_sbuf_tensor_at("pr", [P, TB, NMEM], F32, offset=at_k)
        ay_hi, ay_lo = q_hi, q_lo
        put = placed(base_xg, XG)
        RING = 4
        cache = put("cache", [P, RING, MT, D])
        cache_r = nc.alloc_sbuf_tensor_at("cache_r", [P, RING, MT, D], F32R, offset=base_xg)

        put = placed(base, room)
        gp = put("gp", [P, 32, T])
        rest_g = base + 32 * T * 4
        put = placed(rest_g, room - 32 * T * 4)
        gg_hi = put("gg_hi", [P, KC, P], F32R)
        gg_lo = put("gg_lo", [P, KC, P], F32R)
        cst = put("cst", [P, 24, 24])
        at_st = rest_g + (2 * KC * P + 24 * 24) * 4
        st_in = put("st_in", [24, 3072])
        beta_r = put("beta_r", [GH, T])
        put = placed(rest_g, 2 * KC * P * 4)
        gamr = put("gamr", [GH, LP])
        la_r = put("la_r", [GH, T])
        lg_r = put("lg_r", [GH, T])
        gms = put("gms", [P, 2, 192])
        gsh = put("gsh", [GH, 44])
        put = placed(at_st, 3072 * 4)
        cvo = put("cvo", [11, 3072])
        put = placed(rest_g + LP * 4, room - (32 * T + LP) * 4)
        vNc = put("vNc", [P, GH, P])
        kdec = put("kdec", [P, GH, P])
        rr = put("rr", [P, GH, P])
        uu = put("uu", [P, GH, P])
        SS = put("SS", [P, GH, P])
        put = placed(rest_g, room - 32 * T * 4)
        gk40 = put("gk40", [40, 2, D], F32R)
        at_u = rest_g + 2 * D * 4
        gu40 = put("gu40", [40, D], F32R)
        gt8 = nc.alloc_sbuf_tensor_at("gt8", [NS, D], F32, offset=at_u)
        gUd = nc.alloc_sbuf_tensor_at("gUd", [40, 2, NS, P], F32R, offset=at_u + (D + LP) * 4)
        gk8 = nc.alloc_sbuf_tensor_at("gk8", [NS, D], F32, offset=at_u + (D + LP) * 4)
        gu8 = nc.alloc_sbuf_tensor_at("gu8", [NS, D], F32, offset=at_u + (D + LP) * 4)
        rf40 = nc.alloc_sbuf_tensor_at("rf40", [40, LP], F32R, offset=at_u + D * 4)
        rt_hi = nc.alloc_sbuf_tensor_at("rt_hi", [40, T], F32R, offset=base_tmp)
        rt_lo = nc.alloc_sbuf_tensor_at("rt_lo", [40, T], F32R, offset=base_tmp + T * 4)
        fsq0 = put("fsq0", [P, LP])
        fsqb = [fsq0, nc.alloc_sbuf_tensor_at("fsq1", [P, LP], F32, offset=at_st + 3072 * 4)]
        put = placed(base_xg, XG)
        NT, X, Y, DT, XT, QKD, kTe, qTe = [put(n, [P, GH, P]) for n in
                                           ("NT", "X", "Y", "DT", "XT", "QKD", "kTe", "qTe")]
        put = placed(base_xg, XG)
        sS = put("sS", [P, 2, 4, NS, P])
        put = placed(base, 16 * T * 4)
        gy_hi = put("gy_hi", [P, KC, T], F32R)
        gy_lo = put("gy_lo", [P, KC, T], F32R)
        q8f = keep[:, 64:128].rearrange("p (c b) -> p c b", b=NS)
        xs = keep[:, 0:264].rearrange("p (n t) -> p n t", n=24)

        def rhs_of(ph):
            if ph.kind == "down":
                return hid_hi, hid_lo
            if ph.name == "ml_out":
                return ml_y_hi, ml_y_lo
            if ph.name == "gd_out":
                return gy_hi, gy_lo
            if ph.name.startswith("xo"):
                return ay_hi, ay_lo
            if ph.kind == "memkv":
                return memg_hi, memg_lo
            return xg_hi, xg_lo

        def pe_unit(pe, ph, j, i, extra=None):
            t = j // 2 if ph.per_tile == 2 else j
            pair, slot = t % 2, j % 2
            u = ph.u0 + j
            tau = ph.t0 + t
            hi, lo = rhs_of(ph)
            k0 = (j % 2) * FH if ph.per_tile == 2 else 0
            first, last = (j % 2 == 0, j % 2 == 1) if ph.per_tile == 2 else (True, True)
            pe.wait_ge(w_split, i * 4 + (u + 1))
            if first and not (tau < 2 and isinstance(i, int) and i == 0):
                pe.wait_ge(acc_free, i * (4 // ph.per_tile) + (tau - 1))
            for k in range(ph.kn):
                wh = w_hi[:, slot, k * P:(k + 1) * P]
                wl = w_lo[:, slot, k * P:(k + 1) * P]
                begin, end = first and k == 0, last and k == ph.kn - 1
                if extra:
                    extra(k)
                for h in range(1 if ph.kind == "memkv" else 2):
                    if ph.kind == "memkv":
                        out, m = ACC[:, 2 * pair, 0:NMEM], slice(0, NMEM)
                    else:
                        out, m = ACC[:, 2 * pair + h, 0:TH], slice(h * TH, h * TH + TH)
                    pe.matmul(out, wh, hi[:, k0 + k, m], start=begin, stop=False)
                    pe.matmul(out, wh, lo[:, k0 + k, m], start=False, stop=False)
                    mm = pe.matmul(out, wl, hi[:, k0 + k, m], start=False, stop=end)
            mm.then_inc(mm_done, 1)

        def pe_norm_tok(pe, r):
            pe.wait_ge(ssq_added, (KC - 1) * (r + 1))
            for g in range(NTG):
                mm = pe.matmul(M[0:TG, 0, g:g + 1], ssq[:, g * TG:(g + 1) * TG], ones[:, 0:1], start=True, stop=True)
            mm.then_inc(nrm_tok, 1)

        def pe_norm_bc(pe, r):
            pe.wait_ge(nrm_pow, r + 1)
            for g in range(NTG):
                out = M[:, 1, g * TG:(g + 1) * TG] if g < 4 else M[:, 2, 0:TG]
                mm = pe.matmul(out, rtok[:, g:g + 1].to_broadcast([TG, P]), ident[0:TG, 0:TG], start=True, stop=True)
            mm.then_inc(nrm_bc, 1)

        def pe_phase(pe, ph, before={}):
            r = ph.norm
            for j in range(4):
                def extra(k, j=j):
                    if j == 1 and k == 3 and r is not None:
                        pe_norm_bc(pe, r)
                    if j == 0 and ph.kind in ("gateup", "proj", "conv", "q"):
                        pe.wait_ge(xg_ready, KC * r + k + 1)
                    if j == 0 and ph.kind == "down" and k == 0:
                        pe.wait_ge(hid_ready, FC * (ph.ff + 1))
                if j in before:
                    before[j]()
                pe_unit(pe, ph, j, 0, extra)
                if j == 0 and r is not None:
                    pe_norm_tok(pe, r)
            if before:
                assert ph.units == 8
                for j in range(4):
                    if 4 + j in before:
                        before[4 + j]()
                    pe_unit(pe, ph, j, 1)
            elif ph.units > 4:
                with pe.Fori(1, ph.units // 4) as i:
                    for j in range(4):
                        pe_unit(pe, ph, j, i)

        def sp_phase(sp, ph, first=True, others=True):
            def unit(i, j):
                u = ph.u0 + j
                if not (isinstance(i, int) and u + 4 * i < 4):
                    sp.wait_ge(w_split, i * 4 + (u - 3))
                sp.dma_start(raw[:, j, 0:ph.kn * P].rearrange("p (k c) -> p k c", c=P), ph.src(i, j)).then_inc(w_in[j], 16)
            if first:
                for j in range(4):
                    unit(0, j)
            if others and ph.units > 4:
                with sp.Fori(1, ph.units // 4) as i:
                    for j in range(4):
                        unit(i, j)

        def act_split(act, ph, i, j, d):
            u, q = ph.u0 + j + d, ph
            n = q.kn * P
            act.wait_ge(w_in[(j + d) % 4], i * 16 + 16 * (u // 4 + 1))
            if d == 2:
                act.wait_ge(mm_done, i * 4 + (u - 1))
            act.activation(w_hi[:, j % 2, 0:n], raw[:, (j + d) % 4, 0:n], ACT.Copy).then_inc(w_hi_done, 1)

        def dve_split(dve, ph, i, j, d):
            u = ph.u0 + j + d
            n = ph.kn * P
            dve.wait_ge(w_hi_done, i * 4 + (u + 1))
            dve.tensor_tensor(w_lo[:, j % 2, 0:n], raw[:, (j + d) % 4, 0:n], w_hi[:, j % 2, 0:n].bitcast(F32),
                              ALU.subtract).then_inc(w_split, 1)

        def split_next(split, eng, ph, j):
            q = ph.next
            u = q.u0 + j - 2
            n = q.kn * P
            s = j % 2
            if split is act_split:
                eng.wait_ge(w_in[j - 2], 16 * (u // 4 + 1))
                eng.wait_ge(mm_done, u - 1)
                eng.activation(w_hi[:, s, 0:n], raw[:, j - 2, 0:n], ACT.Copy).then_inc(w_hi_done, 1)
            else:
                eng.wait_ge(w_hi_done, u + 1)
                eng.tensor_tensor(w_lo[:, s, 0:n], raw[:, j - 2, 0:n], w_hi[:, s, 0:n].bitcast(F32),
                                  ALU.subtract).then_inc(w_split, 1)

        def act_chunk(act, c, res, gain, ready):
            ready()
            act.activation(xg_hi[:, c, :], x[:, c, :], ACT.Copy, scale=gcol(gain, c)).then_inc(xg_hi_done, 1)
            if c == 0:
                act.activation(ssq[:], x[:, c, :], ACT.Square).then_inc(sq_done, 1)
            else:
                if c > 2:
                    act.wait_ge(ssq_added, (KC - 1) * res + c - 2)
                elif res > 0:
                    act.wait_ge(ssq_added, (KC - 1) * res)
                act.activation(sq[:, c % 2, :], x[:, c, :], ACT.Square).then_inc(sq_done, 1)

        def dve_chunk(dve, c, res, gain):
            dve.wait_ge(xg_hi_done, KC * res + c + 1)
            dve.scalar_tensor_tensor(xg_lo[:, c, :], x[:, c, :], gcol(gain, c), xg_hi[:, c, :].bitcast(F32),
                                     ALU.mult, ALU.subtract).then_inc(xg_ready, 1)

        def pool_chunks(pool, res):
            for c in range(1, KC):
                pool.wait_ge(sq_done, KC * res + c + 1)
                if c > 1:
                    pool.wait_ge(ssq_added, (KC - 1) * res + c - 1)
                pool.tensor_tensor(ssq[:], ssq[:], sq[:, c % 2, :], ALU.add).then_inc(ssq_added, 1)
            pool.wait_ge(nrm_ms, res + 1)
            pool.tensor_tensor(rtok[:], msq[:], mhalf[0:TG, 0:NTG], ALU.pow).then_inc(nrm_pow, 1)

        def dve_norm(dve, own, r):
            dve.wait_ge(nrm_tok, r + 1)
            dve.tensor_scalar(msq[:], M[0:TG, 0, 0:NTG], 1.0 / D, EPS, ALU.mult, ALU.add).then_inc(nrm_ms, 1)
            dve.wait_ge(nrm_bc, r + 1)
            own.link(dve.tensor_copy(R[:, 0:4 * TG], M[:, 1, 0:4 * TG]))
            own.link(dve.tensor_copy(R[:, 4 * TG:T], M[:, 2, 0:TG]))

        def acc_of(pair):
            return ACC[:, 2 * pair:2 * pair + 2, 0:TH]

        def act_phase(act, ph, after={}):
            its = ph.units // 4
            assert not after or its == 2

            def step(i, j, last):
                split_ahead(act_split, act, ph, i, j, last)
                if ph.kind == "gateup" and j % 2 == 0:
                    act.wait_ge(acc_free, i * 4 + (ph.t0 + j + 1))
                    act.activation(tmp[:, 1, 0:T], tmp[:, 0, 0:T], ACT.Silu).then_inc(silu_done, 1)
                if ph.res is not None and (ph.kind == "out" or j % 2 == 1):
                    c = 4 * i + j if ph.kind == "out" else 2 * i + j // 2
                    act_chunk(act, c, ph.res, ph.gain, lambda: act.wait_ge(acc_free, ph.t0 + c + 1))
                if ph.kind == "conv" and not (isinstance(i, int) and i == 0 and j == 0):
                    conv_silu(i, j - 1)
                if after and 4 * i + j in after:
                    after[4 * i + j]()

            def conv_silu(i, j):
                act.wait_ge(cv_acc, i * 4 + (j + 1))
                act.activation(gp[:, bass.ds(i * 4 + j, 1), 0:LP].rearrange("p o t -> p (o t)"),
                               sq[:, (j + 4) % 2, 0:LP], ACT.Silu).then_inc(cv_silu, 1)
            start = 0
            if ph.kind == "conv":
                start = 1
                for j in range(4):
                    step(0, j, False)
            if ph.kind in ("gateup", "proj", "projz", "conv") and its > 1 and not after:
                with act.Fori(start, its - 1) as i:
                    for j in range(4):
                        step(i, j, False)
            elif its > 1:
                for i in range(its - 1):
                    for j in range(4):
                        step(i, j, False)
            for j in range(4):
                step(its - 1, j, True)
            if ph.kind == "conv":
                conv_silu(its - 1, 3)

        def dve_phase(dve, own, ph, after={}):
            its = ph.units // 4
            assert not after or its == 2
            links = {"gateup": 4, "conv": 16}.get(ph.kind, 0)

            def step(i, j, last):
                unit_step(i, j, last)
                if after and 4 * i + j in after:
                    after[4 * i + j]()

            def unit_step(i, j, last):
                split_ahead(dve_split, dve, ph, i, j, last)
                if ph.per_tile == 2 and j % 2 == 0:
                    return
                t = j // 2 if ph.per_tile == 2 else j
                pair = t % 2
                dve.wait_ge(mm_done, i * 4 + (ph.u0 + j + 1))
                tau1 = ph.t0 + t + 1
                if ph.kind == "gateup" and j % 2 == 0:
                    dve.tensor_tensor(halves(tmp[:, 0, 0:T]), acc_of(pair), halves(R[:]), ALU.mult).then_inc(acc_free, 1)
                elif ph.kind == "gateup":
                    n = i * 2 + j // 2
                    dve.tensor_tensor(halves(tmp[:, 2, 0:T]), acc_of(pair), halves(R[:]), ALU.mult).then_inc(acc_free, 1)
                    dve.wait_ge(acc_free, i * 4 + tau1)
                    dve.wait_ge(silu_done, i * 2 + (FC * ph.ff + j // 2 + 1))
                    own.link(dve.tensor_tensor(tmp[:, 2, 0:T], tmp[:, 1, 0:T], tmp[:, 2, 0:T], ALU.mult))
                    own.link(dve.tensor_copy(hid_hi[:, bass.ds(n, 1), :].rearrange("p o t -> p (o t)"), tmp[:, 2, 0:T]))
                    dve.tensor_tensor(hid_lo[:, bass.ds(n, 1), :].rearrange("p o t -> p (o t)"), tmp[:, 2, 0:T],
                                      hid_hi[:, bass.ds(n, 1), :].rearrange("p o t -> p (o t)").bitcast(F32),
                                      ALU.subtract).then_inc(hid_ready, 1)
                elif ph.res is not None:
                    c = 2 * i + t if ph.per_tile == 2 else 4 * i + t
                    dve.scalar_tensor_tensor(halves(x[:, c, :]), acc_of(pair), ph.factor, halves(x[:, c, :]),
                                             ALU.mult, ALU.add).then_inc(acc_free, 1)
                    dve_chunk(dve, c, ph.res, ph.gain)
                elif ph.kind == "q":
                    n = 4 * i + j
                    dve.tensor_tensor(halves(tmp[:, 2, 0:T]), acc_of(pair), halves(R[:]), ALU.mult).then_inc(acc_free, 1)
                    dve.wait_ge(acc_free, tau1 + 4 * i)
                    own.link(dve.tensor_copy(q_hi[:, n, :], tmp[:, 2, 0:T]))
                    dve.tensor_copy(q8f[:, n, :], tmp[:, 2, LP:T])
                    ins = dve.tensor_tensor(q_lo[:, n, :], tmp[:, 2, 0:T], q_hi[:, n, :].bitcast(F32), ALU.subtract)
                    if n < KC - 1:
                        own.link(ins)
                    else:
                        at_dve.done(ins, "q")
                elif ph.kind in ("proj", "projz"):
                    to = {"proj": pm, "projz": gp}[ph.kind]
                    n = i * 4 + (ph.n0 + j)
                    dst = to[:, bass.ds(n, 1), :].rearrange("p o (a b) -> p (o a) b", a=2)
                    dve.tensor_tensor(dst, acc_of(pair), halves(R[:]), ALU.mult).then_inc(acc_free, 1)
                elif ph.kind == "memkv":
                    to = kT if ph.n0 == 0 else vT
                    dve.tensor_copy(to[:, 4 * i + j, :], ACC[:, 2 * pair, 0:NMEM]).then_inc(acc_free, 1)
                elif ph.kind == "conv":
                    s = j % 2
                    n = i * 4 + j
                    dve.tensor_tensor(halves(tmp[:, s, 3:3 + T]), acc_of(pair), halves(R[:]), ALU.mult).then_inc(acc_free, 1)
                    dve.wait_ge(acc_free, i * 4 + tau1)
                    own.link(dve.tensor_copy(xs[:, bass.ds(n, 1), :].rearrange("p o t -> p (o t)"), tmp[:, s, LP:LP + 11]))
                    if not (isinstance(i, int) and i == 0 and j < 2):
                        dve.wait_ge(cv_silu, i * 4 + (j - 1))

                    def w(tap):
                        return convw[:, bass.ds(i * 4 + (tap * 24 + j), 1)]
                    own.link(dve.tensor_scalar(sq[:, s, 0:LP], tmp[:, s, 0:LP], w(0), None, ALU.mult))
                    for tap in (1, 2, 3):
                        ins = dve.scalar_tensor_tensor(sq[:, s, 0:LP], tmp[:, s, tap:tap + LP], w(tap),
                                                       sq[:, s, 0:LP], ALU.mult, ALU.add)
                        if tap < 3:
                            own.link(ins)
                        else:
                            ins.then_inc(cv_acc, 1)
            if ph.kind == "conv":
                for j in range(4):
                    if j == 0:
                        own.link(dve.memset(tmp[:, 0:2, 0:3], 0.0))
                    if j == 0:
                        split_ahead(dve_split, dve, ph, 0, 0, False)
                        dve_norm(dve, own, ph.norm)
                        step_no_split(step, dve, ph, 0, j)
                    else:
                        step(0, j, False)
                with dve_loop(own, dve, 1, its - 1, 16) as i:
                    for j in range(4):
                        step(i, j, False)
                for j in range(4):
                    step(its - 1, j, True)
                return
            looped = ph.kind in ("gateup", "proj", "projz") and its > 1 and not after
            if ph.norm is not None:
                split_ahead(dve_split, dve, ph, 0, 0, its == 1)
                dve_norm(dve, own, ph.norm)
                step_no_split(step, dve, ph, 0, 0)
                for j in range(1, 4):
                    step(0, j, its == 1)
                start = 1
            else:
                start = 0
            if looped and its - 1 > start:
                with dve_loop(own, dve, start, its - 1, links) as i:
                    for j in range(4):
                        step(i, j, False)
            else:
                for i in range(start, its - 1):
                    for j in range(4):
                        step(i, j, False)
            if its - 1 >= start:
                for j in range(4):
                    step(its - 1, j, True)

        skip_split = [False]

        def step_no_split(step, dve, ph, i, j):
            skip_split[0] = True
            step(i, j, False)
            skip_split[0] = False

        def split_ahead(split, eng, ph, i, j, last):
            if skip_split[0]:
                return
            if not last or j < 2:
                split(eng, ph, i, j, 2)
            elif ph.next is not None:
                split_next(split, eng, ph, j)

        @contextmanager
        def dve_loop(own, dve, lo, hi, per):
            own.base, own.k, own.per = own.base + own.k - lo * per, 0, per
            with dve.Fori(lo, hi) as i:
                own.i = i
                yield i
                assert own.k == per, (own.k, per)
            own.base, own.k, own.i = own.base + hi * per, 0, None

        def steps(name, names):
            return Steps(sem(name), [n if isinstance(n, tuple) else (n,) for n in names])

        def zeros40(n):
            return pick[0:40, 0:1].to_broadcast([40, n])
        su_pe = steps("su_pe", ["vec"] + [("x", c) for c in range(KC)])
        su_dve = steps("su_dve", ["vec", "xs"] + [("x", c) for c in range(KC)])
        su_pool = steps("su_pool", ["const"])
        g_split = sem("g_split")
        g_hi = sem("g_hi")
        g_in = sem("g_in")
        XA = [XA0, XA1]
        at_in = sem("at_in")
        c_in = [sem(f"c_in{n}") for n in range(RING)]
        k_out = sem("k_out")
        v_out = sem("v_out")
        at_pe = steps("at_pe", ["memT", "q8"] + [("qb", b) for b in range(NS)] + [("kvN", n) for n in range(4)]
                      + [("s", 0), "sT", ("s", 1)]
                      + [x for h in range(XH) for x in [("t", h)] + (["pT8"] if h == 0 else [])
                         + [("o", h)] + ([("s", h + 2)] if h < XH - 2 else []) + [("pv", 2 * h), ("pv", 2 * h + 1)]] + ["y8"])
        at_act = steps("at_act", ["msq", "memr", "memhi", "khi"] + [("kvN", n) for n in range(4)] + ["vst", ("e", 0), "e8"]
                       + [x for h in range(XH) for x in
                          [("pT", h)] + ([("e", h + 1)] if h < XH - 1 else []) + [("vh", 2 * h), ("yh", h), ("vh", 2 * h + 1)]]
                       + ["y8"])
        at_dve = steps("at_dve", ["ms", "memT", "memlo", "q", "q8"] + [("sc", b) for b in range(NS)]
                       + ["klo", ("vlo", 0), ("vlo", 1), ("nb", 0), "nb8"]
                       + [x for h in range(XH) for x in [("pn", h)] + ([("nb", h + 1)] if h < XH - 1 else [])
                          + (["pn8"] if h == 0 else []) + [("pl", h)] + (["pT8"] if h == 0 else [])
                          + [("vl", 2 * h), ("yl", h), ("vl", 2 * h + 1)]] + ["o8", "yl8"])
        at_pool = steps("at_pool", ["r"])

        def loads_of_setup():
            f = [(xin[:], a["x_prompt"][0].rearrange("(b p) d -> p b d", p=P)), (xin_s[:], a["x_sample"][:, 0, :])]
            for n, v in enumerate(VEC):
                name, l = (v.split(":") + [None])[:2]
                src = a[name] if l is None else a[name][int(l)]
                f.append((vec_in[n * KC:(n + 1) * KC, :], src.rearrange("(c p) -> c p", p=P)))
            f.append((vec_in[96:97, :], a["gd_g_out"]))
            f.append((conv_in[:], a["gd_conv_w"][0].rearrange("j (c p) -> (j c) p", p=P)))
            for n, v in enumerate(["ml_b_i", "ml_b_f", "gd_a_log", "gd_dt_bias"]):
                f.append((small[0:a[v].shape[1], n:n + 1], a[v].rearrange("o h -> h o")))
            return f
        SETUP = loads_of_setup()

        def sp_setup(sp):
            for dst, src in SETUP:
                sp.dma_start(dst, src).then_inc(ins_done, 16)

        def sp_gate(sp, w, c0, n):
            for k, at in ((0, 0), (1, 32)):
                sp.dma_start(gm_raw[:, :, at:at + n],
                             w[:, c0 + k * n:c0 + (k + 1) * n].rearrange("(k p) c -> p k c", p=P)).then_inc(g_in, 16)

        def pe_setup(pe):
            su_pool.wait(pe, "const")
            pe.wait_ge(ins_done, 16 * len(SETUP))
            pe.transpose(M[:, 0, 0:97], vec_in[:], ident[0:97, 0:97])
            pe.transpose(M[:, 0, 128:224], conv_in[:], ident[0:96, 0:96])
            for c in range(KC):
                mm = pe.transpose(M[:, 1, c * NS:(c + 1) * NS], xin_s[:, c * P:(c + 1) * P], ident[0:NS, 0:NS])
            su_pe.done(mm, "vec")
            for c in range(KC):
                if c >= 4:
                    su_dve.wait(pe, "x", c - 4)
                for b in range(TB):
                    mm = pe.transpose(ACC[:, c % 4, b * P:(b + 1) * P], xin[:, b, c * P:(c + 1) * P], ident[:])
                su_pe.done(mm, "x", c)
            su_dve.wait(pe, "x", KC - 1)

        def dve_setup(dve, own):
            own.link(dve.memset(tmp[:], 0.0))
            su_pool.wait(dve, "const")
            dve.tensor_copy(two_r[:], two[:])
            own.link(dve.tensor_copy(ident_r[:], ident[0:40, 0:40]))
            su_pe.wait(dve, "vec")
            own.link(dve.tensor_copy(cols[:], M[:, 0, 0:97]))
            su_dve.done(dve.tensor_copy(convw[:], M[:, 0, 128:224]), "vec")
            su_dve.done(dve.tensor_copy(x[:, :, LP:T], M[:, 1, 0:KC * NS].rearrange("p (c t) -> p c t", t=NS)), "xs")
            for c in range(KC):
                su_pe.wait(dve, "x", c)
                su_dve.done(dve.tensor_copy(x[:, c, 0:LP], ACC[:, c % 4, :]), "x", c)
                dve_chunk(dve, c, 0, "g_ffn1:0")

        def act_setup(act):
            for c in range(KC):
                act_chunk(act, c, 0, "g_ffn1:0", lambda: su_dve.wait(act, "x", c))

        def first_splits_act(act):
            for u in (0, 1):
                act.wait_ge(w_in[u], 16)
                act.activation(w_hi[:, u, 0:KC * P], raw[:, u, 0:KC * P], ACT.Copy).then_inc(w_hi_done, 1)

        def first_splits_dve(dve):
            for u in (0, 1):
                dve.wait_ge(w_hi_done, u + 1)
                dve.tensor_tensor(w_lo[:, u, 0:KC * P], raw[:, u, 0:KC * P], w_hi[:, u, 0:KC * P].bitcast(F32),
                                  ALU.subtract).then_inc(w_split, 1)

        def pool_setup(pool, own):
            own.link(pool.memset(ones[:], 1.0))
            own.link(pool.memset(mhalf[:], -0.5))
            own.link(pool.memset(pick[:], 0.0))
            own.link(pool.memset(pick[:, 39:40], 1.0))
            own.link(pool.memset(gm_raw[:], 0.0))
            own.link(pool.memset(sq[:, 0, 0:P], 0.0))
            own.link(pool.affine_select(out=ident[:], in_=sq[:, 0, 0:P], compare_op=ALU.not_equal, fill=1.0, base=0,
                                        pattern=[[-1, P]], channel_multiplier=1))
            own.link(pool.affine_select(out=causal[:], in_=sq[:, 0, 0:P], compare_op=ALU.is_ge, fill=BIG, base=0,
                                        pattern=[[1, P]], channel_multiplier=-1))
            prev = ident[:]
            for l in range(7):
                B = 2 << l
                cur = sq[:, (l + 1) % 2, 0:P]
                v = cur.rearrange("p (n b) -> p n b", b=B)
                own.link(pool.memset(cur, 1.0))
                own.link(pool.affine_select(out=v, in_=v, compare_op=ALU.is_ge, fill=0.0, base=0,
                                            pattern=[[-B, P // B], [0, B]], channel_multiplier=1))
                own.link(pool.affine_select(out=v, in_=v, compare_op=ALU.is_ge, fill=0.0, base=B - 1,
                                            pattern=[[B, P // B], [0, B]], channel_multiplier=-1))
                ins = pool.tensor_tensor(level[:, l, :], cur, prev, ALU.subtract)
                own.link(ins)
                prev = cur
            su_pool.done(pool.tensor_tensor(two[:], ident[0:40, 0:NS], ident[0:40, 32:40], ALU.add), "const")

        rm = keep[:, 392:394]
        macc = keep[:, 390:392]
        sc = keep[:, 0:64]
        P32 = keep[0:32, 64:320]

        def pool_cache(pool, l, phs):
            for n in range(2 * NS):
                if n < RING:
                    pool.wait_ge(mm_done, phs[1].u0)
                elif n < NS + 2:
                    at_dve.wait(pool, "sc", n - RING, r=l)
                else:
                    at_pe.wait(pool, "pv", n - NS - 2, r=l)
                s = n % RING if n < NS else n % 2
                src = a["cache_mem_k" if n < NS else "cache_mem_v"][l, n % NS].rearrange("(m p) h d -> p m (h d)", p=P)
                pool.dma_start(cache[:, s], src).then_inc(c_in[s], 16)

        def cache_wait(eng, l, n):
            if n < NS:
                s, k = n % RING, n // RING + 1
            else:
                s, k = n % 2, (n - NS) // 2 + 3
            eng.wait_ge(c_in[s], 16 * (l * (6 if s < 2 else 2) + k))

        def sp_mem(sp, l, phs):
            if l >= 0:
                sp.wait_ge(mm_done, phs[0].u0)
            sp.dma_start(memN[:], a["mem_prompt"][0].rearrange("(m p) d -> p m d", p=P)).then_inc(at_in, 16)

        def sp_kv_out(sp, l):
            at_act.wait(sp, "kvN", 1, r=l)
            sp.dma_start(o["mem_k"][l].rearrange("(m p) d -> p m d", p=P), kN[:]).then_inc(k_out, 16)
            at_act.wait(sp, "vst", r=l)
            sp.dma_start(o["mem_v"][l].rearrange("(m p) d -> p m d", p=P), vN[:]).then_inc(v_out, 16)

        def act_mem(act, own, l):
            def squares():
                act.wait_ge(at_in, 16 * (l + 1))
                for m in range(MT):
                    ins = act.activation(memT[:].rearrange("p c m -> p (c m)")[:, m * D:(m + 1) * D], memN[:, m, :],
                                         ACT.Square, accum_out=macc[:, m:m + 1])
                at_act.done(ins, "msq")

            def scaled():
                at_pool.wait(act, "r", r=l)
                for m in range(MT):
                    ins = act.activation(memN[:, m, :], memN[:, m, :], ACT.Copy, scale=rm[:, m:m + 1])
                at_act.done(ins, "memr")

            def high():
                at_dve.wait(act, "memT", r=l)
                for c in range(KC):
                    ins = act.activation(memg_hi[:, c, :], memT[:, c, :], ACT.Copy, scale=gcol(f"g_mem:{l}", c))
                at_act.done(ins, "memhi")
            return {1: squares, 3: scaled, 5: high}

        def dve_mem(dve, own, l):
            def mean():
                at_act.wait(dve, "msq", r=l)
                at_dve.done(dve.tensor_scalar(macc, macc, 1.0 / D, EPS, ALU.mult, ALU.add), "ms")

            def to_sbuf():
                at_pe.wait(dve, "memT", r=l)
                at_dve.done(dve.tensor_copy(memT[:].rearrange("p (b c) m -> p b (c m)", b=4), M[:]), "memT")

            def low():
                at_act.wait(dve, "memhi", r=l)
                for c in range(KC):
                    ins = dve.scalar_tensor_tensor(memg_lo[:, c, :], memT[:, c, :], gcol(f"g_mem:{l}", c),
                                                   memg_hi[:, c, :].bitcast(F32), ALU.mult, ALU.subtract)
                at_dve.done(ins, "memlo")
            return {1: mean, 4: to_sbuf, 6: low}

        def pool_mem(pool, l):
            at_dve.wait(pool, "ms", r=l)
            at_pool.done(pool.tensor_tensor(rm, macc, mhalf[:, 0:MT], ALU.pow), "r")

        def pe_mem(pe, l):
            pe.wait_ge(acc_free, XA[l][0].t0 + 2)
            at_act.wait(pe, "memr", r=l)
            for c in range(KC):
                for m in range(MT):
                    mm = pe.transpose(M[:, c // 2, (c % 2) * NMEM + m * P:(c % 2) * NMEM + (m + 1) * P],
                                      memN[:, m, c * P:(c + 1) * P], ident[:])
            at_pe.done(mm, "memT")

        def pe_kv_natural(pe, l, phs):
            pe.wait_ge(acc_free, phs[2].t0 + KC)
            at_dve.wait(pe, "sc", NS - 1, r=l)
            for n in range(4):
                b0 = 2 * (n % 2)
                if n >= 2:
                    at_act.wait(pe, "kvN", n - 2, r=l)
                if n == 2:
                    at_act.wait(pe, "khi", r=l)
                for c in range(KC):
                    mm = pe.transpose(M[:, b0 + c // 4, (c % 4) * P:(c % 4 + 1) * P],
                                      (kT if n < 2 else vT)[:, c, (n % 2) * P:(n % 2 + 1) * P], ident[:])
                at_pe.done(mm, "kvN", n)

        def act_kv_natural(act, l):
            for n in range(4):
                b0 = 2 * (n % 2)
                at_pe.wait(act, "kvN", n, r=l)
                to = (kN if n < 2 else vN_hi)[:, n % 2, :].rearrange("p (b c) -> p b c", b=2)
                at_act.done(act.activation(to, M[:, b0:b0 + 2, :], ACT.Copy), "kvN", n)
            at_dve.wait(act, "vlo", 1, r=l)
            at_act.done(act.activation(vN[:].rearrange("p m (b c) -> p (m b) c", b=2), M[:], ACT.Copy), "vst")

        def act_k_high(act, l, phs):
            act.wait_ge(acc_free, phs[1].t0 + KC)
            at_act.done(act.activation(kT_hi[:], kT[:], ACT.Copy), "khi")

        def dve_kv_low(dve, l):
            at_act.wait(dve, "khi", r=l)
            at_dve.done(dve.tensor_tensor(kT_lo[:], kT[:], kT_hi[:].bitcast(F32), ALU.subtract), "klo")
            for m in range(MT):
                at_act.wait(dve, "kvN", 2 + m, r=l)
                v = lambda ap: ap[:, m, :].rearrange("p (b c) -> p b c", b=2)
                at_dve.done(dve.tensor_tensor(v(vN_lo), M[:, 2 * m:2 * m + 2, :], v(vN_hi).bitcast(F32), ALU.subtract), "vlo", m)

        SCALE = float(XD) ** -0.5

        def pe_queries(pe, l, phs):
            def by_token():
                at_dve.wait(pe, "q", r=l)
                for c in range(KC):
                    mm = pe.transpose(M[0:NS, c // 4, (c % 4) * P:(c % 4 + 1) * P], q8f[:, c, :], ident[:])
                at_pe.done(mm, "q8")

            def spread(b):
                if b == 0:
                    at_dve.wait(pe, "q8", r=l)
                if b >= 2:
                    at_dve.wait(pe, "sc", b - 2, r=l)
                for d in range(2):
                    mm = pe.matmul(M[:, 2 * ((b + 1) % 2) + d, :], two_r[:, b:b + 1].to_broadcast([40, P]),
                                   q40[:, d * 512:(d + 1) * 512], start=True, stop=True)
                at_pe.done(mm, "qb", b)
            k = {1: by_token, 2: lambda: spread(0), 4: lambda: spread(1), 6: lambda: spread(2)}
            v = {0: lambda: spread(3), 2: lambda: spread(4), 4: lambda: spread(5), 6: lambda: spread(6)}
            return k, v, lambda: spread(7)

        def pe_attn(pe, l, phs):
            def scores(h):
                if h > 0:
                    at_act.wait(pe, "e", h - 1, r=l)
                for b in range(TB):
                    to, t = M[:, b // 2, (b % 2) * NMEM:(b % 2 + 1) * NMEM], slice(b * P, (b + 1) * P)
                    for c in (2 * h, 2 * h + 1):
                        pe.matmul(to, q_hi[:, c, t], kT_hi[:, c, :], start=c == 2 * h, stop=False)
                        pe.matmul(to, q_hi[:, c, t], kT_lo[:, c, :], start=False, stop=False)
                        mm = pe.matmul(to, q_lo[:, c, t], kT_hi[:, c, :], start=False, stop=c == 2 * h + 1)
                at_pe.done(mm, "s", h)

            def values(b):
                at_dve.wait(pe, "vl", b, r=l)
                for d in range(2 if b == 0 else 0):
                    pe.matmul(ACC[0:NS, 2 + d, :], pd_hi[:, 0, 1:9], cache_r[:, 2, 0, 0:512], start=True, stop=False)
                for h in range(XH):
                    to, c = ACC[0:NS, 2 + h // 2, (h % 2) * XD:(h % 2 + 1) * XD], slice(h * XD, (h + 1) * XD)
                    for m in range(MT):
                        p_hi, p_lo = [w[:, m * XH + h, b * NS:(b + 1) * NS] for w in (pd_hi, pd_lo)]
                        pe.matmul(to, p_hi, cache_r[:, 2 + b % 2, m, c], start=False, stop=False)
                        pe.matmul(to, p_lo, cache_r[:, 2 + b % 2, m, c], start=False, stop=False)
                        mm = pe.matmul(to, p_hi, cache_r[:, b % 2, m, c], start=False, stop=b == NS - 1 and m == MT - 1 and h % 2 == 1)
                at_pe.done(mm, "pv", b)
            at_act.wait(pe, "vst", r=l)
            at_dve.wait(pe, "vlo", 1, r=l)
            scores(0)
            for m in range(MT):
                mm = pe.transpose(ACC[0:32, 2, m * P:(m + 1) * P], sc[:, m * 32:(m + 1) * 32], ident[:])
            at_pe.done(mm, "sT")
            scores(1)
            for h in range(XH):
                at_dve.wait(pe, "pn", h, r=l)
                for m in range(MT):
                    for b in range(TB):
                        mm = pe.transpose(ACC[:, m, b * P:(b + 1) * P], pr[:, b, m * P:(m + 1) * P], ident[:])
                at_pe.done(mm, "t", h)
                if h == 0:
                    at_dve.wait(pe, "pn8", r=l)
                    for m in range(MT):
                        mm = pe.transpose(ACC[:, 3, m * 32:(m + 1) * 32], P32[:, m * P:(m + 1) * P], ident[0:32, 0:32])
                    at_pe.done(mm, "pT8")
                at_dve.wait(pe, "pl", h, r=l)
                if h > 0:
                    at_dve.wait(pe, "yl", h - 1, r=l)
                for d in range(2):
                    c = slice((2 * h + d) * P, (2 * h + d + 1) * P)
                    for m in range(MT):
                        pe.matmul(M[:, 2 + d, :], vN_hi[:, m, c], prT_hi[:, m, :], start=m == 0, stop=False)
                        pe.matmul(M[:, 2 + d, :], vN_hi[:, m, c], prT_lo[:, m, :], start=False, stop=False)
                        mm = pe.matmul(M[:, 2 + d, :], vN_lo[:, m, c], prT_hi[:, m, :], start=False, stop=m == MT - 1)
                at_pe.done(mm, "o", h)
                if h < XH - 2:
                    scores(h + 2)
                if h == 0:
                    at_dve.wait(pe, "pT8", r=l)
                values(2 * h)
                values(2 * h + 1)
            at_dve.wait(pe, "o8", r=l)
            for c in range(KC):
                mm = pe.transpose(M[:, 0, c * NS:(c + 1) * NS], o8n[:, c * P:(c + 1) * P], ident[0:NS, 0:NS])
            at_pe.done(mm, "y8")
            at_dve.wait(pe, "yl8", r=l)

        q40 = nc.alloc_sbuf_tensor_at("q40", [40, D], F32R, offset=base_sq)
        pd_hi = nc.alloc_sbuf_tensor_at("pd_hi", [P, MT * XH, NS * NS], F32R, offset=base_sq)
        pd_lo = nc.alloc_sbuf_tensor_at("pd_lo", [P, MT * XH, NS * NS], F32R, offset=base_sq + MT * XH * NS * NS * 4)
        o8n = tmp[:].rearrange("p a t -> p (a t)")[0:NS, 32:32 + D]
        st4 = tmp[:, 0, 0:4]
        nb4 = tmp[:, 0, 4:8]
        den4 = tmp[:, 0, 8:12]
        rd4 = tmp[:, 0, 12:16]
        st8, nb8, den8, rd8 = [tmp[0:32, 0, 16 + n:17 + n] for n in range(4)]

        def act_attn(act, own, l):
            def exps(h):
                at_dve.wait(act, "nb", h, r=l)
                for b in range(TB):
                    ins = act.activation(pr[:, b, :], M[:, b // 2, (b % 2) * NMEM:(b % 2 + 1) * NMEM], ACT.Exp,
                                         bias=nb4[:, b:b + 1], scale=SCALE, accum_out=den4[:, b:b + 1])
                at_act.done(ins, "e", h)

            def value_high(b):
                cache_wait(act, l, NS + b)
                if b >= 2:
                    at_pe.wait(act, "pv", b - 2, r=l)
                at_act.done(act.activation(cache_r[:, 2 + b % 2], cache[:, b % 2], ACT.Copy), "vh", b)
            at_dve.wait(act, "sc", NS - 1, r=l)
            exps(0)
            at_dve.wait(act, "nb8", r=l)
            at_act.done(act.activation(P32, ACC[0:32, 2, 0:NMEM], ACT.Exp, bias=nb8, scale=SCALE, accum_out=den8), "e8")
            for h in range(XH):
                at_pe.wait(act, "t", h, r=l)
                if h > 0:
                    at_pe.wait(act, "o", h - 1, r=l)
                else:
                    act.wait_ge(k_out, 16 * (l + 1))
                at_act.done(act.activation(prT_hi[:], ACC[:, 0:2, :], ACT.Copy), "pT", h)
                if h < XH - 1:
                    exps(h + 1)
                value_high(2 * h)
                at_pe.wait(act, "o", h, r=l)
                at_act.done(act.activation(ay_hi[:, 2 * h:2 * h + 2, 0:LP], M[:, 2:4, :], ACT.Copy), "yh", h)
                value_high(2 * h + 1)
            at_pe.wait(act, "y8", r=l)
            at_act.done(act.activation(ay_hi[:, :, LP:T], M[:, 0, 0:KC * NS].rearrange("p (c b) -> p c b", b=NS), ACT.Copy), "y8")

        def dve_scores(dve, own, l):
            def by_token():
                at_pe.wait(dve, "q8", r=l)
                v = lambda ap: ap.rearrange("p (a b) -> p a b", a=2)
                own.link(dve.tensor_copy(q40[:], zeros40(D)))
                own.link(dve.tensor_copy(v(q40[0:NS]), M[0:NS, 0:2, :]))
                at_dve.done(dve.tensor_tensor(v(q40[32:40]), M[0:NS, 0:2, :], v(q40[0:NS].bitcast(F32)), ALU.subtract), "q8")

            def sample_scores(b):
                at_pe.wait(dve, "qb", b, r=l)
                cache_wait(dve, l, b)
                for m in range(MT):
                    for h in range(XH):
                        kc = cache[:, b % RING, m, h * XD:(h + 1) * XD]
                        at = m * 32 + b * XH + h
                        ins = dve.tensor_tensor_reduce(kc, kc, M[:, 2 * ((b + 1) % 2) + h // 2, (h % 2) * XD:(h % 2 + 1) * XD],
                                                       1.0, 0.0, ALU.mult, ALU.add, sc[:, at:at + 1])
                at_dve.done(ins, "sc", b)
            do = [lambda b=b: sample_scores(b) for b in range(NS)]
            return {0: by_token, 1: do[0], 3: do[1], 5: do[2], 7: do[3]}, {1: do[4], 3: do[5], 5: do[6]}, do[7]

        def dve_attn(dve, own, l):
            def lo(h):
                at_act.wait(dve, "yh", h, r=l)
                at_dve.done(dve.tensor_tensor(ay_lo[:, 2 * h:2 * h + 2, 0:LP], M[:, 2:4, :],
                                              ay_hi[:, 2 * h:2 * h + 2, 0:LP].bitcast(F32), ALU.subtract), "yl", h)

            def bound(h):
                at_pe.wait(dve, "s", h, r=l)
                own.link(dve.tensor_reduce(st4, M[:, 0:2, :].rearrange("p a (b m) -> p (a b) m", b=2), AX.X, ALU.max))
                at_dve.done(dve.tensor_scalar(nb4, st4, -SCALE, None, ALU.mult), "nb", h)


            def value_low(b):
                at_act.wait(dve, "vh", b, r=l)
                at_dve.done(dve.tensor_tensor(cache_r[:, b % 2], cache[:, b % 2], cache_r[:, 2 + b % 2].bitcast(F32),
                                              ALU.subtract), "vl", b)
            bound(0)
            at_pe.wait(dve, "sT", r=l)
            own.link(dve.tensor_reduce(st8, ACC[0:32, 2, 0:NMEM], AX.X, ALU.max))
            at_dve.done(dve.tensor_scalar(nb8, st8, -SCALE, None, ALU.mult), "nb8")
            for h in range(XH):
                at_act.wait(dve, "e", h, r=l)
                own.link(dve.reciprocal(rd4, den4))
                at_dve.done(dve.tensor_tensor(pr[:], pr[:], rd4.unsqueeze(2).to_broadcast([P, TB, NMEM]), ALU.mult), "pn", h)
                if h < XH - 1:
                    bound(h + 1)
                if h == 0:
                    at_act.wait(dve, "e8", r=l)
                    own.link(dve.reciprocal(rd8, den8))
                    at_dve.done(dve.tensor_scalar(P32, P32, rd8, None, ALU.mult), "pn8")
                at_act.wait(dve, "pT", h, r=l)
                at_dve.done(dve.tensor_tensor(prT_lo[:], ACC[:, 0:2, :], prT_hi[:].bitcast(F32), ALU.subtract), "pl", h)
                if h == 0:
                    at_pe.wait(dve, "pT8", r=l)
                    own.link(dve.tensor_copy(pd_hi[:].rearrange("p a b -> p (a b)"), pick[:, 0:1].to_broadcast([P, 512])))
                    own.link(dve.tensor_copy(pd_lo[:].rearrange("p a b -> p (a b)"), pick[:, 0:1].to_broadcast([P, 512])))
                    for m in range(MT):
                        src = ACC[:, 3, m * 32:(m + 1) * 32].rearrange("p (b h) -> p h b", h=XH)
                        hi, low = [w[:, m * XH:(m + 1) * XH, 0:64:9] for w in (pd_hi, pd_lo)]
                        own.link(dve.tensor_copy(hi, src))
                        ins = dve.tensor_tensor(low, src, hi.bitcast(F32), ALU.subtract)
                    at_dve.done(ins, "pT8")
                value_low(2 * h)
                lo(h)
                value_low(2 * h + 1)
            at_pe.wait(dve, "pv", NS - 1, r=l)
            at_dve.done(dve.tensor_copy(o8n.rearrange("p (a b) -> p a b", a=2), ACC[0:NS, 2:4, :]), "o8")
            at_act.wait(dve, "y8", r=l)
            at_dve.done(dve.tensor_tensor(ay_lo[:, :, LP:T], M[:, 0, 0:KC * NS].rearrange("p (c b) -> p c b", b=NS),
                                          ay_hi[:, :, LP:T].bitcast(F32), ALU.subtract), "yl8")

        ml_pe = steps("ml_pe", [("vT", 0), ("vT", 1), "gates", ("vT", 2), ("vT", 3), "n0", "small"] + [("kT", b) for b in range(TB)]
                      + ["st", ("Mb", 0), ("S", 0)]
                      + [x for h in range(MLH) for x in [("num", h)] + ([("Mb", h + 1), ("S", h + 1)] if h < MLH - 1 else [])
                         + [("nsq", h)]]
                      + ["kv8", "n8", ("out", 0)]
                      + [x for h in range(MLH) for x in ([("out", h + 1)] if h < MLH - 1 else []) + [("hs", h)]] + ["nsq8"]
                      + [("rb", h) for h in range(MLH)])
        ml_act = steps("ml_act", ["ksc"] + [("vN", b) for b in range(TB)] + ["lnf", "rse", "ex", "stc"]
                       + [x for h in range(MLH) for x in [("W", h), ("sqn", h)]] + ["sig", "r8"] + [("yh", h) for h in range(MLH)])
        ml_dve = steps("ml_dve", ["graw", "rows", "sb"] + [("kw", b) for b in range(TB)]
                       + [x for h in range(MLH) for x in [("dg", h), ("PT", h), ("tok", h)]]
                       + ["ms", "kv8", ("Vd", 0), "n", "n8"]
                       + [x for h in range(MLH) for x in [("C", h)] + ([("Vd", h + 1)] if h < MLH - 1 else [])]
                       + ["sq8", "ms8", "y8"] + [("n", 0)]
                       + [x for h in range(MLH) for x in ([("n", h + 1)] if h < MLH - 1 else []) + [("y", h)]])
        ml_pool = steps("ml_pool", ["rt"])
        ml_oz = sem("ml_oz")
        ml_ld = sem("ml_ld")
        ml_cin = [sem(f"ml_cin{n}") for n in range(2)]
        ml_cout = [sem(f"ml_cout{n}") for n in range(2)]
        ml_out = sem("ml_out")
        g_raw_free = sem("g_raw_free")

        class MLstm:
            uT = keep[:, 0:16]
            emT = keep[:, 16:32]
            wkT = keep[0:NS, 32:36]
            wS = keep[:, 36:52]
            SB = keep[:, 64:164].rearrange("p (h x) -> p h x", h=MLH)
            n0T = keep[:, 170:202].rearrange("p (b h) -> p h b", h=MLH)
            dk = keep[:, 204:220]
            nk = keep[:, 220:236]
            rt = keep[:, 236:252]
            n0 = keep[0:32, 256:384]
            m0T = small[0:MLH, 4:12]
            off = [0, 512, 896, 1152]
            Sbank = [(0, 0), (1, 0), (2, 0), (2, 256)]
            g4 = slice(0, MLH)

            def loads(self):
                return [(self.n0, a["state_mlstm_n"][0].rearrange("b h d -> (b h) d")),
                        (self.m0T, a["state_mlstm_m"][0].rearrange("b h -> h b"))]

            def sp_early(self, sp):
                for dst, src in self.loads():
                    sp.dma_start(dst, src, allow_slow_non_contiguous=True).then_inc(ml_ld, 16)
                su_pool.wait(sp, "const")
                sp_gate(sp, a["ml_w_in"][0], 3072, MLH)

            def c_load(self, sp, h):
                sp.dma_start(ml_C[:, h % 2], a["state_mlstm_C"][0, :, h].rearrange("b p e -> p b e")).then_inc(ml_cin[h % 2], 16)

            def sp(self, sp):
                ml_act.wait(sp, "stc")
                sp.dma_start(o["p_C"].rearrange("h p e -> p h e"), ml_Cst[:]).then_inc(ml_out, 16)
                sp.dma_start(o["p_n"], ml_mrow[:]).then_inc(ml_out, 16)
                sp.dma_start(o["p_m"], rw[1][self.g4, LP - 1:LP]).then_inc(ml_out, 16)
                sp.dma_start(o["s_m"].rearrange("b h -> h b"), rw[3][self.g4, 0:NS],
                             allow_slow_non_contiguous=True).then_inc(ml_out, 16)
                ml_pe.wait(sp, "num", MLH - 1)
                self.c_load(sp, 0)
                self.c_load(sp, 1)
                ml_dve.wait(sp, "n8")
                sp.dma_start(o["s_n"], ml_n0[:]).then_inc(ml_out, 16)
                for h in range(MLH):
                    ml_dve.wait(sp, "C", h)
                    sp.dma_start(o["s_C"][:, h].rearrange("b p e -> p b e"), ml_C[:, h % 2]).then_inc(ml_cout[h % 2], 16)
                    if h + 2 < MLH:
                        ml_pe.wait(sp, "hs", h)
                        sp.wait_ge(ml_cout[h % 2], 16 * (h // 2 + 1))
                        self.c_load(sp, h + 2)

            def sp_end(self, sp):
                sp.wait_ge(ml_out, 16 * 5)
                for q in ml_cout:
                    sp.wait_ge(q, 16 * MLH // 2)

            def pe(self, pe):
                pe.wait_ge(acc_free, ML_IN.t0 + ML_IN.units)
                for b in range(TB):
                    if b >= 2:
                        ml_act.wait(pe, "vN", b - 2)
                    for c in range(KC):
                        mm = pe.transpose(ACC[:, 2 * (b % 2) + c // 4, (c % 4) * P:(c % 4 + 1) * P],
                                          pm[:, 8 + c, b * P:(b + 1) * P], ident[:])
                    ml_pe.done(mm, "vT", b)
                    if b == 1:
                        ml_pe.done(pe_gates(pe, 0), "gates")
                pe.wait_ge(ml_ld, 32)
                ml_pe.done(pe.transpose(M[:, 0, 0:32], self.n0, ident[0:32, 0:32]), "n0")
                ml_act.wait(pe, "rse")
                for b in range(TB):
                    pe.transpose(M[:, 1, b * MLH:(b + 1) * MLH], rw[6][self.g4, b * P:(b + 1) * P], ident[self.g4, self.g4])
                    pe.transpose(M[:, 1, 16 + b * MLH:16 + (b + 1) * MLH], rw[1][self.g4, b * P:(b + 1) * P],
                                 ident[self.g4, self.g4])
                pe.transpose(M[0:NS, 1, 32:36], ml_rse[:, 8:16], ident[self.g4, self.g4])
                for h in range(MLH):
                    mm = pe.matmul(M[:, 1, 64 + 25 * h:89 + 25 * h], ident[self.g4, h:h + 1].to_broadcast([MLH, P]),
                                   ml_rse[:, 0:25], start=True, stop=True)
                ml_pe.done(mm, "small")
                ml_act.wait(pe, "vN", TB - 1)
                ml_act.wait(pe, "ksc")
                for b in range(TB):
                    for h in range(MLH):
                        mm = pe.transpose(ACC[:, b, h * P:(h + 1) * P], pm[:, MLH + h, b * P:(b + 1) * P], ident[:])
                    ml_pe.done(mm, "kT", b)
                ml_dve.wait(pe, "kw", TB - 1)
                for h in range(MLH):
                    for b in range(TB):
                        pe.matmul(M[:, 2 + h // 2, (h % 2) * 256:(h % 2 + 1) * 256], ml_kw[:, b, h * P:(h + 1) * P],
                                  ml_vN[:, b, h * 256:(h + 1) * 256], start=b == 0, stop=b == TB - 1)
                for b in range(TB):
                    mm = pe.matmul(M[0:1, 0, :], ones[:, 0:1], ml_kw[:, b, :], start=b == 0, stop=b == TB - 1)
                ml_pe.done(mm, "st")

                def scores(h):
                    if h > 0:
                        ml_act.wait(pe, "W", h - 1)
                    ml_pe.done(pe.matmul(M[:, 1, :], ident[self.g4, h:h + 1].to_broadcast([MLH, P]), rw[7][self.g4, 0:LP],
                                         start=True, stop=True), "Mb", h)
                    if h > 0:
                        ml_dve.wait(pe, "PT", h - 1)
                    for s in range(TB):
                        bank, at = self.Sbank[s]
                        mm = pe.matmul(ACC[:, bank, at:at + LP - s * P], pm[:, MLH + h, s * P:(s + 1) * P],
                                       pm[:, h, s * P:LP], start=True, stop=True)
                    ml_pe.done(mm, "S", h)
                scores(0)
                ml_act.wait(pe, "stc")
                for h in range(MLH):
                    ml_dve.wait(pe, "PT", h)
                    if h > 0:
                        ml_act.wait(pe, "sqn", h - 1)
                        ml_dve.wait(pe, "tok", h - 1)
                    for e in range(2):
                        for s in range(TB):
                            pe.matmul(M[:, 2 + e, s * P:LP], ml_vN[:, s, h * 256 + e * P:h * 256 + (e + 1) * P],
                                      ml_PT[:, self.off[s]:self.off[s] + LP - s * P], start=s == 0, stop=s == TB - 1)
                    for b in range(TB):
                        for s in range(b + 1):
                            at = self.off[s] + (b - s) * P
                            mm = pe.matmul(M[:, 0, b:b + 1], ml_PT[:, at:at + P], ones[:, 0:1], start=s == 0, stop=s == b)
                    ml_pe.done(mm, "num", h)
                    if h < MLH - 1:
                        scores(h + 1)
                    ml_act.wait(pe, "sqn", h)
                    for b in range(TB):
                        for e in range(2):
                            mm = pe.matmul(M[:, 0, 4 + b:5 + b], ml_sq[:, e, b * P:(b + 1) * P], ones[:, 0:1],
                                           start=e == 0, stop=e == 1)
                    ml_pe.done(mm, "nsq", h)
                ml_dve.wait(pe, "ms")
                for h in range(MLH):
                    pe.transpose(M[0:NS, 1, h * P:(h + 1) * P], pm[:, MLH + h, LP:T], ident[:])
                for c in range(KC):
                    mm = pe.transpose(ACC[0:NS, c // 4, (c % 4) * P:(c % 4 + 1) * P], pm[:, 8 + c, LP:T], ident[:])
                ml_pe.done(mm, "kv8")
                ml_dve.wait(pe, "n")
                pe.matmul(M[:, 3, 0:32], ones[:], ml_t8[:, 3, 0:32], start=True, stop=True)
                ml_pe.done(pe.transpose(M[0:32, 0, 0:P], ml_t8[:, 4, 0:32], ident[:]), "n8")

                def outer(h):
                    ml_dve.wait(pe, "Vd", h)
                    for q in range(4):
                        for part in range(2):
                            mm = pe.matmul(ACC[:, q, :], ml_k40[:, part, h * P:(h + 1) * P],
                                           ml_Vd[:, 2 * q:2 * q + 2, :].rearrange("k b e -> k (b e)"),
                                           start=part == 0, stop=part == 1)
                    ml_pe.done(mm, "out", h)
                outer(0)
                for h in range(MLH):
                    ml_dve.wait(pe, "C", h)
                    if h < MLH - 1:
                        outer(h + 1)
                    for e in range(2):
                        for b in range(NS):
                            at = (h * 2 + e) * NS + b
                            mm = pe.matmul(M[:, 2, at:at + 1], ml_C[:, h % 2, b, e * P:(e + 1) * P], pm[:, h, LP + b:LP + b + 1],
                                           start=True, stop=True)
                    ml_pe.done(mm, "hs", h)
                ml_dve.wait(pe, "sq8")
                ml_pe.done(pe.matmul(M[:, 3, 64:128], ones[:], ml_t8[:, 8, :], start=True, stop=True), "nsq8")
                ml_pool.wait(pe, "rt")
                for h in range(MLH):
                    for b in range(TB):
                        mm = pe.matmul(ACC[:, h, b * P:(b + 1) * P],
                                       self.rt[:, b * MLH + h:b * MLH + h + 1].to_broadcast([P, P]), ident[:], start=True, stop=True)
                    ml_pe.done(mm, "rb", h)
                ml_dve.wait(pe, "y", MLH - 1)

            def act(self, act, own):
                act_gates(act, gm_hi, 0)
                act.wait_ge(acc_free, ML_IN.t0 + 8)
                ml_act.done(act.activation(pm[:, 4:8, :], pm[:, 4:8, :], ACT.Copy, scale=float(P) ** -0.5), "ksc")
                act.wait_ge(g_split, 1)
                for b in range(TB):
                    ml_pe.wait(act, "vT", b)
                    if b == 0:
                        ml_pe.wait(act, "gates")
                    ml_act.done(act.activation(ml_vN[:, b].rearrange("p (a c) -> p a c", a=2),
                                               ACC[:, 2 * (b % 2):2 * (b % 2) + 2, :], ACT.Copy), "vN", b)
                ml_dve.wait(act, "graw")
                g = self.g4
                own.link(act.activation(rw[2][g], rw[0][g], ACT.Identity, bias=small[g, 0:1]))
                own.link(act.activation(rw[3][g], rw[1][g], ACT.Abs, bias=small[g, 1:2]))
                own.link(act.activation(rw[3][g], rw[3][g], ACT.Exp, scale=-1.0))
                ml_act.done(act.activation(rw[3][g], rw[3][g], ACT.Ln, bias=ones[g, 0:1]), "lnf")
                ml_dve.wait(act, "rows")
                ml_act.done(act.activation(ml_rse[:, 0:24], ml_rs[:, 0:24], ACT.Exp), "rse")
                ml_dve.wait(act, "sb")
                act.activation(self.wS, self.wS, ACT.Exp)
                ml_act.done(act.activation(self.emT, self.emT, ACT.Exp, scale=-1.0), "ex")
                ml_pe.wait(act, "st")
                act.activation(ml_Cst[:].rearrange("p (a h) e -> p a (h e)", a=2), M[:, 2:4, :], ACT.Copy)
                ml_act.done(act.activation(ml_mrow[:], M[0:1, 0, :], ACT.Copy), "stc")
                for h in range(MLH):
                    ml_dve.wait(act, "dg", h)
                    if h > 0:
                        ml_dve.wait(act, "PT", h - 1)
                    for s in range(TB):
                        at = self.off[s]
                        u = self.uT[:, s * MLH + h:s * MLH + h + 1]
                        ins = act.activation(ml_W[:, at:at + P], ml_Dg[:, s, :], ACT.Exp, scale=-1.0, bias=u)
                        if s < TB - 1:
                            act.activation(ml_W[:, at + P:at + LP - s * P], M[:, 1, (s + 1) * P:LP], ACT.Exp, scale=-1.0, bias=u)
                    ml_act.done(ins, "W", h)
                    ml_pe.wait(act, "num", h)
                    if h > 0:
                        ml_pe.wait(act, "nsq", h - 1)
                    act.activation(ml_sq[:], M[:, 2:4, :], ACT.Square)
                    ml_act.done(act.activation(pm[:, 8 + 2 * h:10 + 2 * h, 0:LP], M[:, 2:4, :], ACT.Copy), "sqn", h)
                own.link(act.activation(pm[:, 16:24, :], pm[:, 16:24, :], ACT.Sigmoid))
                for c in range(KC):
                    ins = act.activation(pm[:, 16 + c, :], pm[:, 16 + c, :], ACT.Copy, scale=gcol("ml_g_head:0", c))
                ml_act.done(ins, "sig")
                ml_dve.wait(act, "ms8")
                ml_act.done(act.activation(ml_t8[:, 11, 0:32], ml_t8[:, 10, 0:32], ACT.Sqrt), "r8")
                for h in range(MLH):
                    ml_dve.wait(act, "n", h)
                    ml_act.done(act.activation(ml_y_hi[:, 2 * h:2 * h + 2, 0:LP], pm[:, 16 + 2 * h:18 + 2 * h, 0:LP], ACT.Copy),
                                "yh", h)
                act.wait_ge(ml_out, 16 * 5)

            def dve(self, dve, own):
                g = self.g4
                dve_gates(dve, gm_hi, gm_lo, 0)
                ml_pe.wait(dve, "gates")
                v2 = lambda ap: ap.rearrange("p (a b) -> p a b", a=2)
                dve.tensor_tensor(v2(rw[0][g]), M[g, 2:4, 0:TH], halves(R[g]), ALU.mult)
                ml_dve.done(dve.tensor_tensor(v2(rw[1][g]), M[32:36, 2:4, 0:TH], halves(R[32:36]), ALU.mult), "graw")
                ml_act.wait(dve, "lnf")
                own.link(dve.tensor_scalar(rw[4][g], rw[1][g], small[g, 1:2], 0.0, ALU.add, ALU.min))
                own.link(dve.tensor_tensor(rw[4][g], rw[4][g], rw[3][g], ALU.subtract))
                own.link(dve.tensor_tensor_scan(rw[5][g, 0:LP], ones[g, 0:1].to_broadcast([MLH, LP]), rw[4][g, 0:LP], 0.0,
                                                ALU.mult, ALU.add))
                own.link(dve.tensor_tensor(rw[6][g, 0:LP], rw[2][g, 0:LP], rw[5][g, 0:LP], ALU.subtract))
                own.link(dve.tensor_tensor_scan(rw[7][g, 0:LP], rw[6][g, 0:LP], rw[6][g, 0:LP], 0.0, ALU.max, ALU.max))
                own.link(dve.tensor_tensor(rw[1][g, 0:LP], rw[5][g, 0:LP], rw[7][g, 0:LP], ALU.add))
                own.link(dve.tensor_copy(ml_rse[:, 24:25], rw[7][g, LP - 1:LP]))
                dve.wait_ge(ml_ld, 32)
                m, am = rw[3][g, 0:NS], rw[3][g, NS:2 * NS]
                own.link(dve.tensor_tensor(am, rw[4][g, LP:T], self.m0T, ALU.add))
                own.link(dve.tensor_tensor(m, am, rw[2][g, LP:T], ALU.max))
                dve.tensor_tensor(ml_rs[:, 0:8], am, m, ALU.subtract)
                dve.tensor_tensor(ml_rs[:, 8:16], rw[2][g, LP:T], m, ALU.subtract)
                ml_dve.done(dve.tensor_scalar(ml_rs[:, 16:24], m, -1.0, None, ALU.mult), "rows")
                ml_pe.wait(dve, "small")
                own.link(dve.tensor_copy(keep[:, 0:32], M[:, 1, 0:32]))
                own.link(dve.tensor_copy(keep[0:NS, 32:36], M[0:NS, 1, 32:36]))
                own.link(dve.tensor_copy(keep[:, 64:164], M[:, 1, 64:164]))
                own.link(dve.tensor_copy(keep[:, 170:202], M[:, 0, 0:32]))
                ml_dve.done(dve.tensor_tensor(self.wS.rearrange("p (b h) -> p b h", h=MLH),
                                              self.uT.rearrange("p (b h) -> p b h", h=MLH),
                                              self.SB[:, :, 24].unsqueeze(1).to_broadcast([P, TB, MLH]), ALU.subtract), "sb")
                ml_act.wait(dve, "ex")
                for b in range(TB):
                    ml_pe.wait(dve, "kT", b)
                    ml_dve.done(dve.tensor_tensor(ml_kw[:, b].rearrange("p (h d) -> p h d", h=MLH),
                                                  ACC[:, b].rearrange("p (h d) -> p h d", h=MLH),
                                                  self.wS[:, b * MLH:(b + 1) * MLH].unsqueeze(2).to_broadcast([P, MLH, P]),
                                                  ALU.mult), "kw", b)
                for h in range(MLH):
                    ml_pe.wait(dve, "Mb", h)
                    if h > 0:
                        ml_act.wait(dve, "W", h - 1)
                    ml_dve.done(dve.tensor_tensor(ml_Dg[:], M[:, 1].rearrange("p (b t) -> p b t", b=TB),
                                                  causal[:].unsqueeze(1).to_broadcast([P, TB, P]), ALU.add), "dg", h)
                    ml_act.wait(dve, "W", h)
                    ml_pe.wait(dve, "S", h)
                    dve.tensor_tensor(ml_PT[:, 0:512], ml_W[:, 0:512], ACC[:, 0, :], ALU.mult)
                    dve.tensor_tensor(ml_PT[:, 512:896], ml_W[:, 512:896], ACC[:, 1, 0:384], ALU.mult)
                    ml_dve.done(dve.tensor_tensor(ml_PT[:, 896:1280], ml_W[:, 896:1280], ACC[:, 2, 0:384], ALU.mult), "PT", h)
                    ml_pe.wait(dve, "nsq", h)
                    own.link(dve.tensor_copy(self.dk.rearrange("p (b h) -> p b h", h=MLH)[:, :, h], M[:, 0, 0:4]))
                    ml_dve.done(dve.tensor_copy(self.nk.rearrange("p (b h) -> p b h", h=MLH)[:, :, h], M[:, 0, 4:8]), "tok", h)
                ml_dve.wait(dve, "tok", MLH - 1)
                own.link(dve.tensor_tensor(self.dk, self.dk, self.dk, ALU.mult))
                own.link(dve.tensor_tensor(self.emT, self.emT, self.emT, ALU.mult))
                own.link(dve.tensor_tensor(self.dk, self.dk, self.emT, ALU.max))
                own.link(dve.tensor_scalar(self.dk, self.dk, EPS, None, ALU.mult))
                ml_dve.done(dve.scalar_tensor_tensor(self.nk, self.nk, 1.0 / 256, self.dk, ALU.mult, ALU.add), "ms")
                ml_pe.wait(dve, "kv8")
                w2 = lambda ap: ap.rearrange("p (a b) -> p a b", a=2)
                own.link(dve.tensor_tensor(ml_k8[:].rearrange("p (h d) -> p h d", h=MLH),
                                           M[0:NS, 1, :].rearrange("p (h d) -> p h d", h=MLH),
                                           self.wkT.unsqueeze(2).to_broadcast([NS, MLH, P]), ALU.mult))
                own.link(dve.tensor_copy(ml_k40[:].rearrange("p a b -> p (a b)"), zeros40(D)))
                own.link(dve.tensor_copy(ml_k40[0:NS, 0], ml_k8[:]))
                own.link(dve.tensor_copy(ml_k40[32:40, 0], ml_k8[:]))
                own.link(dve.tensor_tensor(ml_k40[0:NS, 1], ml_k8[:], ml_k40[0:NS, 0].bitcast(F32), ALU.subtract))
                own.link(dve.tensor_copy(ml_v40[:], zeros40(D)))
                own.link(dve.tensor_copy(w2(ml_v40[0:NS]), ACC[0:NS, 0:2, :]))
                ml_dve.done(dve.tensor_tensor(w2(ml_v40[32:40]), ACC[0:NS, 0:2, :], w2(ml_v40[0:NS].bitcast(F32)), ALU.subtract),
                            "kv8")

                def diagonal(h):
                    if h == 0:
                        ml_dve.wait(dve, "kv8")
                    v = ml_v40[:, h * 256:(h + 1) * 256].bitcast(F32)
                    ml_dve.done(dve.tensor_tensor(ml_Vd[:], v.unsqueeze(1).to_broadcast([40, NS, 256]),
                                                  two[:].unsqueeze(2).to_broadcast([40, NS, 256]), ALU.mult), "Vd", h)
                diagonal(0)
                t8 = lambda n: ml_t8[:, n, 0:32].rearrange("p (h b) -> p h b", h=MLH)
                wi, wk, em = self.SB[:, :, 0:8], self.SB[:, :, 8:16], self.SB[:, :, 16:24]
                own.link(dve.tensor_tensor(t8(0), self.n0T, wi, ALU.mult))
                own.link(dve.tensor_tensor(t8(1), pm[:, 4:8, LP:T], wk, ALU.mult))
                own.link(dve.tensor_tensor(t8(2), t8(0), t8(1), ALU.add))
                own.link(dve.tensor_tensor(t8(3), pm[:, 0:4, LP:T], t8(2), ALU.mult))
                ml_dve.done(dve.tensor_copy(ml_t8[:, 4, 0:32].rearrange("p (b h) -> p h b", h=MLH), t8(2)), "n")
                ml_pe.wait(dve, "n8")
                own.link(dve.tensor_tensor(t8(0), em, em, ALU.mult))
                own.link(dve.tensor_copy(ml_t8[:, 1, 0:32], M[:, 3, 0:32]))
                own.link(dve.tensor_tensor(t8(1), t8(1), t8(1), ALU.mult))
                own.link(dve.tensor_tensor(t8(5), t8(1), t8(0), ALU.max))
                own.link(dve.tensor_scalar(t8(5), t8(5), EPS, None, ALU.mult))
                ml_dve.done(dve.tensor_copy(ml_n0[:], M[0:32, 0, 0:P]), "n8")
                for h in range(MLH):
                    ml_pe.wait(dve, "out", h)
                    dve.wait_ge(ml_cin[h % 2], 16 * (h // 2 + 1))
                    for b in range(NS):
                        ins = dve.scalar_tensor_tensor(ml_C[:, h % 2, b, :], ml_C[:, h % 2, b, :], self.SB[:, h, b:b + 1],
                                                       ACC[:, b // 2, (b % 2) * 256:(b % 2 + 1) * 256], ALU.mult, ALU.add)
                    ml_dve.done(ins, "C", h)
                    if h < MLH - 1:
                        diagonal(h + 1)
                ml_pe.wait(dve, "hs", MLH - 1)
                own.link(dve.tensor_copy(ml_t8[:, 7, :], M[:, 2, 0:64]))
                ml_dve.done(dve.tensor_tensor(ml_t8[:, 8, :], ml_t8[:, 7, :], ml_t8[:, 7, :], ALU.mult), "sq8")
                ml_pe.wait(dve, "nsq8")
                own.link(dve.tensor_copy(ml_t8[:, 9, :], M[:, 3, 64:128]))
                s4 = ml_t8[:, 9, :].rearrange("p (h e b) -> p h e b", h=MLH, e=2)
                own.link(dve.tensor_tensor(t8(10), s4[:, :, 0, :], s4[:, :, 1, :], ALU.add))
                ml_dve.done(dve.scalar_tensor_tensor(t8(10), t8(10), 1.0 / 256, t8(5), ALU.mult, ALU.add), "ms8")
                ml_act.wait(dve, "r8")
                own.link(dve.reciprocal(t8(11), t8(11)))
                num = ml_t8[:, 7, :].rearrange("p (h e b) -> p h e b", h=MLH, e=2)
                own.link(dve.tensor_tensor(ml_t8[:, 0, :].rearrange("p (h e b) -> p h e b", h=MLH, e=2), num,
                                           t8(11).unsqueeze(2).to_broadcast([P, MLH, 2, NS]), ALU.mult))
                ml_act.wait(dve, "sig")
                y8 = ml_t8[:, 0, :].rearrange("p (c b) -> p c b", b=NS)
                own.link(dve.tensor_tensor(y8, y8, pm[:, 16:24, LP:T], ALU.mult))
                for q in ml_cout:
                    dve.wait_ge(q, 16 * MLH // 2)
                ml_pe.wait(dve, "nsq8")
                own.link(dve.tensor_copy(ml_y_hi[:, :, LP:T], y8))
                ml_dve.done(dve.tensor_tensor(ml_y_lo[:, :, LP:T], y8, ml_y_hi[:, :, LP:T].bitcast(F32), ALU.subtract), "y8")

                def normed(h):
                    ml_pe.wait(dve, "rb", h)
                    dve.wait_ge(ml_oz, h + 1)
                    n = pm[:, 16 + 2 * h:18 + 2 * h, 0:LP]
                    ml_dve.done(dve.tensor_tensor(n, n, ACC[:, h, :].unsqueeze(1).to_broadcast([P, 2, LP]), ALU.mult), "n", h)
                normed(0)
                for h in range(MLH):
                    if h < MLH - 1:
                        normed(h + 1)
                    c = slice(2 * h, 2 * h + 2)
                    ml_act.wait(dve, "yh", h)
                    ml_dve.done(dve.tensor_tensor(ml_y_lo[:, c, 0:LP], pm[:, 16 + 2 * h:18 + 2 * h, 0:LP],
                                                  ml_y_hi[:, c, 0:LP].bitcast(F32), ALU.subtract), "y", h)
                dve.wait_ge(ml_out, 16 * 5)

            def pool(self, pool, own):
                ml_dve.wait(pool, "ms")
                ml_pool.done(pool.tensor_tensor(self.rt, self.nk, mhalf[:, 0:16], ALU.pow), "rt")
                ml_act.wait(pool, "sig")
                for h in range(MLH):
                    n, z = [pm[:, c + 2 * h:c + 2 + 2 * h, 0:LP] for c in (8, 16)]
                    pool.tensor_tensor(z, n, z, ALU.mult).then_inc(ml_oz, 1)

        def pe_gates(pe, n):
            pe.wait_ge(g_split, n + 1)
            hi, lo = (gm_hi, gm_lo) if n == 0 else (gg_hi, gg_lo)
            for k in range(KC):
                for h in range(2):
                    out, m = M[:, 2 + h, 0:TH], slice(h * TH, h * TH + TH)
                    pe.matmul(out, hi[:, k, :], xg_hi[:, k, m], start=k == 0, stop=False)
                    pe.matmul(out, hi[:, k, :], xg_lo[:, k, m], start=False, stop=False)
                    mm = pe.matmul(out, lo[:, k, :], xg_hi[:, k, m], start=False, stop=k == KC - 1)
            return mm

        def act_gates(act, hi, n):
            act.wait_ge(g_in, 32 * (n + 1))
            act.activation(hi[:], gm_raw[:], ACT.Copy).then_inc(g_hi, 1)

        def dve_gates(dve, hi, lo, n):
            dve.wait_ge(g_hi, n + 1)
            dve.tensor_tensor(lo[:], gm_raw[:], hi[:].bitcast(F32), ALU.subtract).then_inc(g_split, 1)
        MLX = MLstm()

        G2 = range(2)
        gd_pe = steps("gd_pe", ["cs", "gates", "cvA", "cvB"] + [("sq", n) for n in range(12)] + ["small"]
                      + [("sq", n) for n in range(12, 16)] + [("nb", n) for n in range(16)]
                      + [x for c in range(TB) for x in
                         [(s, c, g) for g in G2 for s in ("gb", "kk", "qk", "v")] + [("kt", c, g) for g in G2]
                         + [("y", c, 0, g) for g in G2]
                         + [(s, c, l, g) for l in range(1, 7) for s in ("y", "xy") for g in G2]
                         + [(s, c, g) for s in ("ks", "u", "o", "ds") for g in G2 if s != "ks" or c > 0]]
                      + ["k8", ("sk", 0), ("sk", 1)] + [("fs", h) for h in range(GH)] + [("out", 0)]
                      + [y for h in range(GH) for y in ([("out", h + 1)] if h < GH - 1 else []) + [("fb", h)]
                         + {1: ["o8"], 4: ["fs8"]}.get(h, [])])
        gd_act = steps("gd_act", ["cs8", "lg", "rse"] + [("sq", n) for n in range(16)] + ["rt", "kd", "z"]
                       + [x for c in range(TB) for x in [(s, c, g) for g in G2 for s in ("dt", "v")]
                          + [("y", c, l, g) for l in range(1, 7) for g in G2] + [("o", c, g) for g in G2]]
                       + [("fsq", h) for h in range(GH)] + ["fr"]
                       + [y for h in range(GH) for y in [("yh", h)] + {2: ["sq8"], 5: ["fr8"]}.get(h, [])])
        gd_dve = steps("gd_dve", ["cst", "cs8", "graw", "cvA", "rows", "cvB", "small", "ms", "rt"]
                       + [("nb", n) for n in range(16)]
                       + [x for c in range(TB) for x in
                          [("dg", c, g) for g in G2] + [("nt", c, g) for g in G2] + [("kd", c, g) for g in G2]
                          + [("x", c, l, g) for l in range(7) for g in G2]
                          + [(s, c, g) for s in ("r", "u", "s") for g in G2 if s != "r" or c > 0]]
                       + [("kq", 0), "k8", "qk", ("kq", 1), ("u8", 0), ("u8", 1), ("Ud", 0), "fms", "fr"]
                       + [y for h in range(GH) for y in ([("Ud", h + 1)] if h < GH - 1 else []) + [("S8", h), ("n", h)]
                          + {1: ["o8"], 4: ["ms8"]}.get(h, []) + ([("y", h - 1)] if h > 0 else [])]
                       + [("y", GH - 1), "y8"])
        gd_oz = sem("gd_oz")
        gd_ld = sem("gd_ld")
        gd_st = sem("gd_st")
        gd_sst = sem("gd_sst")
        gd_sS = [sem(f"gd_sS{n}") for n in G2]

        class Gdn:
            g8 = slice(0, GH)
            gamT = keep[:, 264:296]
            betaT = keep[:, 296:328]
            kdS = keep[:, 328:360]
            egl = keep[:, 360:392]
            SB = keep[:, 0:160].rearrange("p (h x) -> p h x", h=GH)

            def bank(self, g, n):
                return (ACC if n < 2 else M)[:, 2 * g + n % 2, :]

            def four(self, ap):
                return ap.rearrange("p (h t) -> p h t", h=4)

            def per(self, ap, c, g):
                return ap[:, c * GH + 4 * g:c * GH + 4 * g + 4].unsqueeze(2).to_broadcast([P, 4, P])

            def sp_early(self, sp):
                sp.wait_ge(g_split, 1)
                sp_gate(sp, a["gd_w_in"][0], 4096, GH)

            def sp_mid(self, sp):
                sp.wait_ge(mm_done, GD_IN.u0)
                sp.dma_start(st_in[:], a["state_gdn_conv"][0].rearrange("b j f -> (b j) f")).then_inc(gd_ld, 16)

            def sp(self, sp):
                sp.dma_start(o["s_conv"][:, 0:2, :], a["state_gdn_conv"][0][:, 1:3, :]).then_inc(gd_st, 16)
                gd_dve.wait(sp, "cvB")
                sp.dma_start(o["p_conv"], cvo[0:3, :]).then_inc(gd_st, 16)
                sp.dma_start(o["s_conv"][:, 2, :], cvo[3:11, :]).then_inc(gd_st, 16)
                def load(q):
                    for hh in range(4):
                        sp.dma_start(sS[:, q, hh], a["state_gdn_S"][0, :, 4 * q + hh].rearrange("b p e -> p b e")).then_inc(gd_sS[q], 16)
                gd_dve.wait(sp, "x", TB - 1, 6, 1)
                load(0)
                for g in G2:
                    gd_dve.wait(sp, "s", TB - 1, g)
                gd_act.wait(sp, "o", TB - 1, 1)
                load(1)
                sp.dma_start(o["p_S"].rearrange("h p e -> p h e"), SS[:]).then_inc(gd_st, 16)
                for h in range(GH):
                    gd_dve.wait(sp, "S8", h)
                    sp.dma_start(o["s_S"][:, h].rearrange("b p e -> p b e"), sS[:, h // 4, h % 4]).then_inc(gd_sst, 16)

            def sp_end(self, sp):
                sp.wait_ge(gd_st, 16 * 4)
                sp.wait_ge(gd_sst, 16 * GH)

            def pe_prepare(self, pe):
                def state():
                    pe.wait_ge(gd_ld, 16)
                    for n in range(24):
                        mm = pe.transpose(M[:, n // 12, (n % 12) * 24:(n % 12 + 1) * 24], st_in[:, n * P:(n + 1) * P],
                                          ident[0:24, 0:24])
                    gd_pe.done(mm, "cs")

                def gates():
                    gd_pe.done(pe_gates(pe, 1), "gates")

                def conv_rows(n0, n1, name):
                    gd_dve.wait(pe, "graw" if n0 == 0 else "cvA")
                    for n in range(n0, n1):
                        mm = pe.transpose(M[0:11, (n - n0) // 4, (n % 4) * P:(n % 4 + 1) * P], xs[:, n, :], ident[:])
                    gd_pe.done(mm, name)

                def small():
                    gd_act.wait(pe, "rse")
                    gd_dve.wait(pe, "cvB")
                    g8 = self.g8
                    for b in range(TB):
                        pe.transpose(M[:, 0, b * GH:(b + 1) * GH], gamr[:, b * P:(b + 1) * P], ident[g8, g8])
                        pe.transpose(M[:, 0, 32 + b * GH:32 + (b + 1) * GH], beta_r[:, b * P:(b + 1) * P], ident[g8, g8])
                    pe.matmul(M[0:40, 0, 224:232], gsh[:, 4:44], ident[g8, g8], start=True, stop=True)
                    pe.transpose(M[0:NS, 0, 232:240], gsh[:, 12:20], ident[g8, g8])
                    for h in range(GH):
                        mm = pe.matmul(M[:, 0, 64 + 20 * h:84 + 20 * h], ident[g8, h:h + 1].to_broadcast([GH, P]),
                                       gsh[:, 0:20], start=True, stop=True)
                    gd_pe.done(mm, "small")
                return {1: state, 2: gates, 3: lambda: conv_rows(0, 16, "cvA"), 4: lambda: conv_rows(16, 24, "cvB"),
                        5: lambda: self.pe_sums(pe, 0), 6: lambda: self.pe_sums(pe, 4),
                        7: lambda: (self.pe_sums(pe, 8), small())}

            def pe_sums(self, pe, n0):
                if n0 == 0:
                    gd_dve.wait(pe, "cvA")
                for n in range(n0, n0 + 4):
                    gd_act.wait(pe, "sq", n)
                    row = n if n < GH else 32 + n - GH
                    for h in range(2):
                        mm = pe.matmul(M[0:40, 2 + h, 0:TH], pick[:, 39 - row:79 - row], self.sqb(n)[:, h * TH:(h + 1) * TH],
                                       start=n == 0, stop=n == 15)
                    gd_pe.done(mm, "sq", n)

            def pe(self, pe):
                self.pe_sums(pe, 12)
                pe.wait_ge(acc_free, GD_Z.t0 + GD_Z.units)
                gd_dve.wait(pe, "rt")
                for n in range(16):
                    if n >= 2:
                        gd_dve.wait(pe, "nb", n - 2)
                    row = n if n < GH else 32 + n - GH
                    for h, part in ((0, rt_hi), (0, rt_lo), (1, rt_hi), (1, rt_lo)):
                        mm = pe.matmul(ACC[:, 2 * (n % 2) + h, 0:TH], ident_r[:, row:row + 1].to_broadcast([40, P]),
                                       part[:, h * TH:(h + 1) * TH], start=part is rt_hi, stop=part is rt_lo)
                    gd_pe.done(mm, "nb", n)
                gd_dve.wait(pe, "nb", 15)
                gd_act.wait(pe, "kd")
                for c in range(TB):
                    self.pe_chunk(pe, c)
                self.pe_sample(pe)

            def pe_chunk(self, pe, c):
                t = slice(c * P, (c + 1) * P)

                def heads(g, f):
                    for q in range(4):
                        mm = f(4 * g + q, slice(q * P, (q + 1) * P))
                    return mm
                for g in G2:
                    B = [self.bank(g, n) for n in range(4)]
                    if c > 0:
                        gd_dve.wait(pe, "s", c - 1, g)
                        gd_act.wait(pe, "o", c - 1, g)
                    gd_pe.done(heads(g, lambda h, q: pe.matmul(B[0][:, q], ident[self.g8, h:h + 1].to_broadcast([GH, P]),
                                                               gamr[:, t], start=True, stop=True)), "gb", c, g)
                    gd_pe.done(heads(g, lambda h, q: pe.matmul(B[1][:, q], gp[:, GH + h, t], gp[:, GH + h, t],
                                                               start=True, stop=True)), "kk", c, g)
                    gd_pe.done(heads(g, lambda h, q: pe.matmul(B[2][:, q], gp[:, GH + h, t], gp[:, h, t],
                                                               start=True, stop=True)), "qk", c, g)
                    gd_pe.done(heads(g, lambda h, q: pe.transpose(B[3][:, q], gp[:, 16 + h, t], ident[:])), "v", c, g)
                for g in G2:
                    gd_act.wait(pe, "dt", c, g)
                    gd_pe.done(heads(g, lambda h, q: pe.transpose(self.bank(g, 0)[:, q], gp[:, GH + h, t], ident[:])), "kt", c, g)
                for l in range(7):
                    for g in G2:
                        if l == 0:
                            gd_dve.wait(pe, "kd", c, g)
                        else:
                            gd_dve.wait(pe, "x", c, l - 1, g)
                        gd_pe.done(heads(g, lambda h, q: pe.matmul(self.bank(g, 1)[:, q], rr[:, h, :],
                                                                   ident[:] if l == 0 else X[:, h, :],
                                                                   start=True, stop=True)), "y", c, l, g)
                    for g in G2:
                        if l == 0:
                            continue
                        gd_act.wait(pe, "y", c, l, g)
                        if l == 1:
                            gd_act.wait(pe, "v", c, g)
                        if l < 6:
                            heads(g, lambda h, q: pe.matmul(self.bank(g, 2)[:, q], XT[:, h, :], Y[:, h, :], start=True, stop=True))
                        gd_pe.done(heads(g, lambda h, q: pe.matmul(self.bank(g, 3)[:, q], Y[:, h, :], XT[:, h, :],
                                                                   start=True, stop=True)), "xy", c, l, g)
                if c > 0:
                    for g in G2:
                        gd_dve.wait(pe, "x", c, 6, g)
                        gd_pe.done(heads(g, lambda h, q: pe.matmul(self.bank(g, 0)[:, q], kTe[:, h, :], SS[:, h, :],
                                                                   start=True, stop=True)), "ks", c, g)
                for g in G2:
                    gd_dve.wait(pe, *(("r", c, g) if c > 0 else ("x", c, 6, g)))
                    src = rr if c > 0 else vNc
                    gd_pe.done(heads(g, lambda h, q: pe.matmul(self.bank(g, 1)[:, q], XT[:, h, :], src[:, h, :],
                                                               start=True, stop=True)), "u", c, g)

                def out(h, q, g):
                    if c > 0:
                        pe.matmul(self.bank(g, 2)[:, q], SS[:, h, :], qTe[:, h, :], start=True, stop=False)
                    return pe.matmul(self.bank(g, 2)[:, q], uu[:, h, :], QKD[:, h, :], start=c == 0, stop=True)
                for g in G2:
                    gd_dve.wait(pe, "u", c, g)
                    gd_pe.done(heads(g, lambda h, q: out(h, q, g)), "o", c, g)
                for g in G2:
                    gd_pe.done(heads(g, lambda h, q: pe.matmul(self.bank(g, 3)[:, q], kdec[:, h, :], uu[:, h, :],
                                                               start=True, stop=True)), "ds", c, g)

            def pe_sample(self, pe):
                for g in G2:
                    gd_dve.wait(pe, "s", TB - 1, g)
                    gd_act.wait(pe, "o", TB - 1, g)
                for h in range(GH):
                    q = slice((h % 4) * P, (h % 4 + 1) * P)
                    pe.transpose(ACC[0:NS, h // 4, q], gp[:, GH + h, LP:T], ident[:])
                    pe.transpose(ACC[0:NS, 2 + h // 4, q], gp[:, 16 + h, LP:T], ident[:])
                    mm = pe.transpose(M[0:NS, 2 + h // 4, q], gp[:, h, LP:T], ident[:])
                gd_pe.done(mm, "k8")
                for q in G2:
                    gd_dve.wait(pe, "kq", q)
                    pe.wait_ge(gd_sS[q], 64)
                    for hh in range(4):
                        for b in range(NS):
                            mm = pe.matmul(M[0:40, q, hh * P:(hh + 1) * P], KQ[:, hh, 40 * b:40 * (b + 1)], sS[:, q, hh, b, :],
                                           start=b == 0, stop=b == NS - 1)
                    gd_pe.done(mm, "sk", q)
                gd_dve.wait(pe, "qk")
                for h in range(GH):
                    gd_act.wait(pe, "fsq", h)
                    gd_pe.done(pe.matmul(M[0:GH, 3, :], pick[:, 39 - h:39 - h + GH], fsqb[h % 2][:],
                                         start=h == 0, stop=h == GH - 1), "fs", h)

                def outer(h):
                    gd_dve.wait(pe, "Ud", h)
                    if h >= 2:
                        gd_dve.wait(pe, "S8", h - 2)
                    for k in range(2):
                        for part in range(2):
                            mm = pe.matmul(ACC[:, 2 * (h % 2) + k, :], gk40[:, part, h * P:(h + 1) * P],
                                           gUd[:, h % 2, 4 * k:4 * k + 4, :].rearrange("k b e -> k (b e)"),
                                           start=part == 0, stop=part == 1)
                    gd_pe.done(mm, "out", h)
                outer(0)
                for h in range(GH):
                    if h < GH - 1:
                        outer(h + 1)
                    if h >= 2:
                        gd_dve.wait(pe, "n", h - 2)
                    elif h == 0:
                        gd_dve.wait(pe, "fr")
                    gd_pe.done(pe.matmul(M[:, h % 2, :], two_r[:, h:h + 1].to_broadcast([40, P]), rf40[:],
                                         start=True, stop=True), "fb", h)
                    if h == 1:
                        for n in range(GH):
                            mm = pe.transpose(M[:, 2, n * NS:(n + 1) * NS], go8[:, n * P:(n + 1) * P], ident[0:NS, 0:NS])
                        gd_pe.done(mm, "o8")
                    if h == 4:
                        gd_act.wait(pe, "sq8")
                        gd_pe.done(pe.matmul(M[:, 3, 0:64], ones[:], gs8, start=True, stop=True), "fs8")
                gd_dve.wait(pe, "y8")

            def sqb(self, n):
                return (sq[:, n % 4, :] if n % 4 < 2 else tmp[:, n % 4 - 2, 0:T])

            def act_prepare(self, act, own):
                g = self.g8

                def sample_conv():
                    gd_dve.wait(act, "cs8")
                    gd_act.done(act.activation(gp[:, 0:24, LP:T], gms[:, 0].rearrange("p (n b) -> p n b", b=NS), ACT.Silu), "cs8")

                def decay():
                    gd_dve.wait(act, "graw")
                    own.link(act.activation(small[g, 12:13], small[g, 2:3], ACT.Exp))
                    own.link(act.activation(sp_r, la_r[:], ACT.Abs, bias=small[g, 3:4]))
                    own.link(act.activation(sp_r, sp_r, ACT.Exp, scale=-1.0))
                    own.link(act.activation(sp_r, sp_r, ACT.Ln, bias=ones[g, 0:1]))
                    gd_act.done(act.activation(beta_r[:], beta_r[:], ACT.Sigmoid), "lg")

                def sample_decay():
                    gd_dve.wait(act, "rows")
                    act.activation(gsh[:, 4:12], gsh[:, 4:12], ACT.Exp)
                    gd_act.done(act.activation(gsh[:, 36:44], gsh[:, 36:44], ACT.Exp), "rse")

                def squares(n0):
                    gd_act.wait(act, "cs8")
                    for n in range(n0, n0 + 4):
                        if n >= 4:
                            gd_pe.wait(act, "sq", n - 4)
                        gd_act.done(act.activation(self.sqb(n), gp[:, n, :], ACT.Square), "sq", n)
                return {0: lambda: act_gates(act, gg_hi, 1), 2: lambda: (sample_conv(), decay()),
                        3: lambda: (sample_decay(), squares(0)), 4: lambda: squares(4), 5: lambda: squares(8),
                        6: lambda: squares(12)}

            def act(self, act, own):
                gd_dve.wait(act, "ms")
                gd_act.done(act.activation(rt40, rt40, ACT.Sqrt), "rt")
                gd_dve.wait(act, "small")
                act.activation(self.kdS, self.kdS, ACT.Exp)
                gd_act.done(act.activation(self.egl, self.egl, ACT.Exp), "kd")
                act.wait_ge(acc_free, GD_Z.t0 + GD_Z.units)
                own.link(act.activation(gp[:, 24:32, :], gp[:, 24:32, :], ACT.Silu))
                gd_act.done(act.activation(gp[:, 24:32, :], gp[:, 24:32, :], ACT.Copy, scale=cols[:, 96:97]), "z")
                for c in range(TB):
                    t = slice(c * P, (c + 1) * P)
                    for g in G2:
                        hs = slice(4 * g, 4 * g + 4)
                        gd_dve.wait(act, "dg", c, g)
                        act.activation(Y[:, hs], self.four(self.bank(g, 0)), ACT.Exp)
                        gd_act.done(act.activation(DT[:, hs], DT[:, hs], ACT.Exp), "dt", c, g)
                        gd_pe.wait(act, "v", c, g)
                        gd_act.done(act.activation(vNc[:, hs], self.four(self.bank(g, 3)), ACT.Copy), "v", c, g)
                    for l in range(1, 7):
                        for g in G2:
                            hs = slice(4 * g, 4 * g + 4)
                            gd_pe.wait(act, "y", c, l, g)
                            gd_act.done(act.activation(Y[:, hs], self.four(self.bank(g, 1)), ACT.Copy), "y", c, l, g)
                    for g in G2:
                        gd_pe.wait(act, "o", c, g)
                        gd_act.done(act.activation(gp[:, 16 + 4 * g:20 + 4 * g, t], self.four(self.bank(g, 2)), ACT.Copy), "o", c, g)
                gd_act.wait(act, "o", TB - 1, 1)
                for h in range(GH):
                    if h >= 2:
                        gd_pe.wait(act, "fs", h - 2)
                    else:
                        gd_dve.wait(act, "s", TB - 1, 1)
                    gd_act.done(act.activation(fsqb[h % 2][:], gp[:, 16 + h, 0:LP], ACT.Square), "fsq", h)
                gd_dve.wait(act, "fms")
                gd_act.done(act.activation(R[self.g8, 0:LP], R[self.g8, 0:LP], ACT.Sqrt), "fr")
                for h in range(GH):
                    gd_dve.wait(act, "n", h)
                    gd_act.done(act.activation(gy_hi[:, h, 0:LP], gp[:, 24 + h, 0:LP], ACT.Copy), "yh", h)
                    if h == 2:
                        gd_dve.wait(act, "o8")
                        gd_act.done(act.activation(gs8.rearrange("p (h b) -> p h b", b=NS), gp[:, 16:24, LP:T], ACT.Square), "sq8")
                    if h == 5:
                        gd_dve.wait(act, "ms8")
                        gd_act.done(act.activation(gs8, gs8, ACT.Sqrt), "fr8")
                act.wait_ge(gd_sst, 16 * GH)

            def dve_prepare(self, dve, own):
                g = self.g8
                v2 = lambda ap: ap.rearrange("p (a b) -> p a b", a=2)

                def state():
                    gd_pe.wait(dve, "cs")
                    gd_dve.done(dve.tensor_copy(cst[:].rearrange("p (a n) x -> p a n x", a=2),
                                                M[:, 0:2, 0:288].rearrange("p a (n x) -> p a n x", x=24)), "cst")
                    gd_dve.wait(dve, "cst")
                    cs = cst[:].rearrange("p n (b j) -> p n b j", j=3)
                    acc, one = [gms[:, k].rearrange("p (n b) -> p n b", b=NS) for k in range(2)]
                    cw = lambda j: convw[:, j * 24:(j + 1) * 24].unsqueeze(2).to_broadcast([P, 24, NS])
                    gd_pe.wait(dve, "gates")
                    own.link(dve.tensor_tensor(acc, cs[:, :, :, 0], cw(0), ALU.mult))
                    for j in (1, 2, 3):
                        own.link(dve.tensor_tensor(one, cs[:, :, :, j] if j < 3 else xs[:, :, 3:11], cw(j), ALU.mult))
                        ins = dve.tensor_tensor(acc, acc, one, ALU.add)
                        if j < 3:
                            own.link(ins)
                    gd_dve.done(ins, "cs8")
                    dve.tensor_tensor(v2(beta_r[:]), M[0:GH, 2:4, 0:TH], halves(R[0:GH]), ALU.mult)
                    gd_dve.done(dve.tensor_tensor(v2(la_r[:]), M[32:40, 2:4, 0:TH], halves(R[32:40]), ALU.mult), "graw")

                def rows():
                    gd_pe.wait(dve, "cvA")
                    gd_dve.done(dve.tensor_copy(cvo[:, 0:2048].rearrange("p (a b) -> p a b", a=4), M[0:11]), "cvA")
                    gd_act.wait(dve, "lg")
                    own.link(dve.tensor_scalar(lg_r[:], la_r[:], small[g, 3:4], 0.0, ALU.add, ALU.max))
                    own.link(dve.tensor_tensor(lg_r[:], lg_r[:], sp_r, ALU.add))
                    own.link(dve.tensor_scalar(lg_r[:], lg_r[:], small[g, 12:13], -1.0, ALU.mult, ALU.mult))
                    for b in range(TB):
                        dve.tensor_tensor_scan(gamr[:, b * P:(b + 1) * P], ones[g, 0:1].to_broadcast([GH, P]),
                                               lg_r[:, b * P:(b + 1) * P], 0.0, ALU.mult, ALU.add)
                    own.link(dve.memset(gsh[:, 20:36], 0.0))
                    dve.tensor_copy(gsh[:, 0:4], gamr[:].rearrange("p (b t) -> p b t", t=P)[:, :, P - 1])
                    dve.tensor_copy(gsh[:, 12:20], beta_r[:, LP:T])
                    dve.tensor_copy(gsh[:, 36:44], lg_r[:, LP:T])
                    gd_dve.done(dve.tensor_copy(gsh[:, 4:12], lg_r[:, LP:T]), "rows")

                def last_rows():
                    gd_pe.wait(dve, "cvB")
                    gd_dve.done(dve.tensor_copy(cvo[:, 2048:3072].rearrange("p (a b) -> p a b", a=2), M[0:11, 0:2]), "cvB")
                return {0: lambda: dve_gates(dve, gg_hi, gg_lo, 1), 1: state, 2: rows, 3: last_rows}

            def dve(self, dve, own):
                gd_pe.wait(dve, "small")
                own.link(dve.tensor_copy(keep[:, 264:328], M[:, 0, 0:64]))
                own.link(dve.tensor_copy(keep[0:40, 160:176], M[0:40, 0, 224:240]))
                own.link(dve.tensor_copy(keep[:, 0:160], M[:, 0, 64:224]))
                bh = lambda ap: ap.rearrange("p (b h) -> p b h", h=GH)
                glast = self.SB[:, :, 0:4].rearrange("p h b -> p b h")
                own.link(dve.tensor_copy(bh(self.egl), glast))
                gd_dve.done(dve.tensor_tensor(bh(self.kdS), glast, bh(self.gamT), ALU.subtract), "small")
                gd_pe.wait(dve, "sq", 15)
                own.link(dve.tensor_scalar(halves(rt40), M[0:40, 2:4, 0:TH], EPS, None, ALU.add))
                gd_dve.done(dve.tensor_scalar(rt40[0:GH], rt40[0:GH], float(P), None, ALU.mult), "ms")
                gd_act.wait(dve, "rt")
                own.link(dve.reciprocal(rt40, rt40))
                own.link(dve.tensor_copy(rt_hi[:], rt40))
                gd_dve.done(dve.tensor_tensor(rt_lo[:], rt40, rt_hi[:].bitcast(F32), ALU.subtract), "rt")
                for n in range(16):
                    gd_pe.wait(dve, "nb", n)
                    gd_dve.done(dve.tensor_tensor(halves(gp[:, n, :]), halves(gp[:, n, :]), ACC[:, 2 * (n % 2):2 * (n % 2) + 2, 0:TH],
                                                  ALU.mult), "nb", n)
                dve.wait_ge(gd_st, 48)
                gd_dve.wait(dve, "nb", 15)
                for c in range(TB):
                    self.dve_chunk(dve, own, c)
                self.dve_sample(dve, own)
                dve.wait_ge(gd_sst, 16 * GH)

            def dve_chunk(self, dve, own, c):
                t = slice(c * P, (c + 1) * P)
                eye = ident[:].unsqueeze(1).to_broadcast([P, 4, P])
                for g in G2:
                    hs = slice(4 * g, 4 * g + 4)
                    gd_pe.wait(dve, "gb", c, g)
                    own.link(dve.tensor_tensor(DT[:, hs], self.four(self.bank(g, 0)), self.per(self.gamT, c, g), ALU.subtract))
                    gd_dve.done(dve.tensor_tensor(DT[:, hs], DT[:, hs], causal[:].unsqueeze(1).to_broadcast([P, 4, P]),
                                                  ALU.subtract), "dg", c, g)
                for g in G2:
                    hs = slice(4 * g, 4 * g + 4)
                    gd_act.wait(dve, "dt", c, g)
                    gd_pe.wait(dve, "kk", c, g)
                    own.link(dve.tensor_tensor(NT[:, hs], DT[:, hs], self.four(self.bank(g, 1)), ALU.mult))
                    own.link(dve.tensor_tensor(NT[:, hs], NT[:, hs], self.per(self.betaT, c, g), ALU.mult))
                    gd_pe.wait(dve, "qk", c, g)
                    dve.tensor_tensor(QKD[:, hs], DT[:, hs], self.four(self.bank(g, 2)), ALU.mult)
                    dve.tensor_tensor(kTe[:, hs], gp[:, GH + 4 * g:GH + 4 * g + 4, t], Y[:, hs], ALU.mult)
                    gd_dve.done(dve.tensor_tensor(qTe[:, hs], gp[:, 4 * g:4 * g + 4, t], Y[:, hs], ALU.mult), "nt", c, g)
                for g in G2:
                    hs = slice(4 * g, 4 * g + 4)
                    own.link(dve.tensor_tensor(rr[:, hs], NT[:, hs], level[:, 0].unsqueeze(1).to_broadcast([P, 4, P]), ALU.mult))
                    own.link(dve.tensor_tensor(XT[:, hs], eye, rr[:, hs], ALU.subtract))
                    gd_pe.wait(dve, "kt", c, g)
                    gd_dve.done(dve.tensor_tensor(kdec[:, hs], self.four(self.bank(g, 0)), self.per(self.kdS, c, g), ALU.mult),
                                "kd", c, g)
                for l in range(7):
                    for g in G2:
                        hs = slice(4 * g, 4 * g + 4)
                        if l == 0:
                            gd_pe.wait(dve, "y", c, 0, g)
                            ins = dve.tensor_tensor(X[:, hs], eye, self.four(self.bank(g, 1)), ALU.subtract)
                        else:
                            gd_pe.wait(dve, "xy", c, l, g)
                            if l < 6:
                                dve.tensor_tensor(X[:, hs], X[:, hs], self.four(self.bank(g, 2)), ALU.subtract)
                            ins = dve.tensor_tensor(XT[:, hs], XT[:, hs], self.four(self.bank(g, 3)), ALU.subtract)
                        if l < 6:
                            ins = dve.tensor_tensor(rr[:, hs], NT[:, hs], level[:, l + 1].unsqueeze(1).to_broadcast([P, 4, P]),
                                                    ALU.mult)
                        gd_dve.done(ins, "x", c, l, g)
                if c > 0:
                    for g in G2:
                        hs = slice(4 * g, 4 * g + 4)
                        gd_pe.wait(dve, "ks", c, g)
                        gd_dve.done(dve.tensor_tensor(rr[:, hs], vNc[:, hs], self.four(self.bank(g, 0)), ALU.subtract), "r", c, g)
                for g in G2:
                    hs = slice(4 * g, 4 * g + 4)
                    gd_pe.wait(dve, "u", c, g)
                    gd_dve.done(dve.tensor_tensor(uu[:, hs], self.four(self.bank(g, 1)), self.per(self.betaT, c, g), ALU.mult),
                                "u", c, g)
                for g in G2:
                    gd_pe.wait(dve, "ds", c, g)
                    hs = slice(4 * g, 4 * g + 4)
                    if c == 0:
                        ins = dve.tensor_copy(SS[:, hs], self.four(self.bank(g, 3)))
                    else:
                        for q in range(4):
                            h = 4 * g + q
                            ins = dve.scalar_tensor_tensor(SS[:, h, :], SS[:, h, :], self.egl[:, c * GH + h:c * GH + h + 1],
                                                           self.bank(g, 3)[:, q * P:(q + 1) * P], ALU.mult, ALU.add)
                    gd_dve.done(ins, "s", c, g)

            def dve_sample(self, dve, own):
                e3 = lambda ap, n: ap.rearrange("p (h e) -> p h e", h=n)
                gB = lambda r, q: keep[r:r + NS, 160 + 4 * q:164 + 4 * q].unsqueeze(2).to_broadcast([NS, 4, P])
                bB = lambda q: keep[0:NS, 168 + 4 * q:172 + 4 * q].unsqueeze(2).to_broadcast([NS, 4, P])
                qk = keep[0:NS, 176:184]
                gv8, t8 = go8, gt8[:]
                w2 = lambda ap: ap.rearrange("p (a b) -> p a b", a=2)

                def stationary(q):
                    dve.tensor_copy(KQ[:, :, 0:288:41], gp[:, GH + 4 * q:GH + 4 * q + 4, LP:T])
                    gd_dve.done(dve.tensor_copy(KQ[:, :, 32:320:41], gp[:, 4 * q:4 * q + 4, LP:T]), "kq", q)
                own.link(dve.memset(KQ[:], 0.0))
                stationary(0)
                own.link(dve.tensor_copy(gk40[:, 0], zeros40(D)))
                own.link(dve.tensor_copy(gk40[:, 1], zeros40(D)))
                gd_pe.wait(dve, "k8")
                own.link(dve.tensor_copy(gk8[:].rearrange("p (a b) -> p a b", a=2), ACC[0:NS, 0:2, :]))
                gd_dve.done(dve.tensor_copy(gv8.rearrange("p (a b) -> p a b", a=2), ACC[0:NS, 2:4, :]), "k8")
                own.link(dve.tensor_tensor(t8.rearrange("p (a b) -> p a b", a=2), gk8[:].rearrange("p (a b) -> p a b", a=2),
                                           M[0:NS, 2:4, :], ALU.mult))
                gd_dve.done(dve.tensor_reduce(qk, e3(t8, GH), AX.X, ALU.add), "qk")
                own.link(dve.tensor_copy(gk40[0:NS, 0], gk8[:]))
                own.link(dve.tensor_copy(gk40[32:40, 0], gk8[:]))
                own.link(dve.tensor_tensor(gk40[0:NS, 1], gk8[:], gk40[0:NS, 0].bitcast(F32), ALU.subtract))
                gd_pe.wait(dve, "sk", 0)
                stationary(1)
                for q in G2:
                    c = slice(512 * q, 512 * (q + 1))
                    u, t, v = e3(gu8[:, c], 4), e3(t8[:, c], 4), e3(gv8[:, c], 4)
                    if q == 1:
                        gd_pe.wait(dve, "sk", 1)
                    own.link(dve.tensor_tensor(u, e3(M[0:NS, q, :], 4), gB(0, q), ALU.mult))
                    own.link(dve.tensor_tensor(u, v, u, ALU.subtract))
                    own.link(dve.tensor_tensor(u, u, bB(q), ALU.mult))
                    own.link(dve.tensor_tensor(v, e3(M[32:40, q, :], 4), gB(32, q), ALU.mult))
                    own.link(dve.tensor_tensor(t, u, qk[:, 4 * q:4 * q + 4].unsqueeze(2).to_broadcast([NS, 4, P]), ALU.mult))
                    gd_dve.done(dve.tensor_tensor(v, v, t, ALU.add), "u8", q)

                def diagonal(h):
                    u = gu40[:, h * P:(h + 1) * P].bitcast(F32)
                    gd_dve.done(dve.tensor_tensor(gUd[:, h % 2], u.unsqueeze(1).to_broadcast([40, NS, P]),
                                                  two[:].unsqueeze(2).to_broadcast([40, NS, P]), ALU.mult), "Ud", h)

                def low(h):
                    gd_act.wait(dve, "yh", h)
                    gd_dve.done(dve.tensor_tensor(gy_lo[:, h, 0:LP], gp[:, 24 + h, 0:LP], gy_hi[:, h, 0:LP].bitcast(F32),
                                                  ALU.subtract), "y", h)
                gd_dve.wait(dve, "u8", 1)
                own.link(dve.tensor_copy(gu40[:], zeros40(D)))
                own.link(dve.tensor_copy(gu40[0:NS], gu8[:]))
                own.link(dve.tensor_tensor(gu40[32:40], gu8[:], gu40[0:NS].bitcast(F32), ALU.subtract))
                dve.wait_ge(gd_st, 64)
                diagonal(0)
                r = R[self.g8, 0:LP]
                gd_pe.wait(dve, "fs", GH - 1)
                gd_dve.done(dve.tensor_scalar(r, M[0:GH, 3, :], 1.0 / P, EPS, ALU.mult, ALU.add), "fms")
                gd_act.wait(dve, "fr")
                own.link(dve.reciprocal(r, r))
                own.link(dve.tensor_copy(rf40[:], zeros40(LP)))
                own.link(dve.tensor_copy(rf40[0:GH], r))
                gd_dve.done(dve.tensor_tensor(rf40[32:40], r, rf40[0:GH].bitcast(F32), ALU.subtract), "fr")
                for h in range(GH):
                    if h < GH - 1:
                        diagonal(h + 1)
                    gd_pe.wait(dve, "out", h)
                    for b in range(NS):
                        s = sS[:, h // 4, h % 4, b, :]
                        ins = dve.scalar_tensor_tensor(s, s, self.SB[:, h, 4 + b:5 + b],
                                                       ACC[:, 2 * (h % 2) + b // 4, (b % 4) * P:(b % 4 + 1) * P],
                                                       ALU.mult, ALU.add)
                    gd_dve.done(ins, "S8", h)
                    gd_pe.wait(dve, "fb", h)
                    dve.wait_ge(gd_oz, h + 1)
                    gd_dve.done(dve.tensor_tensor(gp[:, 24 + h, 0:LP], gp[:, 24 + h, 0:LP], M[:, h % 2, :], ALU.mult), "n", h)
                    if h == 1:
                        gd_pe.wait(dve, "o8")
                        gd_dve.done(dve.tensor_copy(gp[:, 16:24, LP:T], M[:, 2, 0:64].rearrange("p (h b) -> p h b", b=NS)), "o8")
                    if h == 4:
                        gd_pe.wait(dve, "fs8")
                        gd_dve.done(dve.tensor_scalar(gs8, M[:, 3, 0:64], 1.0 / P, EPS, ALU.mult, ALU.add), "ms8")
                    if h > 0:
                        low(h - 1)
                low(GH - 1)
                gd_act.wait(dve, "fr8")
                own.link(dve.reciprocal(gs8, gs8))
                n = gp[:, 16:24, LP:T]
                own.link(dve.tensor_tensor(n, n, gs8.rearrange("p (h b) -> p h b", b=NS), ALU.mult))
                own.link(dve.tensor_tensor(n, n, gp[:, 24:32, LP:T], ALU.mult))
                own.link(dve.tensor_copy(gy_hi[:, :, LP:T], n))
                gd_dve.done(dve.tensor_tensor(gy_lo[:, :, LP:T], n, gy_hi[:, :, LP:T].bitcast(F32), ALU.subtract), "y8")

            def pool(self, pool):
                gd_act.wait(pool, "o", TB - 1, 1)
                gd_act.wait(pool, "z")
                for h in range(GH):
                    pool.tensor_tensor(gp[:, 24 + h, 0:LP], gp[:, 16 + h, 0:LP], gp[:, 24 + h, 0:LP], ALU.mult).then_inc(gd_oz, 1)
        KQ = tmp[:].rearrange("p a t -> p (a t)")[:, 0:1280].rearrange("p (h x) -> p h x", h=4)
        go8 = sq[:].rearrange("p a t -> p (a t)")[0:NS, 0:D]
        rt40 = R[0:40, :]
        gs8 = keep[:, 184:248]
        sp_r = tmp[0:GH, 2, 0:T]
        GDX = Gdn()

        fi_pe = steps("fi_pe", [("t", n) for n in range(TB + 1)])
        fi_act = steps("fi_act", [("g", c) for c in range(KC)])
        fi_dve = steps("fi_dve", [("y", n) for n in range(TB + 1)])
        put = placed(base, room)
        yf = put("yf", [P, TB + 1, D])
        fg = put("fg", [P, KC, T])
        rfin = put("rfin", [P, 8])
        NRES = n_res[0] - 1

        def pe_final(pe):
            pe.wait_ge(ssq_added, (KC - 1) * (NRES + 1))
            for b in range(TB + 1):
                n = P if b < TB else NS
                mm = pe.matmul(M[0:n, 0, b:b + 1], ssq[:, b * P:b * P + n], ones[:, 0:1], start=True, stop=True)
            mm.then_inc(nrm_tok, 1)
            fi_act.wait(pe, "g", KC - 1)
            for b in range(TB + 1):
                n = P if b < TB else NS
                s = ACC[:, 2 * (b % 2):2 * (b % 2) + 2, :]
                if b >= 2:
                    fi_dve.wait(pe, "y", b - 2)
                for c in range(KC):
                    mm = pe.transpose(s[0:n, c // 4, (c % 4) * P:(c % 4 + 1) * P], fg[:, c, b * P:b * P + n], ident[:])
                fi_pe.done(mm, "t", b)

        def act_final(act):
            for c in range(KC):
                fi_act.done(act.activation(fg[:, c, :], x[:, c, :], ACT.Copy, scale=gcol("g_final", c)), "g", c)

        def dve_final(dve, own):
            dve.wait_ge(nrm_tok, N_NORM + 1)
            own.link(dve.memset(rfin[:], 1.0))
            own.link(dve.tensor_scalar(rfin[:, 0:TB], M[:, 0, 0:TB], 1.0 / D, EPS, ALU.mult, ALU.add))
            dve.tensor_scalar(rfin[0:NS, TB:TB + 1], M[0:NS, 0, TB:TB + 1], 1.0 / D, EPS, ALU.mult, ALU.add).then_inc(nrm_ms, 1)
            dve.wait_ge(nrm_pow, NRES + 1)
            for b in range(TB + 1):
                n = P if b < TB else NS
                fi_pe.wait(dve, "t", b)
                fi_dve.done(dve.tensor_scalar(yf[0:n, b, :].rearrange("p (a c) -> p a c", a=2),
                                              ACC[0:n, 2 * (b % 2):2 * (b % 2) + 2, :], rfin[0:n, b:b + 1], None, ALU.mult), "y", b)

        def pool_final(pool, res):
            for c in range(1, KC):
                pool.wait_ge(sq_done, KC * res + c + 1)
                if c > 1:
                    pool.wait_ge(ssq_added, (KC - 1) * res + c - 1)
                pool.tensor_tensor(ssq[:], ssq[:], sq[:, c % 2, :], ALU.add).then_inc(ssq_added, 1)
            pool.wait_ge(nrm_ms, NRES + 1)
            pool.tensor_tensor(rfin[:, 0:TB + 1], rfin[:, 0:TB + 1], mhalf[:, 0:TB + 1], ALU.pow).then_inc(nrm_pow, 1)

        def sp_final(sp):
            for b in range(TB):
                fi_dve.wait(sp, "y", b)
                sp.dma_start(o["y_prompt"][b * P:(b + 1) * P, :], yf[:, b, :]).then_inc(stored, 16)
            fi_dve.wait(sp, "y", TB)
            sp.dma_start(o["y_sample"], yf[0:NS, TB, :]).then_inc(stored, 16)
            sp.wait_ge(stored, 16 * (TB + 1))
            sp.wait_ge(k_out, 16 * 2)
            sp.wait_ge(v_out, 16 * 2)

        def sp_attention(sp, l, phs):
            sp_phase(sp, phs[0], others=False)
            sp_mem(sp, l, phs)
            sp_phase(sp, phs[0], first=False)
            for ph in phs[1:3]:
                sp_phase(sp, ph)
            sp_phase(sp, phs[3], others=False)
            sp_kv_out(sp, l)
            sp_phase(sp, phs[3], first=False)

        def pe_attention(pe, l, phs):
            pe_phase(pe, phs[0], before={4: lambda: pe_mem(pe, l)})
            k, v, rest = pe_queries(pe, l, phs)
            at_dve.wait(pe, "memlo", r=l)
            pe_phase(pe, phs[1], before=k)
            pe_phase(pe, phs[2], before=v)
            rest()
            pe_kv_natural(pe, l, phs)
            pe_attn(pe, l, phs)
            pe_phase(pe, phs[3])

        def act_attention(act, own, l, phs):
            act_phase(act, phs[0], after=act_mem(act, own, l))
            act_phase(act, phs[1])
            act_phase(act, phs[2], after={1: lambda: act_k_high(act, l, phs)})
            act_kv_natural(act, l)
            act_attn(act, own, l)
            act_phase(act, phs[3])

        def dve_attention(dve, own, l, phs):
            dve_phase(dve, own, phs[0], after=dve_mem(dve, own, l))
            k, v, rest = dve_scores(dve, own, l)
            dve_phase(dve, own, phs[1], after=k)
            dve_phase(dve, own, phs[2], after=v)
            rest()
            dve_kv_low(dve, l)
            dve_attn(dve, own, l)
            dve.wait_ge(v_out, 16 * (l + 1))
            dve_phase(dve, own, phs[3])

        block = ctx.enter_context(nc.Block())

        @block.sync
        def _(sp):
            sp_setup(sp)
            MLX.sp_early(sp)
            for ph in FF10:
                sp_phase(sp, ph)
            sp_phase(sp, ML_IN)
            sp_phase(sp, ML_OUT, others=False)
            MLX.sp(sp)
            sp_phase(sp, ML_OUT, first=False)
            GDX.sp_early(sp)
            sp_attention(sp, 0, XA0)
            for ph in FF20 + FF11:
                sp_phase(sp, ph)
            sp_phase(sp, GD_IN, others=False)
            GDX.sp_mid(sp)
            sp_phase(sp, GD_IN, first=False)
            sp_phase(sp, GD_Z)
            sp_phase(sp, GD_OUT, others=False)
            GDX.sp(sp)
            sp_phase(sp, GD_OUT, first=False)
            sp_attention(sp, 1, XA1)
            for ph in FF21:
                sp_phase(sp, ph)
            sp_final(sp)
            MLX.sp_end(sp)
            GDX.sp_end(sp)

        @block.tensor
        def _(pe):
            pe_setup(pe)
            for ph in FF10:
                pe_phase(pe, ph)
            pe_phase(pe, ML_IN)
            MLX.pe(pe)
            pe_phase(pe, ML_OUT)
            pe_attention(pe, 0, XA0)
            for ph in FF20 + FF11:
                pe_phase(pe, ph)
            pe_phase(pe, GD_IN)
            pe_phase(pe, GD_Z, before=GDX.pe_prepare(pe))
            GDX.pe(pe)
            pe_phase(pe, GD_OUT)
            pe_attention(pe, 1, XA1)
            for ph in FF21:
                pe_phase(pe, ph)
            pe_final(pe)

        @block.scalar
        def _(act):
            own = Own(act, act_own)
            first_splits_act(act)
            act_setup(act)
            for ph in FF10:
                act_phase(act, ph)
            act_phase(act, ML_IN)
            MLX.act(act, own)
            act_phase(act, ML_OUT)
            act_attention(act, own, 0, XA0)
            for ph in FF20 + FF11:
                act_phase(act, ph)
            act_phase(act, GD_IN)
            act_phase(act, GD_Z, after=GDX.act_prepare(act, own))
            GDX.act(act, own)
            act_phase(act, GD_OUT)
            act_attention(act, own, 1, XA1)
            for ph in FF21:
                act_phase(act, ph)
            act_final(act)

        @block.vector
        def _(dve):
            own = Own(dve, dve_own)
            first_splits_dve(dve)
            dve_setup(dve, own)
            for ph in FF10:
                dve_phase(dve, own, ph)
            dve_phase(dve, own, ML_IN)
            MLX.dve(dve, own)
            dve_phase(dve, own, ML_OUT)
            dve_attention(dve, own, 0, XA0)
            for ph in FF20 + FF11:
                dve_phase(dve, own, ph)
            dve_phase(dve, own, GD_IN)
            dve_phase(dve, own, GD_Z, after=GDX.dve_prepare(dve, own))
            GDX.dve(dve, own)
            dve_phase(dve, own, GD_OUT)
            dve_attention(dve, own, 1, XA1)
            for ph in FF21:
                dve_phase(dve, own, ph)
            dve_final(dve, own)

        @block.gpsimd
        def _(pool):
            own = Own(pool, pool_own)
            pool_setup(pool, own)
            pool_chunks(pool, 0)
            pool_chunks(pool, 1)
            MLX.pool(pool, own)
            pool_chunks(pool, 2)
            pool_mem(pool, 0)
            pool_cache(pool, 0, XA0)
            pool_chunks(pool, 3)
            pool_chunks(pool, 4)
            pool_chunks(pool, 5)
            GDX.pool(pool)
            pool_chunks(pool, 6)
            pool_mem(pool, 1)
            pool_cache(pool, 1, XA1)
            pool_chunks(pool, 7)
            pool_final(pool, NRES)


_INS = ['x_prompt', 'x_sample', 'mem_prompt', 'cache_mem_k', 'cache_mem_v', 'state_mlstm_C', 'state_mlstm_n',
        'state_mlstm_m', 'state_gdn_S', 'state_gdn_conv', 'g_ffn1', 'ffn1_w_gate', 'ffn1_w_up', 'ffn1_w_down', 'g_mix',
        'ml_w_in', 'ml_b_i', 'ml_b_f', 'ml_g_head', 'ml_w_out', 'gd_w_in', 'gd_conv_w', 'gd_a_log', 'gd_dt_bias',
        'gd_g_out', 'gd_w_out', 'g_xattn', 'g_mem', 'xa_w_q', 'xa_w_k', 'xa_w_v', 'xa_w_o', 'g_ffn2', 'ffn2_w_gate',
        'ffn2_w_up', 'ffn2_w_down', 'g_final']
_OUTS = [("y_prompt", (LP, D), (1, LP, D)), ("y_sample", (NS, D), (NS, 1, D)),
         ("mem_k", (2, NMEM, D), (2, 1, NMEM, XH, XD)), ("mem_v", (2, NMEM, D), (2, 1, NMEM, XH, XD)),
         ("p_C", (MLH, P, 256), (1, 1, MLH, P, 256)), ("p_n", (1, MLH * P), (1, 1, MLH, P)), ("p_m", (MLH, 1), (1, 1, MLH)),
         ("p_S", (GH, P, P), (1, 1, GH, P, P)), ("p_conv", (3, 3072), (1, 1, 3, 3072)),
         ("s_C", (NS, MLH, P, 256), (1, NS, MLH, P, 256)), ("s_n", (NS * MLH, P), (1, NS, MLH, P)),
         ("s_m", (NS, MLH), (1, NS, MLH)), ("s_S", (NS, GH, P, P), (1, NS, GH, P, P)),
         ("s_conv", (NS, 3, 3072), (1, NS, 3, 3072))]


def kernel(**inputs):
    import numpy as _np
    import concourse.bacc as _bacc
    from concourse import mybir as _mybir
    from concourse.bass_utils import run_bass_kernel_spmd as _run

    nc = _bacc.Bacc("TRN2", target_bir_lowering=False, num_devices=1)
    arrays, a, o = {}, {}, {}
    for name in _INS:
        v = _np.ascontiguousarray(inputs[name])
        arrays[f"in_{name}"] = v
        a[name] = nc.dram_tensor(f"in_{name}", v.shape, _mybir.dt.from_np(v.dtype), kind="ExternalInput").ap()
    for name, shape, _ in _OUTS:
        o[name] = nc.dram_tensor(f"out_{name}", shape, F32, kind="ExternalOutput").ap()
    program(nc, a, o)
    r = _run(nc, [arrays], core_ids=[0])
    return tuple(_np.asarray(r.results[0][f"out_{name}"]).reshape(full) for name, _, full in _OUTS)
```
